# Optimizing a Trainium2 kernel written in Bass

```python
import math
import jax
import jax.numpy as jnp
from jax import lax
import numpy as np

D_MODEL = 1024
BATCH = 1
SEQ = 256
DEPTH = 2
DEC_BATCH = 8
DEC_SEQ = 8
PAST_LEN = 2048
PAGE_SIZE = 128

HEAD_DIM = 64
D_MIX = D_MODEL
N_MIX_HEADS = D_MIX // HEAD_DIM
H_B = N_MIX_HEADS // 4
H_A = (N_MIX_HEADS - H_B) // 2
H_C = N_MIX_HEADS - H_A - H_B
W_A = H_A * HEAD_DIM
W_B = H_B * HEAD_DIM
W_C = H_C * HEAD_DIM
DECAY_LORA = 64
AAA_LORA = 64
GATE_LORA = 128
COLS_A = 3 * W_A + DECAY_LORA + AAA_LORA + GATE_LORA
COLS_B = 4 * W_B
N_STATE = 128
N_GROUPS = 2
CONV_W = 4
CONV_DIM = W_C + 2 * N_GROUPS * N_STATE
COLS_C = W_C + CONV_DIM + H_C
IN_COLS = COLS_A + COLS_B + COLS_C
CHUNK = 64
ROPE_BASE = 10000.0
D_FF = ((8 * D_MODEL // 3 + 127) // 128) * 128
N_EXPERTS = 8
TOP_K = 2
D_FF_EXPERT = D_FF // TOP_K
N_DENSE = (DEPTH + 1) // 2
N_MOE = DEPTH // 2
RMS_EPS = 1e-6
GN_EPS = 64e-5
GATED_NORM_EPS = 1e-5

kernel_name = 'hybrid_rwkv7_retnet_mamba2_step'

def rmsnorm(x, g, eps=RMS_EPS):
    xf = x.astype(jnp.float32)
    y = xf * lax.rsqrt(jnp.mean(xf * xf, axis=-1, keepdims=True) + eps)
    return (y * g.astype(jnp.float32)).astype(x.dtype)

def chunk_len(T):
    return CHUNK if T % CHUNK == 0 else T

def to_chunks(t, L):
    b, T = t.shape[0], t.shape[1]
    return jnp.moveaxis(t.reshape((b, T // L, L) + t.shape[2:]), 1, 0)

def from_chunks(t):
    t = jnp.moveaxis(t, 0, 1)
    return t.reshape((t.shape[0], t.shape[1] * t.shape[2]) + t.shape[3:])

def rwkv7_recurrence(r, decay, k, v, kk, a, S0):
    def step(S, inp):
        r_t, w_t, k_t, v_t, kk_t, a_t = inp
        sa = jnp.einsum('bhvk,bhk->bhv', S, -kk_t)
        S = (S * w_t[:, :, None, :] + sa[..., None] * (kk_t * a_t)[:, :, None, :]
             + v_t[..., None] * k_t[:, :, None, :])
        return S, jnp.einsum('bhvk,bhk->bhv', S, r_t)
    xs = tuple(jnp.moveaxis(t, 1, 0) for t in (r, decay, k, v, kk, a))
    S, ys = lax.scan(step, S0, xs)
    return jnp.moveaxis(ys, 0, 1), S

def rwkv7_mixer(c, c_prev, S0, mu, w0, w_up, a0, a_up, g_up, k_k, k_a, r_k, ln_w, ln_b):
    f32 = jnp.float32
    b, T, _ = c.shape
    prev = jnp.concatenate([c_prev[:, None, :].astype(c.dtype), c[:, :-1]], axis=1)
    xm = c + (prev - c) * mu
    r = xm[..., :W_A]
    k = xm[..., W_A:2 * W_A]
    v = xm[..., 2 * W_A:3 * W_A]
    o = 3 * W_A
    wd = xm[..., o:o + DECAY_LORA]
    o += DECAY_LORA
    ad = xm[..., o:o + AAA_LORA]
    o += AAA_LORA
    gd = xm[..., o:o + GATE_LORA]
    w = (w0 + jnp.tanh(wd) @ w_up).astype(f32)
    decay = jnp.exp(-jnp.exp(-jax.nn.softplus(-w) - 0.5))
    a = jax.nn.sigmoid((a0 + ad @ a_up).astype(f32))
    g = (jax.nn.sigmoid(gd) @ g_up).astype(f32)
    heads = lambda t: t.astype(f32).reshape(b, T, H_A, HEAD_DIM)
    r, k, v, a, decay = heads(r), heads(k), heads(v), heads(a), heads(decay)
    kk = k * k_k.astype(f32).reshape(H_A, HEAD_DIM)
    kk = kk / jnp.maximum(jnp.sqrt(jnp.sum(kk * kk, axis=-1, keepdims=True)), 1e-12)
    k = k * (1.0 + (a - 1.0) * k_a.astype(f32).reshape(H_A, HEAD_DIM))
    y, S = rwkv7_recurrence(r, decay, k, v, kk, a, S0.astype(f32))
    mean = jnp.mean(y, axis=-1, keepdims=True)
    var = jnp.mean(jnp.square(y - mean), axis=-1, keepdims=True)
    y = ((y - mean) * lax.rsqrt(var + GN_EPS)).reshape(b, T, W_A)
    y = y * ln_w.astype(f32) + ln_b.astype(f32)
    bonus = jnp.sum(r * k * r_k.astype(f32), axis=-1, keepdims=True) * v
    y = (y + bonus.reshape(b, T, W_A)) * g
    return y.astype(c.dtype), c[:, -1], S

def rotate(t, cos, sin):
    t1, t2 = t[..., :HEAD_DIM // 2], t[..., HEAD_DIM // 2:]
    return jnp.concatenate([t1 * cos - t2 * sin, t1 * sin + t2 * cos], axis=-1)

def retention_chunked(q, k, v, S0):
    T, H = q.shape[1], q.shape[2]
    L = chunk_len(T)
    log_g = jnp.log(1.0 - 2.0 ** (-5.0 - jnp.arange(H, dtype=jnp.float32)))
    idx = jnp.arange(L, dtype=jnp.float32)
    diff = idx[:, None] - idx[None, :]
    intra = jnp.where(diff >= 0, jnp.exp(log_g[:, None, None] * jnp.maximum(diff, 0.0)), 0.0)
    q_decay = jnp.exp(log_g[:, None] * (idx[None, :] + 1.0))
    k_decay = jnp.exp(log_g[:, None] * (L - 1.0 - idx[None, :]))
    c_decay = jnp.exp(log_g * L)

    def step(S, inp):
        qc, kc, vc = inp
        scores = jnp.einsum('blhd,bmhd->bhlm', qc, kc) * intra
        out = jnp.einsum('bhlm,bmhd->blhd', scores, vc)
        out = out + jnp.einsum('blhk,bhkv,hl->blhv', qc, S, q_decay)
        S = S * c_decay[None, :, None, None] + jnp.einsum('blhk,blhv,hl->bhkv', kc, vc, k_decay)
        return S, out

    S, outs = lax.scan(step, S0, (to_chunks(q, L), to_chunks(k, L), to_chunks(v, L)))
    return from_chunks(outs), S

def retention_mixer(c, S0, pos0, norm_w):
    f32 = jnp.float32
    b, T, _ = c.shape
    heads = lambda t: t.astype(f32).reshape(b, T, H_B, HEAD_DIM)
    q = heads(c[..., :W_B])
    k = heads(c[..., W_B:2 * W_B])
    v = heads(c[..., 2 * W_B:3 * W_B])
    g = c[..., 3 * W_B:].astype(f32)
    pos = pos0 + jnp.arange(T, dtype=f32)
    theta = 1.0 / (ROPE_BASE ** jnp.linspace(0.0, 1.0, HEAD_DIM // 2, dtype=f32))
    ang = pos[:, None] * theta[None, :]
    cos, sin = jnp.cos(ang)[:, None, :], jnp.sin(ang)[:, None, :]
    q = rotate(q, cos, sin)
    k = rotate(k, cos, sin) * (HEAD_DIM ** -0.5)
    out, S = retention_chunked(q, k, v, S0.astype(f32))
    out = out * lax.rsqrt(jnp.mean(out * out, axis=-1, keepdims=True) + RMS_EPS)
    out = out.reshape(b, T, W_B) * norm_w.astype(f32)
    out = jax.nn.silu(g) * out
    return out.astype(c.dtype), S

def ssd_chunked(x, dt, A, Bm, Cm, h0):
    b, T, H, P = x.shape
    G, N = Bm.shape[2], Bm.shape[3]
    R = H // G
    L = chunk_len(T)
    x = x.reshape(b, T, G, R, P)
    dt = dt.reshape(b, T, G, R)
    A = A.reshape(G, R)
    h0 = h0.reshape(b, G, R, P, N)
    mask = jnp.tril(jnp.ones((L, L), dtype=bool))[None, :, :, None, None]

    def step(h, inp):
        xc, dtc, Bc, Cc = inp
        cum = jnp.cumsum(dtc * A, axis=1)
        seg = cum[:, :, None] - cum[:, None, :]
        decay = jnp.exp(jnp.where(mask, seg, -jnp.inf))
        cb = jnp.einsum('blgn,bmgn->blmg', Cc, Bc)
        wts = cb[..., None] * decay * dtc[:, None]
        y = jnp.einsum('blmgr,bmgrp->blgrp', wts, xc)
        y = y + jnp.einsum('blgn,bgrpn,blgr->blgrp', Cc, h, jnp.exp(cum))
        last = cum[:, -1]
        wk = jnp.exp(last[:, None] - cum) * dtc
        h = h * jnp.exp(last)[..., None, None] + jnp.einsum('blgr,blgrp,blgn->bgrpn', wk, xc, Bc)
        return h, y

    h, ys = lax.scan(step, h0, (to_chunks(x, L), to_chunks(dt, L), to_chunks(Bm, L), to_chunks(Cm, L)))
    return from_chunks(ys).reshape(b, T, H, P), h.reshape(b, H, P, N)

def mamba2_mixer(c, conv_prev, h0, conv_w, conv_b, dt_bias, a_log, d_skip, norm_w):
    f32 = jnp.float32
    b, T, _ = c.shape
    z = c[..., :W_C].astype(f32)
    xbc = c[..., W_C:W_C + CONV_DIM]
    dt_raw = c[..., W_C + CONV_DIM:].astype(f32)
    xpad = jnp.concatenate([conv_prev.astype(c.dtype), xbc], axis=1)
    conv = lax.conv_general_dilated(xpad, conv_w[:, None, :].astype(c.dtype), window_strides=(1,),
                                    padding='VALID', dimension_numbers=('NWC', 'WIO', 'NWC'),
                                    feature_group_count=CONV_DIM)
    xbc = jax.nn.silu(conv.astype(f32) + conv_b.astype(f32))
    xs = xbc[..., :W_C].reshape(b, T, H_C, HEAD_DIM)
    Bm = xbc[..., W_C:W_C + N_GROUPS * N_STATE].reshape(b, T, N_GROUPS, N_STATE)
    Cm = xbc[..., W_C + N_GROUPS * N_STATE:].reshape(b, T, N_GROUPS, N_STATE)
    dt = jax.nn.softplus(dt_raw + dt_bias.astype(f32))
    A = -jnp.exp(a_log.astype(f32))
    y, h = ssd_chunked(xs, dt, A, Bm, Cm, h0.astype(f32))
    y = y + d_skip.astype(f32)[:, None] * xs
    y = y.reshape(b, T, W_C) * jax.nn.silu(z)
    y = y * lax.rsqrt(jnp.mean(y * y, axis=-1, keepdims=True) + GATED_NORM_EPS) * norm_w.astype(f32)
    return y.astype(c.dtype), xpad[:, -(CONV_W - 1):], h

def swiglu(h, wg, wu, wd):
    return (jax.nn.silu(h @ wg) * (h @ wu)) @ wd

def moe_swiglu(h, router, wg, wu, wd):
    probs = jax.nn.softmax((h @ router).astype(jnp.float32), axis=-1)
    top_p, top_i = lax.top_k(probs, TOP_K)
    top_p = top_p / jnp.sum(top_p, axis=-1, keepdims=True)
    gates = jnp.sum(jax.nn.one_hot(top_i, N_EXPERTS, dtype=jnp.float32) * top_p[..., None], axis=-2)
    out = jnp.zeros_like(h)
    for e in range(N_EXPERTS):
        out = out + gates[..., e:e + 1].astype(h.dtype) * swiglu(h, wg[e], wu[e], wd[e])
    return out

def trunk(x, s_rwkv, s_shift, s_ret, s_ssm, s_conv, pos0, W):
    n_rwkv, n_shift, n_ret, n_ssm, n_conv = [], [], [], [], []
    for i in range(DEPTH):
        h = rmsnorm(x, W['norm_mix'][i])
        cp = h @ W['w_in'][i]
        ca = cp[..., :COLS_A]
        cb = cp[..., COLS_A:COLS_A + COLS_B]
        cc = cp[..., COLS_A + COLS_B:]
        ya, sh, Sa = rwkv7_mixer(ca, s_shift[i], s_rwkv[i], W['rwkv_mu'][i], W['rwkv_w0'][i],
                                 W['rwkv_w_up'][i], W['rwkv_a0'][i], W['rwkv_a_up'][i],
                                 W['rwkv_g_up'][i], W['rwkv_k_k'][i], W['rwkv_k_a'][i],
                                 W['rwkv_r_k'][i], W['rwkv_ln_w'][i], W['rwkv_ln_b'][i])
        yb, Sb = retention_mixer(cb, s_ret[i], pos0, W['ret_norm'][i])
        yc, cv, hc = mamba2_mixer(cc, s_conv[i], s_ssm[i], W['ssm_conv_w'][i], W['ssm_conv_b'][i],
                                  W['ssm_dt_bias'][i], W['ssm_a_log'][i], W['ssm_d'][i],
                                  W['ssm_norm'][i])
        x = x + jnp.concatenate([ya, yb, yc], axis=-1) @ W['w_out'][i]
        h = rmsnorm(x, W['norm_ffn'][i])
        j = i // 2
        if i % 2 == 0:
            x = x + swiglu(h, W['ffn_w_gate'][j], W['ffn_w_up'][j], W['ffn_w_down'][j])
        else:
            x = x + moe_swiglu(h, W['moe_router'][j], W['moe_w_gate'][j], W['moe_w_up'][j],
                               W['moe_w_down'][j])
        n_rwkv.append(Sa)
        n_shift.append(sh)
        n_ret.append(Sb)
        n_ssm.append(hc)
        n_conv.append(cv)
    y = rmsnorm(x, W['norm_final'])
    return (y, jnp.stack(n_rwkv), jnp.stack(n_shift), jnp.stack(n_ret), jnp.stack(n_ssm),
            jnp.stack(n_conv))

def setup_inputs(seed: int = 0) -> dict:
    key = jax.random.key(seed)
    ks = iter(jax.random.split(key, 48))
    f32 = jnp.float32

    def nrm(shape, scale):
        return scale * jax.random.normal(next(ks), shape, f32)

    def gain(shape):
        return 1.0 + nrm(shape, 0.02)

    x_prompt = nrm((BATCH, SEQ, D_MODEL), 1.0)
    x_sample = nrm((DEC_BATCH, DEC_SEQ, D_MODEL), 1.0)
    state_rwkv = nrm((DEPTH, DEC_BATCH, H_A, HEAD_DIM, HEAD_DIM), 0.5)
    state_shift = nrm((DEPTH, DEC_BATCH, COLS_A), 1.0)
    state_ret = nrm((DEPTH, DEC_BATCH, H_B, HEAD_DIM, HEAD_DIM), 0.5)
    state_ssm = nrm((DEPTH, DEC_BATCH, H_C, HEAD_DIM, N_STATE), 0.5)
    state_conv = nrm((DEPTH, DEC_BATCH, CONV_W - 1, CONV_DIM), 1.0)
    norm_mix = gain((DEPTH, D_MODEL))
    w_in = nrm((DEPTH, D_MODEL, IN_COLS), D_MODEL ** -0.5)
    rwkv_mu = jax.random.uniform(next(ks), (DEPTH, COLS_A), f32)
    rwkv_w0 = -2.0 + nrm((DEPTH, W_A), 1.0)
    rwkv_w_up = nrm((DEPTH, DECAY_LORA, W_A), 0.1 * DECAY_LORA ** -0.5)
    rwkv_a0 = nrm((DEPTH, W_A), 0.1)
    rwkv_a_up = nrm((DEPTH, AAA_LORA, W_A), 0.1 * AAA_LORA ** -0.5)
    rwkv_g_up = nrm((DEPTH, GATE_LORA, W_A), GATE_LORA ** -0.5)
    rwkv_k_k = 0.85 + nrm((DEPTH, W_A), 0.05)
    rwkv_k_a = 1.0 + nrm((DEPTH, W_A), 0.05)
    rwkv_r_k = nrm((DEPTH, H_A, HEAD_DIM), 0.1)
    rwkv_ln_w = gain((DEPTH, W_A))
    rwkv_ln_b = nrm((DEPTH, W_A), 0.02)
    ret_norm = gain((DEPTH, W_B))
    ssm_conv_w = nrm((DEPTH, CONV_W, CONV_DIM), CONV_W ** -0.5)
    ssm_conv_b = nrm((DEPTH, CONV_DIM), 0.02)
    dt0 = jnp.exp(jax.random.uniform(next(ks), (DEPTH, H_C), f32,
                                     minval=math.log(1e-3), maxval=math.log(1e-1)))
    ssm_dt_bias = dt0 + jnp.log(-jnp.expm1(-dt0))
    ssm_a_log = jnp.log(jax.random.uniform(next(ks), (DEPTH, H_C), f32, minval=1.0, maxval=16.0))
    ssm_d = 1.0 + nrm((DEPTH, H_C), 0.1)
    ssm_norm = gain((DEPTH, W_C))
    w_out = nrm((DEPTH, D_MIX, D_MODEL), D_MIX ** -0.5)
    norm_ffn = gain((DEPTH, D_MODEL))
    ffn_w_gate = nrm((N_DENSE, D_MODEL, D_FF), D_MODEL ** -0.5)
    ffn_w_up = nrm((N_DENSE, D_MODEL, D_FF), D_MODEL ** -0.5)
    ffn_w_down = nrm((N_DENSE, D_FF, D_MODEL), D_FF ** -0.5)
    moe_router = nrm((N_MOE, D_MODEL, N_EXPERTS), D_MODEL ** -0.5)
    moe_w_gate = nrm((N_MOE, N_EXPERTS, D_MODEL, D_FF_EXPERT), D_MODEL ** -0.5)
    moe_w_up = nrm((N_MOE, N_EXPERTS, D_MODEL, D_FF_EXPERT), D_MODEL ** -0.5)
    moe_w_down = nrm((N_MOE, N_EXPERTS, D_FF_EXPERT, D_MODEL), D_FF_EXPERT ** -0.5)
    norm_final = gain((D_MODEL,))
    return {'x_prompt': x_prompt, 'x_sample': x_sample, 'state_rwkv': state_rwkv,
            'state_shift': state_shift, 'state_ret': state_ret, 'state_ssm': state_ssm,
            'state_conv': state_conv, 'norm_mix': norm_mix, 'w_in': w_in, 'rwkv_mu': rwkv_mu,
            'rwkv_w0': rwkv_w0, 'rwkv_w_up': rwkv_w_up, 'rwkv_a0': rwkv_a0,
            'rwkv_a_up': rwkv_a_up, 'rwkv_g_up': rwkv_g_up, 'rwkv_k_k': rwkv_k_k,
            'rwkv_k_a': rwkv_k_a, 'rwkv_r_k': rwkv_r_k, 'rwkv_ln_w': rwkv_ln_w,
            'rwkv_ln_b': rwkv_ln_b, 'ret_norm': ret_norm, 'ssm_conv_w': ssm_conv_w,
            'ssm_conv_b': ssm_conv_b, 'ssm_dt_bias': ssm_dt_bias, 'ssm_a_log': ssm_a_log,
            'ssm_d': ssm_d, 'ssm_norm': ssm_norm, 'w_out': w_out, 'norm_ffn': norm_ffn,
            'ffn_w_gate': ffn_w_gate, 'ffn_w_up': ffn_w_up, 'ffn_w_down': ffn_w_down,
            'moe_router': moe_router, 'moe_w_gate': moe_w_gate, 'moe_w_up': moe_w_up,
            'moe_w_down': moe_w_down, 'norm_final': norm_final}

def reference(x_prompt, x_sample, state_rwkv, state_shift, state_ret, state_ssm, state_conv,
              norm_mix, w_in, rwkv_mu, rwkv_w0, rwkv_w_up, rwkv_a0, rwkv_a_up, rwkv_g_up,
              rwkv_k_k, rwkv_k_a, rwkv_r_k, rwkv_ln_w, rwkv_ln_b, ret_norm, ssm_conv_w,
              ssm_conv_b, ssm_dt_bias, ssm_a_log, ssm_d, ssm_norm, w_out, norm_ffn,
              ffn_w_gate, ffn_w_up, ffn_w_down, moe_router, moe_w_gate, moe_w_up, moe_w_down,
              norm_final):
    W = dict(norm_mix=norm_mix, w_in=w_in, rwkv_mu=rwkv_mu, rwkv_w0=rwkv_w0,
             rwkv_w_up=rwkv_w_up, rwkv_a0=rwkv_a0, rwkv_a_up=rwkv_a_up, rwkv_g_up=rwkv_g_up,
             rwkv_k_k=rwkv_k_k, rwkv_k_a=rwkv_k_a, rwkv_r_k=rwkv_r_k, rwkv_ln_w=rwkv_ln_w,
             rwkv_ln_b=rwkv_ln_b, ret_norm=ret_norm, ssm_conv_w=ssm_conv_w,
             ssm_conv_b=ssm_conv_b, ssm_dt_bias=ssm_dt_bias, ssm_a_log=ssm_a_log, ssm_d=ssm_d,
             ssm_norm=ssm_norm, w_out=w_out, norm_ffn=norm_ffn, ffn_w_gate=ffn_w_gate,
             ffn_w_up=ffn_w_up, ffn_w_down=ffn_w_down, moe_router=moe_router,
             moe_w_gate=moe_w_gate, moe_w_up=moe_w_up, moe_w_down=moe_w_down,
             norm_final=norm_final)
    f32 = jnp.float32
    bp = x_prompt.shape[0]
    y_prompt, p_rwkv, p_shift, p_ret, p_ssm, p_conv = trunk(
        x_prompt,
        jnp.zeros((DEPTH, bp, H_A, HEAD_DIM, HEAD_DIM), f32),
        jnp.zeros((DEPTH, bp, COLS_A), x_prompt.dtype),
        jnp.zeros((DEPTH, bp, H_B, HEAD_DIM, HEAD_DIM), f32),
        jnp.zeros((DEPTH, bp, H_C, HEAD_DIM, N_STATE), f32),
        jnp.zeros((DEPTH, bp, CONV_W - 1, CONV_DIM), x_prompt.dtype),
        0, W)
    y_sample, s_rwkv, s_shift, s_ret, s_ssm, s_conv = trunk(
        x_sample, state_rwkv, state_shift, state_ret, state_ssm, state_conv, PAST_LEN, W)
    return (y_prompt, y_sample,
            p_rwkv.astype(state_rwkv.dtype), p_shift.astype(state_shift.dtype),
            p_ret.astype(state_ret.dtype), p_ssm.astype(state_ssm.dtype),
            p_conv.astype(state_conv.dtype),
            s_rwkv.astype(state_rwkv.dtype), s_shift.astype(state_shift.dtype),
            s_ret.astype(state_ret.dtype), s_ssm.astype(state_ssm.dtype),
            s_conv.astype(state_conv.dtype))


_drawn_inputs = setup_inputs


def setup_inputs(seed=0):
    import zlib

    import numpy as np

    out = dict(_drawn_inputs(seed))
    spreads = {}
    factors = {'rwkv_w_up': 5.477,
     'rwkv_ln_b': 10.747,
     'norm_final': 19.254,
     'rwkv_ln_w': 11.902,
     'ret_norm': 6.78,
     'ssm_norm': 5.259,
     'norm_ffn': 4.223}
    for name, (base, spread) in spreads.items():
        noise = np.random.default_rng([zlib.crc32(name.encode()), seed]).standard_normal(out[name].shape)
        drawn = base * np.exp(spread * noise) if base else spread * noise
        out[name] = jnp.asarray(drawn.astype(out[name].dtype))
    for name, factor in factors.items():
        out[name] = (out[name] * factor).astype(out[name].dtype)
    return out
```

```python
from contextlib import ExitStack

import numpy as np
import concourse.bass as bass
from concourse import mybir

F32 = mybir.dt.float32
F32R = mybir.dt.float32r
ALU = mybir.AluOpType
ACT = mybir.ActivationFunctionType
AX = mybir.AxisListType

P = 128
D = 1024
SEQ = 256
DEPTH = 2
NSEQ = 8
STEP = 8
PAST = 2048
T = SEQ + NSEQ * STEP
KT = D // P
HD = 64
HA, HB, HC = 6, 4, 6
TA, TB, TC = HA // 2, HB // 2, HC // 2
COLS_A = 3 * HA * HD + 256
COLS_B = 4 * HB * HD
NST = 128
CONV = 4
CONV_DIM = HC * HD + 2 * 2 * NST
XT = CONV_DIM // P
FE = 1408
FT = FE // P
NEXP = 8
A_TILES = COLS_A // P
B_TILES = COLS_B // P
C_TILES = TC + XT
WIN = A_TILES + B_TILES + C_TILES + 1
EXP_SLOTS = 3 * FT
BLOCKS = [(0, 128), (128, 128), (256, 64)]
CH = 64
SQE = float(np.exp(-0.5))
EA, EX = 1 + SEQ, 3 + SEQ
WA_, WX_ = EA + NSEQ * (STEP + 1), EX + NSEQ * (STEP + 3)

RAW, HI = 11, 3
G_IN = [0, WIN + KT + 2 * EXP_SLOTS]
G_OUT = [g + WIN for g in G_IN]
G_FFN = [G_OUT[0] + KT, G_OUT[1] + KT + 1]
N_E = [2, NEXP]
E0 = [0, 2]
G_END = G_FFN[1] + NEXP * EXP_SLOTS
N_SLOTS = G_END + HI

PAR = {}


def _par(name, n, at=[0]):
    PAR[name] = at[0]
    at[0] += n
    return at[0]


for _n, _w in [("g_mix", 8), ("g_ffn", 8), ("g_fin", 8), ("mu", A_TILES), ("w0", 3), ("a0", 3), ("k_k", 3),
               ("k_a", 3), ("r_k", 3), ("ln_w", 3), ("ln_b", 3), ("ret_norm", 2), ("conv_w", 4 * XT),
               ("conv_b", XT), ("d", 3), ("ssm_norm", 3), ("dt_bias", 1), ("a_log", 1),
               ("wa_up", 384), ("g_up", 384)]:
    NPAR = _par(_n, _w)


def constants():
    i = np.arange(P)
    c = {}
    c["ident"] = np.eye(P)
    c["ones"] = np.ones((P, P))
    c["bd"] = (i[:, None] // HD == i[None, :] // HD) * 1.0
    c["swap"] = (i[:, None] == (i[None, :] ^ 32)) * 1.0
    pos = np.concatenate([np.arange(SEQ), np.tile(PAST + np.arange(STEP), NSEQ)]).astype(np.float32)
    theta = (1.0 / (np.float32(10000.0) ** np.linspace(0.0, 1.0, HD // 2, dtype=np.float32))).astype(np.float32)
    ang = (pos[None, :] * theta[i % 32][:, None]).astype(np.float32).astype(np.float64)
    c["cos"] = np.cos(ang)
    c["sin"] = np.sin(ang) * np.where(i % HD < 32, -1.0, 1.0)[:, None]
    gam = 1.0 - 2.0 ** (-5.0 - np.arange(HB))
    hb = (np.arange(TB)[None, :] * 2 + (i // HD)[:, None])
    g = gam[hb]
    at = np.concatenate([np.arange(SEQ) % P, np.tile(np.arange(STEP), NSEQ)])
    ln = np.concatenate([np.full(SEQ, P), np.full(NSEQ * STEP, STEP)])
    c["qdec"] = g[:, :, None] ** (at + 1)[None, None, :]
    c["kdec"] = g[:, :, None] ** (ln - 1 - at)[None, None, :]
    c["cdec"] = np.stack([g ** P, g ** STEP], 1)
    diff = i[None, :] - i[:, None]
    same8 = i[:, None] // STEP == i[None, :] // STEP
    gam = gam[[0, 2, 1, 3]]
    c["rmask"] = np.where((diff >= 0)[:, None], gam[None, :, None] ** np.maximum(diff, 0)[:, None], 0.0)
    c["rmask8"] = c["rmask"][:, :, :HD] * same8[:, None, :HD]
    c["causal"] = (diff >= 0) * 1.0
    c["causal8"] = ((diff >= 0) & same8)[:, :HD] * 1.0
    j = np.arange(CH)
    s, t = (i % CH)[:, None], j[None, :]
    s8 = s // STEP == t // STEP
    c["strict"], c["incl"] = (s < t) * 1.0, (s <= t) * 1.0
    c["strict8"], c["incl8"] = (s < t) & s8, (s <= t) & s8
    c["i64"] = (s == t) * 1.0
    c["lev"] = np.stack([(s >> (q + 1) == t >> (q + 1)) & (s >> q & 1 == 0) & (t >> q & 1 == 1)
                         for q in range(6)], 1)
    c["scan64"] = np.tile((np.arange(P) % CH != 0) * 1.0, (P, 1))
    c["scan8"] = np.tile((np.arange(CH) % STEP != 0) * 1.0, (P, 1))
    c["scanm"] = np.tile((at != 0) * 1.0, (P, 1))
    c["seq"] = (i[:, None] // STEP == np.arange(NSEQ)[None, :]) * 1.0
    c["sel"] = np.repeat(i[:, None] == np.arange(NEXP)[None, :], P, 1) * 1.0
    c["before"] = np.tile((np.arange(8)[None, :] < np.arange(8)[:, None]).reshape(1, 64), (P, 1)) * 1.0
    c["eps"] = np.tile(np.array([1e-6, 64e-5, 1e-5, 0.0]), (P, 1))
    cols, parts, n = {}, [], 0
    for k, v in c.items():
        v = np.asarray(v, np.float64).reshape(P, -1)
        cols[k] = (n, v.shape[1])
        parts.append(v)
        n += v.shape[1]
    return np.ascontiguousarray(np.concatenate(parts, 1).astype(np.float32)), cols


def trunk(nc, x_in, w_in, consts_in, par_in, s_rw, s_rt, s_mb, s_sh, s_cv,
          y_out, p_rw, p_rt, p_mb, o_rw, o_rt, o_mb, o_sh, o_cv):
    CC = constants()[1]
    NCONST = consts_in.shape[1]
    ctx = ExitStack()
    with ctx:
        sems = {}

        def S(name):
            if name not in sems:
                sems[name] = ctx.enter_context(nc.semaphore(name))
            return sems[name]

        base = (nc.sbuf_base + 63) // 64 * 64
        top = [base]

        def sb(name, shape, dt=F32, offset=None):
            size = int(np.prod(shape[1:])) * 4
            at = top[0] if offset is None else offset
            t = nc.alloc_sbuf_tensor_at(name, shape, dt, offset=at)
            if offset is None:
                top[0] = (at + size + 63) // 64 * 64
            return t

        raw_at = top[0]
        wraw = sb("wraw", [P, RAW, D])
        wlo = sb("wlo", [P, RAW, D], F32R, offset=raw_at)
        whi = sb("whi", [P, HI, D], F32R)
        x = sb("x", [P, KT, T])
        hh = sb("hh", [P, KT, T], F32R)
        hl = sb("hl", [P, KT, T], F32R)
        rstd = sb("rstd", [P, T])
        cst = sb("cst", [P, NCONST])
        par = sb("par", [P, NPAR])
        srw_p = sb("srw_p", [P, TA, HD])
        srt_p = sb("srt_p", [P, TB, HD])
        smb_p = sb("smb_p", [P, HC * HD])
        sh_out = sb("sh_out", [P, A_TILES, 1 + NSEQ])
        sh_in = sb("sh_in", [P, A_TILES, NSEQ])
        cv_in = sb("cv_in", [P, XT, NSEQ, 3])
        cv_out = sb("cv_out", [P, XT, 1 + NSEQ, 3])
        area = top[0]
        cR = sb("cR", [P, A_TILES, WA_])
        cB = sb("cB", [P, B_TILES, T])
        cZ = sb("cZ", [P, TC, T])
        cX = sb("cX", [P, XT, WX_])
        cD = sb("cD", [8, T])
        work = top[0]
        srw = sb("srw", [P, TA, NSEQ, HD])
        lent = top[0]
        TM, Wm = (sb(n, [P, HA, CH]) for n in ("TM", "Wm"))
        Sbd = sb("Sbd", [P, TA, P])
        AL = sb("AL", [P, 2, HA, CH])
        tw = sb("tw", [P, P])
        rwx = sb("rwx", [HD, 2, NSEQ, P], offset=lent)
        assert lent + 8 * 1024 == top[0]
        Dx = sb("Dx", [P, A_TILES, P])
        U = {k: sb("u_" + k, [P, TA, P]) for k in
             ("sg", "L", "P", "Pi", "Pm", "aa", "kr", "kp", "t1", "be", "rho", "g")}
        U["Lm"], U["sq"], U["br"], U["ka"] = U["sg"], U["rho"], U["t1"], U["Pi"]
        U["kk"], U["al"], U["bonus"] = U["kr"], U["Pm"], U["L"]
        gs = U["rho"][:, 0, :]
        tok = sb("tok", [P, 3, TA, P])
        AB, C12 = (sb(n, [P, 2, 2, TA, CH]) for n in ("AB", "C12"))
        TT = sb("TT", [P, HA, CH])
        Rs = sb("Rs", [P, HA, CH])
        Rs0 = Rs[:, 0:TA, :]
        SA = U["sg"][:, :, :].rearrange("p t (h c) -> p (t h) c", c=CH)
        rw_end = top[0]
        top[0] = work
        qk = sb("qk", [P, 4, P])
        qk2 = sb("qk2", [P, 4, P])
        qkd = sb("qkd", [P, 4, P])
        rsc = sb("rsc", [P, HB, P])
        vkt = sb("vkt", [P, 4, P])
        vx = sb("vx", [HD, HB, NSEQ, HD])
        ro = sb("ro", [P, TB, P])
        rsq = sb("rsq", [P, TB, P])
        rsg = sb("rsg", [P, TB, P])
        srt = sb("srt", [P, TB, NSEQ, HD])
        rt_end = top[0]
        top[0] = work
        smb = sb("smb", [P, 2, NSEQ, 3, HD])
        dd = {k: sb("d_" + k, [8, T]) for k in ("x", "e", "z", "z2", "p", "dt")}
        dd["dA"], dd["cum"], dd["lm"], dd["wk"] = dd["z"], dd["p"], dd["z2"], dd["e"]
        an = sb("an", [8, 1])
        xc = sb("xc", [P, XT, P])
        xwe = sb("xwe", [HD, NSEQ, 3, HD])
        xcs = sb("xcs", [P, XT, P], offset=top[0] - NSEQ * 3 * HD * 4)
        tk3 = sb("tk3", [P, 3, HC])
        ecb = sb("ecb", [P, HC, P])
        seg = sb("seg", [P, HC, P])
        xdt = sb("xdt", [P, HC, HD])
        xw = sb("xw", [P, HC, HD])
        Btk = sb("Btk", [P, 2, P])
        cbm = sb("cbm", [P, 2, P])
        wts = sb("wts", [P, HC, P])
        cde = sb("cde", [P, HC, P])
        yz = sb("yz", [P, TC, P])
        ysq = sb("ysq", [P, TC, P])
        zs = sb("zs", [P, TC, P])
        mb_end = top[0]
        mix_end = max(rw_end, rt_end, mb_end)
        htmp = sb("htmp", [P, 2, T], offset=mix_end - 4 * T * 4)
        sqb = sb("sqb", [P, 2, T], offset=mix_end - 2 * T * 4)
        top[0] = area
        hidh = sb("hidh", [P, FT, T], F32R)
        hidl = sb("hidl", [P, FT, T], F32R)
        sil = sb("sil", [P, 2, T])
        hid = sb("hid", [P, 2, T])
        yt = sb("yt", [P, 4, T])
        gbc = sb("gbc", [P, NEXP, T])
        lg = sb("lg", [NEXP, T])
        rt = {k: sb("rt_" + k, [P, 3, NEXP]) for k in ("l", "e", "p", "rank", "g")}
        rt1 = sb("rt1", [P, 3, 4])
        cmp = sb("cmp", [P, 3, NEXP, NEXP])
        cmq = sb("cmq", [P, 3, NEXP, NEXP])
        assert max(mix_end, top[0]) <= nc.sbuf_usable_end, (mix_end, top[0], nc.sbuf_usable_end)

        B = [ctx.enter_context(nc.psum_tensor(f"bank{i}", [P, 512], F32)) for i in range(8)]

        def C(name, lo=0, n=None, rows=slice(0, P)):
            at, w = CC[name]
            return cst[rows, at + lo:at + (w if n is None else lo + n)]

        def V(name, i=0, n=1, rows=slice(0, P)):
            return par[rows, PAR[name] + i:PAR[name] + i + n]

        def over(ap, n):
            return ap.unsqueeze(2).to_broadcast([ap.shape[0], ap.shape[1], n])

        def rep(ap, n):
            return ap.unsqueeze(1).to_broadcast([ap.shape[0], n, ap.shape[1]])

        def bank(b, n_tiles, n, rows=slice(0, P)):
            return B[b][rows, 0:n_tiles * P].rearrange("p (a c) -> p a c", c=P)[:, :, 0:n]

        def b64(b, k, rows=slice(0, P)):
            return B[b][rows, 0:k * HD].rearrange("p (a c) -> p a c", c=HD)

        def halves(ap, q, odd):
            return ap.rearrange("p h (a o s) -> p h a o s", o=2, s=1 << q)[:, :, :, odd, :]

        def half1(ap, q, odd):
            return ap.rearrange("p (a o s) -> p a o s", o=2, s=1 << q)[:, :, odd, :]

        def c3(ap, q):
            return ap.rearrange("p h (a s) -> p h a s", s=1 << q)

        def ho(h):
            return (h % 2) * TA + h // 2

        def levels(b):
            return 3 if b == 2 else 6

        def chunks(b):
            return 1 if b == 2 else 2

        def expert_loop(eng, l, body):
            with eng.Fori(0, N_E[l]) as i:
                body(i, i * EXP_SLOTS + G_FFN[l], i + E0[l])

        block = ctx.enter_context(nc.Block())

        @block.sync
        def _(sp):
            def slot(g, ring):
                if not isinstance(g, int) or g >= RAW:
                    sp.wait_ge(S("slot_used"), g - RAW + 1)
                if isinstance(g, int):
                    sp.dma_start(wraw[:, ring % RAW, :], w_in[g, :, :]).then_inc(S(f"slot_in{ring % RAW}"), 16)
                else:
                    src = w_in[bass.ds(g, 1), :, :].rearrange("o p c -> (o p) c")
                    sp.dma_start(wraw[:, ring % RAW, :], src).then_inc(S(f"slot_in{ring % RAW}"), 16)

            sp.dma_start(x[:, :, :], x_in).then_inc(S("x_in"), 16)
            for l in range(DEPTH):
                for g in range(G_IN[l], G_FFN[l]):
                    slot(g, g)

                def body(i, g, e):
                    for j in range(EXP_SLOTS):
                        slot(g + j, G_FFN[l] + j)
                expert_loop(sp, l, body)
            for g in range(G_END, N_SLOTS):
                slot(g, g)
            sp.wait_ge(S("y_done"), 1)
            sp.dma_start(y_out, x[:, :, :]).then_inc(S("y_out"), 16)
            sp.wait_ge(S("y_out"), 16)

        @block.tensor
        def _(pe):
            mm = pe.matmul

            def mx(out, lhsT, rhs, start, stop):
                return pe.matmul(out, lhsT, rhs, start=start, stop=stop, skip_group_check=True)

            def three(out, k, slot_ring, rh, rl, first, last):
                hi = whi[:, slot_ring % HI, k * P:(k + 1) * P]
                lo = wlo[:, slot_ring % RAW, k * P:(k + 1) * P]
                mm(out, hi, rh, start=first, stop=False)
                mm(out, hi, rl, start=False, stop=False)
                return mm(out, lo, rh, start=False, stop=last)

            def full_slot(g, ring, out, h_from=None):
                pe.wait_ge(S("slot_split"), g + 1)
                for k in range(KT):
                    if h_from is not None:
                        pe.wait_ge(S("h_split"), h_from + k + 1)
                    m = three(out, k, ring, hh[:, k, :], hl[:, k, :], k == 0, k == KT - 1)
                m.then_inc(S("slot_used"), 1)

            def norm(i):
                for k in range(KT):
                    pe.wait_ge(S("sq_ready"), KT * i + k + 1)
                    m = mm(B[0][:, 0:T], C("ones"), sqb[:, k % 2, :], start=(k == 0), stop=(k == KT - 1))
                    m.then_inc(S("sq_used"), 1)

            def rwkv(l, b):
                it, n = 3 * l + b + 1, BLOCKS[b][1]
                nch, cb, lv = chunks(b), 5 * l + 2 * b, 15 * l + 6 * b
                pe.wait_ge(S("rw_lora"), it)
                for q, (rows, src, name) in enumerate([(slice(0, 64), tw[0:64, 0:n], "wa_up"),
                                                       (slice(64, P), Dx[64:P, 9, 0:n], "wa_up"),
                                                       (slice(0, P), gs[:, 0:n], "g_up")]):
                    for t in range(TA):
                        m = mm(B[q][:, t * P:t * P + n], V(name, t * P, P, rows), src, start=True, stop=True)
                    m.then_inc(S("rw_up"), 1)
                pe.wait_ge(S("rw_sq"), it)
                mm(bank(3, 3, n), C("bd"), U["sq"][:, :, 0:n], start=True, stop=True).then_inc(S("rw_ss"), 1)
                pe.wait_ge(S("rw_br"), it)
                mm(bank(4, 3, n), C("bd"), U["br"][:, :, 0:n], start=True, stop=True).then_inc(S("rw_bsum"), 1)
                pe.wait_ge(S("rw_ops"), it)
                pe.wait_ge(S("rw_sig"), 3 * it)
                for q, (bk, src) in enumerate([(5, Dx[:, 6:9, 0:n]), (0, U["be"][:, :, 0:n]), (1, U["ka"][:, :, 0:n])]):
                    for t in range(TA):
                        m = pe.transpose(B[bk][0:n, t * P:(t + 1) * P], src[:, t, :], C("ident"))
                    m.then_inc(S("rw_tr"), 1)
                pe.wait_ge(S("rw_ssm"), it)
                for q, bk in ((0, 2), (1, 4)):
                    if q == 1:
                        pe.wait_ge(S("rw_bonus"), it)
                        pe.wait_ge(S("rw_tok"), 3 * it)
                    for par_ in range(2):
                        r = slice(64 * par_, 64 * par_ + 64)
                        for z, lh in enumerate(("be", "ka")):
                            for t in range(TA):
                                for c in range(nch):
                                    lo = (z * TA + t) * CH
                                    m = mm(B[bk + par_][64 * c:64 * c + 64, lo:lo + CH],
                                           U[lh][r, t, c * CH:(c + 1) * CH],
                                           U[("al", "rho")[q]][r, t, c * CH:(c + 1) * CH], start=True, stop=True)
                        m.then_inc(S("rw_sc"), 1)
                for q in range(levels(b)):
                    pe.wait_ge(S("rw_T"), lv + q + it)
                    pe.wait_ge(S("rw_AL"), lv + q + 1)
                    for h in range(HA):
                        for c in range(nch):
                            r = slice(64 * c, 64 * c + 64)
                            m = mm(B[0][r, h * CH:(h + 1) * CH], AL[r, q % 2, h, :], TM[r, h, :], start=True, stop=True)
                    m.then_inc(S("rw_W"), 1)
                    pe.wait_ge(S("rw_Wc"), lv + q + 1)
                    if q == 0:
                        pe.wait_ge(S("rw_AT"), it)
                    for bk, odd in ((1, 0), (2, 1)):
                        for h in range(HA):
                            for c in range(nch):
                                r = slice(64 * c, 64 * c + 64)
                                out = B[bk][r, h * 32:(h + 1) * 32]
                                if odd:
                                    m = mm(out, Wm[r, h, :], half1(TT[r, h, :], q, 1), start=True, stop=True)
                                else:
                                    m = mm(out, TT[r, h, :], half1(Wm[r, h, :], q, 0), start=True, stop=True)
                    m.then_inc(S("rw_TW"), 1)
                pe.wait_ge(S("rw_T"), lv + levels(b) + it)
                pe.wait_ge(S("rw_C"), it)
                for c in range(nch):
                    r = slice(64 * c, 64 * c + 64)
                    cs = slice(c * CH, (c + 1) * CH)
                    vt, bt, kt = (tok[r, q, :, :].rearrange("p a c -> p (a c)") for q in range(3))
                    if b == 2:
                        pe.wait_ge(S("srw_in"), 16 * (l + 1))
                        for h in range(HA):
                            p = slice(64 * (h % 2), 64 * (h % 2) + 64)
                            for s in range(NSEQ):
                                m = mm(B[0][p, (h // 2) * CH + s * STEP:(h // 2) * CH + (s + 1) * STEP],
                                       srw[p, h // 2, s, :], U["al"][p, h // 2, s * STEP:(s + 1) * STEP],
                                       start=True, stop=True)
                        m.then_inc(S("rw_S0"), 1)
                        pe.wait_ge(S("rw_S0c"), l + 1)
                    else:
                        pe.wait_ge(S("rw_Sbd"), 5 * l + 2 * b + c + 1)
                    for t in range(TA):
                        pair = B[3][r, t * P:(t + 1) * P]
                        for o in range(2):
                            hs = slice(t * P + o * HD, t * P + (o + 1) * HD)
                            mx(B[3][r, hs], AB[r, o, 1, t, :], vt[:, hs], o == 0, False)
                        if b == 2:
                            m = mx(pair, Rs0[:, t, :], C("ident"), False, True)
                        else:
                            m = mx(pair, U["al"][:, t, cs], Sbd[:, t, :], False, True)
                    m.then_inc(S("rw_R"), 1)
                    pe.wait_ge(S("rw_Rc"), cb + c + 1)
                    for h in range(HA):
                        m = mm(B[4][r, h * HD:(h + 1) * HD], TT[r, ho(h), :], Rs[r, h, :], start=True, stop=True)
                    m.then_inc(S("rw_SA"), 1)
                    pe.wait_ge(S("rw_SAc"), cb + c + 1)
                    if b < 2:
                        for h in range(HA):
                            p = slice(64 * (h % 2), 64 * (h % 2) + 64)
                            out = B[0][p, (h // 2) * HD:(h // 2 + 1) * HD]
                            hs = slice(h * HD, (h + 1) * HD)
                            mx(out, bt[:, hs], SA[r, h, :], True, False)
                            m = mx(out, kt[:, hs], vt[:, hs], False, True)
                        m.then_inc(S("rw_dS"), 1)
                    for h in range(HA):
                        p = slice(64 * (h % 2), 64 * (h % 2) + 64)
                        lo = (h // 2) * P + c * CH
                        out = B[5][p, lo:lo + CH]
                        mx(out, SA[r, h, :], C12[r, h % 2, 0, h // 2, :], True, False)
                        m = mx(out, vt[:, h * HD:(h + 1) * HD], C12[r, h % 2, 1, h // 2, :], False, b == 2)
                        if b == 2:
                            for s in range(NSEQ):
                                t8 = slice(s * STEP, (s + 1) * STEP)
                                m = mm(B[0][p, (h // 2) * P + s * STEP:(h // 2) * P + (s + 1) * STEP], srw[p, h // 2, s, :],
                                       U["rho"][p, h // 2, t8], start=True, stop=True)
                        elif h % 2:
                            m = mx(B[5][:, lo:lo + CH], Sbd[:, h // 2, :], U["rho"][:, h // 2, cs], False, True)
                    m.then_inc(S("rw_y"), 1)
                if b == 2:
                    for t in range(TA):
                        pe.wait_ge(S("rw_xs"), 3 * l + t + 1)
                        pe.wait_ge(S("rw_xv"), 3 * l + t + 1)
                        for h in (2 * t, 2 * t + 1):
                            p = slice(64 * (h % 2), 64 * (h % 2) + 64)
                            o = slice((h % 2) * HD, (h % 2) * HD + HD)
                            hs = slice(h * HD, (h + 1) * HD)
                            mx(B[1 + t][p, :], bt[:, hs], rwx[:, 0, :, o], True, False)
                            m = mx(B[1 + t][p, :], kt[:, hs], rwx[:, 1, :, o], False, True)
                        m.then_inc(S("rw_ds"), 1)
                pe.wait_ge(S("rw_yc"), it)
                if b == 2:
                    pe.wait_ge(S("rw_sSa"), l + 1)
                mm(bank(3, 3, n), C("bd"), U["kr"][:, :, 0:n], start=True, stop=True).then_inc(S("rw_mean"), 1)
                pe.wait_ge(S("rw_ysq"), it)
                mm(bank(4, 3, n), C("bd"), U["sq"][:, :, 0:n], start=True, stop=True).then_inc(S("rw_var"), 1)

            def retention(l, b):
                it, (c0, n) = 3 * l + b + 1, BLOCKS[b]
                pe.wait_ge(S("mix_done"), 9 * l + 3 + b)
                mm(bank(0, 4, n), C("swap"), cB[:, 0:4, c0:c0 + n], start=True, stop=True).then_inc(S("rt_sw"), 1)
                pe.wait_ge(S("rt_qk"), it)
                for o in range(2):
                    p = slice(64 * o, 64 * o + 64)
                    for t in range(TB):
                        m = mm(B[(1, 5)[o]][0:n, t * P:t * P + n], qk[p, 2 + t, 0:n], qk[p, t, 0:n], start=True, stop=True)
                m.then_inc(S("rt_sc"), 1)
                pe.wait_ge(S("rt_dec"), it)
                for q in range(2):
                    pe.transpose(B[2][0:n, q * P:(q + 1) * P], cB[:, 4 + q, c0:c0 + n], C("ident"))
                for q in range(2):
                    m = pe.transpose(B[2][0:n, (2 + q) * P:(3 + q) * P], qkd[:, 2 + q, 0:n], C("ident"))
                m.then_inc(S("rt_tr"), 1)
                pe.wait_ge(S("rt_tok"), it)
                pe.wait_ge(S("rt_scm"), it)
                if b == 2:
                    pe.wait_ge(S("srt_in"), 16 * (l + 1))
                else:
                    pe.wait_ge(S("zeroed"), l + 1)
                    if b > 0:
                        pe.wait_ge(S("rt_S"), 2 * l + b)
                for h in range(HB):
                    p = slice(64 * (h % 2), 64 * (h % 2) + 64)
                    lo = (h // 2) * P
                    mx(B[3][p, lo:lo + n], vkt[0:n, h // 2, 64 * (h % 2):64 * (h % 2) + 64],
                       rsc[0:n, (h % 2) * TB + h // 2, 0:n], True, b == 2)
                    if b == 2:
                        for s in range(NSEQ):
                            m = mm(B[5][p, lo + s * STEP:lo + (s + 1) * STEP], srt[p, h // 2, s, :],
                                   qkd[p, h // 2, s * STEP:(s + 1) * STEP], start=True, stop=True)
                    else:
                        m = mx(B[3][p, lo:lo + n], srt_p[p, h // 2, :], qkd[p, h // 2, 0:n], False, True)
                m.then_inc(S("rt_o"), 1)
                if b == 2:
                    pe.wait_ge(S("rt_vx"), l + 1)
                for h in range(HB):
                    p = slice(64 * (h % 2), 64 * (h % 2) + 64)
                    kd = vkt[0:n, 2 + h // 2, 64 * (h % 2):64 * (h % 2) + 64]
                    if b == 2:
                        m = mm(B[(4, 1)[h // 2]][p, :], kd, vx[:, h, :, :], start=True, stop=True)
                    else:
                        m = mm(B[4][p, (h // 2) * HD:(h // 2 + 1) * HD], kd,
                               vkt[0:n, h // 2, 64 * (h % 2):64 * (h % 2) + 64], start=True, stop=True)
                m.then_inc(S("rt_dS"), 1)
                pe.wait_ge(S("rt_sq"), it)
                mm(bank(0, 2, n), C("bd"), rsq[:, :, 0:n], start=True, stop=True).then_inc(S("rt_ms"), 1)

            def mamba(l, b):
                it, (c0, n) = 3 * l + b + 1, BLOCKS[b]
                if b == 0:
                    pe.wait_ge(S("mb_dt"), l + 1)
                pe.wait_ge(S("mix_done"), 9 * l + 6 + b)
                for q, k in enumerate(("dt", "cum", "wk")):
                    m = pe.transpose(B[5][0:n, q * HC:(q + 1) * HC], dd[k][0:HC, c0:c0 + n], C("ident", 0, HC, slice(0, HC)))
                m.then_inc(S("mb_t3"), 1)
                for h in range(HC):
                    m = mm(B[h // 3][:, (h % 3) * P:(h % 3) * P + n], C("sel", h * P, P, slice(0, HC)),
                           dd["cum"][0:HC, c0:c0 + n], start=True, stop=True)
                m.then_inc(S("mb_cb"), 1)
                pe.wait_ge(S("mb_xc"), it)
                for q in range(3):
                    m = pe.transpose(B[2][0:n, q * P:(q + 1) * P], xc[:, q, 0:n], C("ident"))
                for q in range(2):
                    m = pe.transpose(B[3][0:n, q * P:(q + 1) * P], xc[:, 3 + q, 0:n], C("ident"))
                m.then_inc(S("mb_tB"), 1)
                for q in range(2):
                    m = mm(B[4][0:n, q * P:q * P + n], xc[:, 3 + q, 0:n], xc[:, 5 + q, 0:n], start=True, stop=True)
                m.then_inc(S("mb_BC"), 1)
                pe.wait_ge(S("mb_tk3"), it)
                pe.wait_ge(S("mb_xdt"), it)
                pe.wait_ge(S("mb_wts"), it)
                pe.wait_ge(S("mb_cde"), it)
                if b == 2:
                    pe.wait_ge(S("smb_in"), 16 * (l + 1))
                else:
                    pe.wait_ge(S("zeroed"), l + 1)
                    if b > 0:
                        pe.wait_ge(S("mb_S"), 2 * l + b)
                for h in range(HC):
                    p = slice(64 * (h % 2), 64 * (h % 2) + 64)
                    lo = (h // 2) * P
                    mx(B[5][p, lo:lo + n], xdt[0:n, h, :], wts[0:n, h, 0:n], True, False)
                    if b == 2:
                        for s in range(NSEQ):
                            m = mx(B[5][p, lo + s * STEP:lo + (s + 1) * STEP], smb[:, h // 3, s, h % 3, :],
                                   cde[:, h, s * STEP:(s + 1) * STEP], False, s == NSEQ - 1)
                    else:
                        m = mx(B[5][p, lo:lo + n], smb_p[:, h * HD:(h + 1) * HD], cde[:, h, 0:n], False, True)
                m.then_inc(S("mb_y"), 1)
                pe.wait_ge(S("mb_Btk"), it)
                if b == 2:
                    for g in range(2):
                        pe.wait_ge(S("mb_xwe"), 2 * l + g + 1)
                        if g == 1:
                            pe.wait_ge(S("mb_ds_used"), 2 * l + 1)
                        flat = xwe[:, :, :, :].rearrange("p s h d -> p (s h d)")
                        for q in range(3):
                            m = mm(B[q][:, :], Btk[0:n, g, :], flat[:, q * 512:(q + 1) * 512], start=True, stop=True)
                        m.then_inc(S("mb_ds"), 1)
                else:
                    for g in range(2):
                        m = mm(B[0][:, g * 192:(g + 1) * 192], Btk[0:n, g, :], xw[0:n, 3 * g:3 * g + 3, :],
                               start=True, stop=True)
                    m.then_inc(S("mb_dS"), 1)
                pe.wait_ge(S("mb_sq"), it)
                for q in range(3):
                    m = mm(B[4][:, 0:n], C("ones"), ysq[:, q, 0:n], start=(q == 0), stop=(q == 2))
                m.then_inc(S("mb_ms"), 1)

            pe.wait_ge(S("const_in"), 16)
            for l in range(DEPTH):
                pe.wait_ge(S("par_in"), 16 * (l + 1))
                norm(2 * l)
                for j in range(WIN):
                    if j >= 2:
                        pe.wait_ge(S("in_read"), WIN * l + j - 1)
                    full_slot(G_IN[l] + j, G_IN[l] + j, B[6 + j % 2][:, 0:T], KT * 2 * l if j == 0 else None)
                for b in range(3):
                    rwkv(l, b)
                for b in range(3):
                    retention(l, b)
                for b in range(3):
                    mamba(l, b)
                pe.wait_ge(S("mix_done"), 9 * (l + 1))
                for j in range(KT):
                    if j >= 2:
                        pe.wait_ge(S("out_read"), KT * l + j - 1)
                    full_slot(G_OUT[l] + j, G_OUT[l] + j, B[6 + j % 2][:, 0:T])
                norm(2 * l + 1)
                pe.wait_ge(S("h_split"), KT * (2 * l + 2))
                if l == DEPTH - 1:
                    full_slot(G_FFN[1] - 1, G_FFN[1] - 1, B[6][:, 0:T])
                    pe.wait_ge(S("lg"), 1)
                    for q, (c0, n) in enumerate(BLOCKS):
                        m = pe.transpose(B[7][0:n, q * NEXP:(q + 1) * NEXP], lg[:, c0:c0 + n],
                                         C("ident", 0, NEXP, slice(0, NEXP)))
                    m.then_inc(S("lgT"), 1)
                    pe.wait_ge(S("gates"), 1)
                    for q, (c0, n) in enumerate(BLOCKS):
                        m = pe.transpose(B[5][0:NEXP, c0:c0 + n], rt["g"][0:n, q, :], C("ident", 0, n, slice(0, n)))
                    m.then_inc(S("lgT"), 1)
                    pe.wait_ge(S("lg"), 2)
                    for e in range(NEXP):
                        if e >= 2:
                            pe.wait_ge(S("gbc"), e - 1)
                        mm(B[e % 2][:, 0:T], C("sel", e * P, P, slice(0, NEXP)), lg[:, :],
                           start=True, stop=True).then_inc(S("gb"), 1)
                    pe.wait_ge(S("gbc"), NEXP)

                def body(i, g, e):
                    for f in range(FT):
                        pe.wait_ge(S("gu_free"), e * FT + f + 1)
                        full_slot(g + 2 * f, G_FFN[l] + 2 * f, B[2 * (f % 2)][:, 0:T])
                        full_slot(g + 2 * f + 1, G_FFN[l] + 2 * f + 1, B[2 * (f % 2) + 1][:, 0:T])
                    for m_ in range(KT):
                        pe.wait_ge(S("dn_free"), e * KT + m_ + 5)
                        for f in range(FT):
                            if m_ == 0:
                                pe.wait_ge(S("hid_split"), e * FT + f + 1)
                            j = m_ * FT + f
                            s = 2 * FT + j // KT
                            if j % KT == 0:
                                pe.wait_ge(S("slot_split"), g + s + 1)
                            m = three(B[4 + m_ % 4][:, 0:T], j % KT, G_FFN[l] + s, hidh[:, f, :], hidl[:, f, :],
                                      f == 0, f == FT - 1)
                            if j % KT == KT - 1:
                                m.then_inc(S("slot_used"), 1)
                            elif f == FT - 1:
                                m.then_inc(S("dn"), 1)
                expert_loop(pe, l, body)
            norm(2 * DEPTH)

        @block.scalar
        def _(act):
            af = act.activation

            def hi(g, ring, rounds):
                act.wait_ge(S(f"slot_in{ring % RAW}"), 16 * rounds)
                if not isinstance(g, int) or g >= HI:
                    act.wait_ge(S("slot_used"), g - HI + 1)
                af(whi[:, ring % HI, :], wraw[:, ring % RAW, :], ACT.Copy).then_inc(S("slot_hi"), 1)

            def hi_ahead(g):
                hi(g + HI, g + HI, (g + HI) // RAW + 1)

            def norm(i):
                for k in range(KT):
                    l = i // 2
                    if i == 0:
                        act.wait_ge(S("x_in"), 16)
                    elif i % 2:
                        act.wait_ge(S("out_read"), KT * l + k + 1)
                    elif i < 2 * DEPTH:
                        act.wait_ge(S("dn_free"), KT + KT * (N_E[0] - 1) + k + 1)
                    else:
                        act.wait_ge(S("yt_free"), KT + KT * (NEXP - 1) + k + 1)
                    if KT * i + k >= 2:
                        act.wait_ge(S("sq_used"), KT * i + k - 1)
                    af(sqb[:, k % 2, :], x[:, k, :], ACT.Square).then_inc(S("sq_ready"), 1)
                act.wait_ge(S("sq_used"), KT * (i + 1))
                af(rstd[:, :], B[0][:, 0:T], ACT.Sqrt, scale=1.0 / D, bias=C("eps", 0, 1)).then_inc(S("nrm_sd"), 1)
                if i == 2 * DEPTH:
                    return
                for k in range(KT):
                    act.wait_ge(S("h_k"), KT * i + k + 1)
                    af(hh[:, k, :], htmp[:, k % 2, :], ACT.Copy).then_inc(S("hh_k"), 1)

            def evac_in(l, j):
                act.wait_ge(S("slot_used"), G_IN[l] + j + 1)
                src = B[6 + j % 2]
                smp = src[:, SEQ:T].rearrange("p (s k) -> p s k", k=STEP)
                if j < A_TILES:
                    af(cR[:, j, 1:EA], src[:, 0:SEQ], ACT.Copy)
                    m = af(cR[:, j, EA:WA_].rearrange("p (s k) -> p s k", k=STEP + 1)[:, :, 1:], smp, ACT.Copy)
                elif j < A_TILES + B_TILES:
                    m = af(cB[:, j - A_TILES, :], src[:, 0:T], ACT.Copy)
                elif j < A_TILES + B_TILES + TC:
                    m = af(cZ[:, j - A_TILES - B_TILES, :], src[:, 0:T], ACT.Copy)
                elif j < WIN - 1:
                    t = j - A_TILES - B_TILES - TC
                    af(cX[:, t, 3:EX], src[:, 0:SEQ], ACT.Copy)
                    m = af(cX[:, t, EX:WX_].rearrange("p (s k) -> p s k", k=STEP + 3)[:, :, 3:], smp, ACT.Copy)
                else:
                    m = af(cD[0:HC, :], src[0:HC, 0:T], ACT.Copy)
                m.then_inc(S("in_read"), 1)

            def rwkv(l, b):
                it, (c0, n) = 3 * l + b + 1, BLOCKS[b]
                nch, cb = chunks(b), 5 * l + 2 * b
                act.wait_ge(S("rw_xm"), it)
                af(tw[0:64, 0:n], Dx[0:64, 9, 0:n], ACT.Tanh)
                af(gs[:, 0:n], Dx[:, 10, 0:n], ACT.Sigmoid).then_inc(S("rw_lora"), 1)
                for q, dst, bias in ((0, "sg", "w0"), (1, "aa", "a0")):
                    act.wait_ge(S("rw_up"), 3 * it - 2 + q)
                    for t in range(TA):
                        m = af(U[dst][:, t, 0:n], B[q][:, t * P:t * P + n], ACT.Sigmoid, bias=V(bias, t))
                    m.then_inc(S("rw_sig"), 1)
                act.wait_ge(S("rw_up"), 3 * it)
                af(U["g"][:, :, 0:n], bank(2, 3, n), ACT.Copy).then_inc(S("rw_sig"), 1)
                act.wait_ge(S("rw_kr"), it)
                af(U["sq"][:, :, 0:n], U["kr"][:, :, 0:n], ACT.Square).then_inc(S("rw_sq"), 1)
                act.wait_ge(S("rw_scan"), it)
                af(U["P"][:, :, 0:n], U["L"][:, :, 0:n], ACT.Exp, scale=-SQE)
                af(U["Pi"][:, :, 0:n], U["L"][:, :, 0:n], ACT.Exp, scale=SQE)
                act.wait_ge(S("rw_lm"), it)
                af(U["Pm"][:, :, 0:n], U["Lm"][:, :, 0:n], ACT.Exp, scale=-SQE).then_inc(S("rw_exp"), 1)
                act.wait_ge(S("rw_ssm"), it)
                af(U["be"][:, :, 0:n], U["be"][:, :, 0:n], ACT.Sqrt).then_inc(S("rw_sd"), 1)
                for q, bk in enumerate((5, 0, 1)):
                    act.wait_ge(S("rw_tr"), 3 * it - 2 + q)
                    af(tok[0:n, q, :, :], bank(bk, 3, P, slice(0, n)), ACT.Copy).then_inc(S("rw_tok"), 1)
                for c in range(nch):
                    r = slice(64 * c, 64 * c + 64)
                    if b == 2:
                        act.wait_ge(S("rw_S0"), l + 1)
                        af(Rs0[:, :, :], b64(0, TA), ACT.Copy).then_inc(S("rw_S0c"), 1)
                    act.wait_ge(S("rw_SA"), cb + c + 1)
                    af(SA[r, :, :], b64(4, HA, r), ACT.Copy).then_inc(S("rw_SAc"), 1)
                act.wait_ge(S("rw_y"), cb + nch)
                af(U["kr"][:, :, 0:n], bank(5, 3, n), ACT.Copy).then_inc(S("rw_y5" if b == 2 else "rw_yc"), 1)
                act.wait_ge(S("rw_yd"), it)
                af(U["sq"][:, :, 0:n], U["kp"][:, :, 0:n], ACT.Square).then_inc(S("rw_ysq"), 1)
                act.wait_ge(S("rw_var"), it)
                af(U["be"][:, :, 0:n], bank(4, 3, n), ACT.Sqrt, scale=1.0 / HD, bias=C("eps", 1, 1)).then_inc(S("rw_ysd"), 1)
                act.wait_ge(S("rw_yf"), it)
                af(hh[:, 0:TA, c0:c0 + n], U["kp"][:, :, 0:n], ACT.Copy).then_inc(S("rw_yh"), 1)

            def retention(l, b):
                it, (c0, n) = 3 * l + b + 1, BLOCKS[b]
                act.wait_ge(S("rt_tr"), it)
                af(vkt[0:n, :, :], bank(2, 4, P, slice(0, n)), ACT.Copy).then_inc(S("rt_tok"), 1)
                act.wait_ge(S("rt_o"), it)
                af(ro[:, :, 0:n], bank(3, 2, n), ACT.Copy).then_inc(S("rt_oc"), 1)
                if b == 2:
                    act.wait_ge(S("rt_o2"), l + 1)
                else:
                    act.wait_ge(S("rt_oc"), it)
                af(rsq[:, :, 0:n], ro[:, :, 0:n], ACT.Square).then_inc(S("rt_sq"), 1)
                af(rsg[:, :, 0:n], cB[:, 6:8, c0:c0 + n], ACT.Silu).then_inc(S("rt_sg"), 1)
                act.wait_ge(S("rt_ms"), it)
                af(rsq[:, :, 0:n], bank(0, 2, n), ACT.Sqrt, scale=1.0 / HD, bias=C("eps", 0, 1)).then_inc(S("rt_sd"), 1)
                act.wait_ge(S("rt_y"), it)
                af(hh[:, TA:TA + TB, c0:c0 + n], ro[:, :, 0:n], ACT.Copy).then_inc(S("rt_yh"), 1)

            def mamba_dt(l):
                r = slice(0, HC)
                act.wait_ge(S("mix_done"), 9 * l + 6)
                act.wait_ge(S("st_out"), 16 * (8 * l + 6))
                af(an[r, :], V("a_log", rows=r), ACT.Exp)
                af(dd["x"][r, :], cD[r, :], ACT.Identity, bias=V("dt_bias", rows=r))
                af(dd["e"][r, :], cD[r, :], ACT.Abs, bias=V("dt_bias", rows=r)).then_inc(S("mb_abs"), 1)
                act.wait_ge(S("mb_abs"), l + 1)
                af(dd["e"][r, :], dd["e"][r, :], ACT.Exp, scale=-1.0).then_inc(S("mb_e"), 1)
                act.wait_ge(S("mb_lm"), l + 1)
                af(dd["wk"][r, :], dd["lm"][r, :], ACT.Exp).then_inc(S("mb_e"), 1)

            def mamba(l, b):
                it, (c0, n) = 3 * l + b + 1, BLOCKS[b]
                act.wait_ge(S("mb_cv"), 4 * it)
                af(xc[:, :, 0:n], xcs[:, :, 0:n], ACT.Silu).then_inc(S("mb_xc"), 1)
                af(zs[:, :, 0:n], cZ[:, :, c0:c0 + n], ACT.Silu).then_inc(S("mb_zs"), 1)
                act.wait_ge(S("mb_t3"), it)
                af(tk3[0:n, :, :], B[5][0:n, 0:3 * HC].rearrange("p (a c) -> p a c", c=HC), ACT.Copy).then_inc(S("mb_tk3"), 1)
                act.wait_ge(S("mb_cb"), it)
                af(ecb[:, 0:3, 0:n], bank(0, 3, n), ACT.Exp)
                af(ecb[:, 3:6, 0:n], bank(1, 3, n), ACT.Exp).then_inc(S("mb_ecb"), 1)
                act.wait_ge(S("mb_seg"), it)
                af(seg[0:n, :, 0:n], seg[0:n, :, 0:n], ACT.Exp).then_inc(S("mb_E"), 1)
                act.wait_ge(S("mb_tB"), it)
                af(Btk[0:n, :, :], bank(3, 2, P, slice(0, n)), ACT.Copy).then_inc(S("mb_Btk"), 1)
                act.wait_ge(S("mb_y2"), it)
                af(ysq[:, :, 0:n], yz[:, :, 0:n], ACT.Square).then_inc(S("mb_sq"), 1)
                act.wait_ge(S("mb_ms"), it)
                af(zs[:, 0, 0:n], B[4][:, 0:n], ACT.Sqrt, scale=1.0 / (HC * HD), bias=C("eps", 2, 1)).then_inc(S("mb_sd"), 1)
                act.wait_ge(S("mb_y3"), it)
                af(hh[:, TA + TB:KT, c0:c0 + n], yz[:, :, 0:n], ACT.Copy).then_inc(S("mb_yh"), 1)

            act.dma_start(cst[:, :], consts_in).then_inc(S("const_in"), 16)
            act.wait_ge(S("const_in"), 16)
            for g in range(HI):
                hi(g, g, 1)
            for l in range(DEPTH):
                act.wait_ge(S("par_in"), 16 * (l + 1))
                norm(2 * l)
                for j in range(WIN):
                    hi_ahead(G_IN[l] + j)
                    evac_in(l, j)
                for b in range(3):
                    rwkv(l, b)
                for b in range(3):
                    retention(l, b)
                mamba_dt(l)
                for b in range(3):
                    mamba(l, b)
                for j in range(KT):
                    hi_ahead(G_OUT[l] + j)
                norm(2 * l + 1)
                if l == DEPTH - 1:
                    hi_ahead(G_FFN[l] - 1)
                    act.wait_ge(S("slot_used"), G_FFN[l])
                    act.wait_ge(S("st_out"), 16 * 8 * (l + 1))
                    af(lg[:, :], B[6][0:NEXP, 0:T], ACT.Copy).then_inc(S("lg"), 1)
                    act.wait_ge(S("rt_lm"), 1)
                    af(rt["e"][:, :, :], rt["l"][:, :, :], ACT.Exp).then_inc(S("rt_ex"), 1)
                    act.wait_ge(S("lgT"), 2)
                    af(lg[:, :], B[5][0:NEXP, 0:T], ACT.Copy).then_inc(S("lg"), 1)
                    for e in range(NEXP):
                        act.wait_ge(S("gb"), e + 1)
                        af(gbc[:, e, :], B[e % 2][:, 0:T], ACT.Copy).then_inc(S("gbc"), 1)
                else:
                    act.wait_ge(S("st_out"), 16 * 8 * (l + 1))

                def body(i, g, e):
                    def hidden_hi(f):
                        act.wait_ge(S("gu_free"), e * FT + f + 3)
                        af(hidh[:, f, :], hid[:, f % 2, :], ACT.Copy).then_inc(S("hid_hi"), 1)

                    for j in range(EXP_SLOTS):
                        r = G_FFN[l] + j + HI
                        hi(g + j + HI, r, i * (EXP_SLOTS // RAW) + r // RAW + 1)
                        f = j // 2
                        if j < 2 * FT and j % 2:
                            act.wait_ge(S("slot_used"), g + 2 * f + 1)
                            af(sil[:, f % 2, :], B[2 * (f % 2)][:, 0:T], ACT.Silu).then_inc(S("sil"), 1)
                        elif 0 < j <= 2 * FT:
                            hidden_hi(f - 1)
                expert_loop(act, l, body)
            norm(2 * DEPTH)

        @block.vector
        def _(v):
            tt, ts, stt, cp = v.tensor_tensor, v.tensor_scalar, v.scalar_tensor_tensor, v.tensor_copy
            own = [0]

            def own_count():
                own[0] += 1
                return own[0]

            def lo(g, ring):
                v.wait_ge(S("slot_hi"), g + 1)
                tt(wlo[:, ring % RAW, :], wraw[:, ring % RAW, :], whi[:, ring % HI, :].bitcast(F32),
                   ALU.subtract).then_inc(S("slot_split"), 1)

            def norm(i):
                v.wait_ge(S("nrm_sd"), i + 1)
                v.reciprocal(rstd[:, :], rstd[:, :]).then_inc(S("v_step"), 1)
                v.wait_ge(S("v_step"), own_count())
                if i == 2 * DEPTH:
                    for k in range(KT):
                        m = stt(x[:, k, :], x[:, k, :], V("g_fin", k), rstd[:, :], ALU.mult, ALU.mult)
                    m.then_inc(S("y_done"), 1)
                    return
                gain = "g_ffn" if i % 2 else "g_mix"

                def scaled(k):
                    stt(htmp[:, k % 2, :], x[:, k, :], V(gain, k), rstd[:, :], ALU.mult, ALU.mult).then_inc(S("h_k"), 1)
                scaled(0)
                scaled(1)
                for k in range(KT):
                    v.wait_ge(S("hh_k"), KT * i + k + 1)
                    tt(hl[:, k, :], htmp[:, k % 2, :], hh[:, k, :].bitcast(F32), ALU.subtract).then_inc(S("h_split"), 1)
                    if k + 2 < KT:
                        if k >= 0:
                            v.wait_ge(S("h_split"), KT * i + k + 1)
                        scaled(k + 2)

            def rwkv(l, b):
                it, (c0, n) = 3 * l + b + 1, BLOCKS[b]
                nch, cb, lv = chunks(b), 5 * l + 2 * b, 15 * l + 6 * b
                nn = nch * CH
                u = {k: t[:, :, 0:n] for k, t in U.items()}
                rr = slice(0, nn)
                if b == 0:
                    v.wait_ge(S("in_read"), WIN * (l + 1))
                    v.wait_ge(S("ext_ready"), l + 1)
                if b < 2:
                    now, prev = cR[:, :, c0 + 1:c0 + 1 + n], cR[:, :, c0:c0 + n]
                    d3 = Dx[:, :, 0:n]
                else:
                    e3 = cR[:, :, EA:WA_].rearrange("p t (s k) -> p t s k", k=STEP + 1)
                    now, prev = e3[:, :, :, 1:], e3[:, :, :, 0:STEP]
                    d3 = Dx[:, :, 0:n].rearrange("p t (s k) -> p t s k", k=STEP)
                tt(d3, prev, now, ALU.subtract).then_inc(S("v_step"), 1)
                v.wait_ge(S("v_step"), own_count())
                for t in range(A_TILES):
                    m = stt(d3[:, t], d3[:, t], V("mu", t), now[:, t], ALU.mult, ALU.add)
                m.then_inc(S("rw_xm"), 1)
                v.wait_ge(S("rw_xm"), it)
                r_, k_, v_ = Dx[:, 0:3, 0:n], Dx[:, 3:6, 0:n], Dx[:, 6:9, 0:n]
                tt(u["kr"], k_, over(V("k_k", 0, 3), n), ALU.mult).then_inc(S("rw_kr"), 1)
                v.wait_ge(S("rw_sig"), 3 * it - 2)
                for t in range(TA):
                    m = v.tensor_tensor_scan(U["L"][:, t, 0:n], C("scan8" if b == 2 else "scan64", 0, n),
                                             U["sg"][:, t, 0:n], 0.0, ALU.mult, ALU.add)
                m.then_inc(S("rw_scan"), 1)
                v.wait_ge(S("rw_scan"), it)
                tt(u["Lm"], u["L"], u["sg"], ALU.subtract).then_inc(S("rw_lm"), 1)
                v.wait_ge(S("rw_sig"), 3 * it - 1)
                stt(u["t1"], u["aa"], -1.0, over(V("k_a", 0, 3), n), ALU.add, ALU.mult).then_inc(S("v_step"), 1)
                v.wait_ge(S("v_step"), own_count())
                stt(u["kp"], u["t1"], 1.0, k_, ALU.add, ALU.mult).then_inc(S("rw_kp"), 1)
                v.wait_ge(S("rw_ss"), it)
                ts(u["be"], bank(3, 3, n), 1e-24, None, ALU.max).then_inc(S("rw_ssm"), 1)
                v.wait_ge(S("rw_sd"), it)
                v.reciprocal(u["be"], u["be"]).then_inc(S("v_step"), 1)
                v.wait_ge(S("v_step"), own_count())
                tt(u["kk"], u["kr"], u["be"], ALU.mult).then_inc(S("v_step"), 1)
                v.wait_ge(S("v_step"), own_count())
                v.wait_ge(S("rw_exp"), it)
                stt(u["al"], u["Pm"], -1.0, u["kk"], ALU.mult, ALU.mult)
                tt(u["be"], u["kk"], u["aa"], ALU.mult).then_inc(S("v_step"), 1)
                v.wait_ge(S("v_step"), own_count())
                tt(u["be"], u["be"], u["Pi"], ALU.mult)
                v.wait_ge(S("rw_kp"), it)
                tt(u["ka"], u["kp"], u["Pi"], ALU.mult)
                tt(u["rho"], u["P"], r_, ALU.mult).then_inc(S("rw_ops"), 1)
                v.wait_ge(S("rw_bsum"), it)
                tt(u["bonus"], bank(4, 3, n), v_, ALU.mult).then_inc(S("rw_bonus"), 1)
                cp(TM[rr, :, :], rep(C("i64", rows=rr), HA))
                cp(TT[rr, :, :], rep(C("i64", rows=rr), HA)).then_inc(S("rw_T"), 1)
                sfx = "8" if b == 2 else ""
                for q, (dst, mask) in enumerate(((AB, "strict"), (C12, "incl"))):
                    for o in range(2):
                        v.wait_ge(S("rw_sc"), 4 * it - 3 + 2 * q + o)
                        m = tt(dst[rr, o, :, :, :].rearrange("p z t c -> p (z t) c"), b64(2 + 2 * q + o, 2 * TA, rr),
                               rep(C(mask + sfx, rows=rr), 2 * TA), ALU.mult)
                    m.then_inc(S(("rw_AT", "rw_C")[q]), 1)
                for q in range(levels(b)):
                    v.wait_ge(S("rw_W"), lv + q + 1)
                    cp(Wm[rr, :, :], b64(0, HA, rr)).then_inc(S("rw_Wc"), 1)
                    v.wait_ge(S("rw_TW"), lv + q + 1)
                    v.wait_ge(S("rw_T"), lv + q + it)
                    for bk, mt, odd in ((1, TM, 0), (2, TT, 1)):
                        got = B[bk][rr, 0:HA * 32].rearrange("p (x s) -> p x s", s=1 << q)
                        part = mt[rr, :, :].rearrange("p h (a o s) -> p (h a) o s", o=2, s=1 << q)[:, :, odd, :]
                        m = tt(part, part, got, ALU.add)
                    m.then_inc(S("rw_T"), 1)
                for c in range(nch):
                    r = slice(64 * c, 64 * c + 64)
                    if b < 2 and c == 0:
                        if b == 0:
                            v.memset(Sbd[:, :, :], 0.0).then_inc(S("rw_Sbd"), 1)
                    v.wait_ge(S("rw_R"), cb + c + 1)
                    cp(Rs[r, :, :], b64(3, HA, r)).then_inc(S("rw_Rc"), 1)
                    if b < 2:
                        v.wait_ge(S("rw_dS"), 4 * l + 2 * b + c + 1)
                        v.wait_ge(S("zeroed"), l + 1)
                        v.wait_ge(S("rw_Sbd"), 5 * l + 2 * b + c + 1)
                        v.wait_ge(S("rw_y"), cb + c + 1)
                        tt(srw_p[:, :, :], srw_p[:, :, :], b64(0, TA), ALU.add).then_inc(S("v_step"), 1)
                        v.wait_ge(S("v_step"), own_count())
                        last = U["P"][:, :, c * CH + CH - 1:c * CH + CH]
                        tt(srw_p[:, :, :], srw_p[:, :, :], last.to_broadcast([P, TA, HD]), ALU.mult).then_inc(S("v_step"), 1)
                        v.wait_ge(S("v_step"), own_count())
                        for o in range(2):
                            p = slice(64 * o, 64 * o + 64)
                            m = cp(Sbd[p, :, 64 * o:64 * o + 64], srw_p[p, :, :])
                        m.then_inc(S("rw_Sbd"), 1)
                if b == 2:
                    v.wait_ge(S("rw_SAc"), cb + 1)
                    for t in range(TA):
                        if t >= 1:
                            v.wait_ge(S("rw_ds"), 3 * l + t)
                        tt(rwx[:, 0, :, :], rep(SA[0:CH, 2 * t:2 * t + 2, :].rearrange("p h c -> p (h c)"), NSEQ),
                           over(C("seq", rows=slice(0, CH)), P), ALU.mult).then_inc(S("rw_xs"), 1)
                    for t in range(TA):
                        v.wait_ge(S("rw_ds"), 3 * l + t + 1)
                        st = srw[:, t, :, :]
                        m = tt(st, st, B[1 + t][:, :].rearrange("p (s c) -> p s c", c=HD), ALU.add)
                        if t == TA - 1:
                            m.then_inc(S("rw_sSa"), 1)
                            v.wait_ge(S("rw_sSa"), l + 1)
                        else:
                            m.then_inc(S("v_step"), 1)
                            v.wait_ge(S("v_step"), own_count())
                        last = U["P"][:, t, STEP - 1:NSEQ * STEP:STEP]
                        tt(st, st, over(last, HD), ALU.mult).then_inc(S("rw_sS"), 1)
                    v.wait_ge(S("rw_y5"), l + 1)
                    tt(u["kr"], u["kr"], bank(0, 3, n), ALU.add).then_inc(S("rw_yc"), 1)
                    v.wait_ge(S("rw_yc"), it)
                v.wait_ge(S("rw_mean"), it)
                stt(u["kp"], bank(3, 3, n), -1.0 / HD, u["kr"], ALU.mult, ALU.add).then_inc(S("rw_yd"), 1)
                v.wait_ge(S("rw_ysd"), it)
                v.reciprocal(u["be"], u["be"]).then_inc(S("v_step"), 1)
                v.wait_ge(S("v_step"), own_count())
                tt(u["kp"], u["kp"], u["be"], ALU.mult).then_inc(S("v_step"), 1)
                v.wait_ge(S("v_step"), own_count())
                for t in range(TA):
                    m = ts(U["kp"][:, t, 0:n], U["kp"][:, t, 0:n], V("ln_w", t), V("ln_b", t), ALU.mult, ALU.add)
                m.then_inc(S("v_step"), 1)
                v.wait_ge(S("v_step"), own_count())
                v.wait_ge(S("rw_bonus"), it)
                tt(u["kp"], u["kp"], u["bonus"], ALU.add).then_inc(S("v_step"), 1)
                v.wait_ge(S("v_step"), own_count())
                v.wait_ge(S("rw_sig"), 3 * it)
                tt(u["kp"], u["kp"], u["g"], ALU.mult).then_inc(S("rw_yf"), 1)
                v.wait_ge(S("rw_yh"), it)
                tt(hl[:, 0:TA, c0:c0 + n], u["kp"], hh[:, 0:TA, c0:c0 + n].bitcast(F32), ALU.subtract)\
                    .then_inc(S("mix_done"), 1)

            def retention(l, b):
                it, (c0, n) = 3 * l + b + 1, BLOCKS[b]
                q_ = qk[:, :, 0:n]
                if b == 0:
                    v.wait_ge(S("st_out"), 16 * (8 * l + 4))
                v.wait_ge(S("rt_sw"), it)
                tt(q_, bank(0, 4, n), rep(C("sin", c0, n), 4), ALU.mult).then_inc(S("v_step"), 1)
                v.wait_ge(S("v_step"), own_count())
                v.wait_ge(S("rt_q2"), it)
                tt(q_, q_, qk2[:, :, 0:n], ALU.add).then_inc(S("v_step"), 1)
                v.wait_ge(S("v_step"), own_count())
                ts(qk[:, 2:4, 0:n], qk[:, 2:4, 0:n], HD ** -0.5, None, ALU.mult).then_inc(S("rt_qk"), 1)
                v.wait_ge(S("rt_qk"), it)
                for q, nm in enumerate(("qdec", "kdec")):
                    dec = C(nm).rearrange("p (t c) -> p t c", c=T)[:, :, c0:c0 + n]
                    m = tt(qkd[:, 2 * q:2 * q + 2, 0:n], qk[:, 2 * q:2 * q + 2, 0:n], dec, ALU.mult)
                m.then_inc(S("rt_dec"), 1)
                v.wait_ge(S("rt_sc"), it)
                mask = C("rmask8" if b == 2 else "rmask", rows=slice(0, n)).rearrange("p (h c) -> p h c", h=HB)
                for o in range(2):
                    hs = slice(o * TB, (o + 1) * TB)
                    m = tt(rsc[0:n, hs, 0:n], bank((1, 5)[o], TB, n, slice(0, n)), mask[:, hs, :], ALU.mult)
                m.then_inc(S("rt_scm"), 1)
                v.wait_ge(S("rt_dS"), it)
                if b < 2:
                    v.wait_ge(S("zeroed"), l + 1)
                    if b > 0:
                        v.wait_ge(S("rt_S"), 2 * l + b)
                for t in range(TB):
                    if b < 2:
                        m = stt(srt_p[:, t, :], srt_p[:, t, :], C("cdec", t, 1), B[4][:, t * HD:(t + 1) * HD],
                                ALU.mult, ALU.add)
                    else:
                        st = srt[:, t, :, :].rearrange("p s c -> p (s c)")
                        m = stt(st, st, C("cdec", TB + t, 1), B[(4, 1)[t]][:, :], ALU.mult, ALU.add)
                m.then_inc(S("rt_S" if b < 2 else "rt_sS"), 1)
                if b == 2:
                    v.wait_ge(S("rt_oc"), it)
                    tt(ro[:, :, 0:n], ro[:, :, 0:n], bank(5, TB, n), ALU.add).then_inc(S("rt_o2"), 1)
                    v.wait_ge(S("rt_o2"), l + 1)
                v.wait_ge(S("rt_sd"), it)
                v.reciprocal(rsq[:, :, 0:n], rsq[:, :, 0:n]).then_inc(S("v_step"), 1)
                v.wait_ge(S("v_step"), own_count())
                v.wait_ge(S("rt_oc"), it)
                for t in range(TB):
                    m = stt(ro[:, t, 0:n], ro[:, t, 0:n], V("ret_norm", t), rsq[:, t, 0:n], ALU.mult, ALU.mult)
                m.then_inc(S("v_step"), 1)
                v.wait_ge(S("v_step"), own_count())
                v.wait_ge(S("rt_sg"), it)
                tt(ro[:, :, 0:n], ro[:, :, 0:n], rsg[:, :, 0:n], ALU.mult).then_inc(S("rt_y"), 1)
                v.wait_ge(S("rt_yh"), it)
                tt(hl[:, TA:TA + TB, c0:c0 + n], ro[:, :, 0:n], hh[:, TA:TA + TB, c0:c0 + n].bitcast(F32),
                   ALU.subtract).then_inc(S("mix_done"), 1)

            def mamba_dt(l):
                r = slice(0, HC)
                d = {k: t[r, :] for k, t in dd.items()}
                coef = [1.0 / k for k in (13, 11, 9, 7, 5, 3)]
                v.wait_ge(S("mb_e"), 2 * l + 1)
                ts(d["z"], d["e"], 2.0, None, ALU.add).then_inc(S("v_step"), 1)
                v.wait_ge(S("v_step"), own_count())
                v.reciprocal(d["z"], d["z"]).then_inc(S("v_step"), 1)
                v.wait_ge(S("v_step"), own_count())
                tt(d["z"], d["z"], d["e"], ALU.mult).then_inc(S("v_step"), 1)
                v.wait_ge(S("v_step"), own_count())
                tt(d["z2"], d["z"], d["z"], ALU.mult).then_inc(S("v_step"), 1)
                v.wait_ge(S("v_step"), own_count())
                ts(d["p"], d["z2"], 1.0 / 15, None, ALU.mult).then_inc(S("v_step"), 1)
                v.wait_ge(S("v_step"), own_count())
                for c in coef:
                    stt(d["p"], d["p"], c, d["z2"], ALU.add, ALU.mult).then_inc(S("v_step"), 1)
                    v.wait_ge(S("v_step"), own_count())
                stt(d["p"], d["p"], 1.0, d["z"], ALU.add, ALU.mult).then_inc(S("v_step"), 1)
                v.wait_ge(S("v_step"), own_count())
                ts(d["x"], d["x"], 0.0, None, ALU.max).then_inc(S("v_step"), 1)
                v.wait_ge(S("v_step"), own_count())
                stt(d["dt"], d["p"], 2.0, d["x"], ALU.mult, ALU.add).then_inc(S("v_step"), 1)
                v.wait_ge(S("v_step"), own_count())
                ts(d["dA"], d["dt"], an[r, :], -1.0, ALU.mult, ALU.mult).then_inc(S("v_step"), 1)
                v.wait_ge(S("v_step"), own_count())
                v.tensor_tensor_scan(d["cum"], C("scanm", rows=r), d["dA"], 0.0, ALU.mult, ALU.add).then_inc(S("v_step"), 1)
                v.wait_ge(S("v_step"), own_count())
                for lo_, n_, k_ in ((0, 2, P), (SEQ, NSEQ, STEP)):
                    c3_ = d["cum"][:, lo_:lo_ + n_ * k_].rearrange("p (a k) -> p a k", k=k_)
                    o3 = d["lm"][:, lo_:lo_ + n_ * k_].rearrange("p (a k) -> p a k", k=k_)
                    m = tt(o3, c3_[:, :, k_ - 1:k_].to_broadcast([HC, n_, k_]), c3_, ALU.subtract)
                m.then_inc(S("mb_lm"), 1)
                v.wait_ge(S("mb_e"), 2 * l + 2)
                tt(d["wk"], d["wk"], d["dt"], ALU.mult).then_inc(S("mb_dt"), 1)

            def mamba(l, b):
                it, (c0, n) = 3 * l + b + 1, BLOCKS[b]
                rn = slice(0, n)
                for j in range(CONV):
                    if j:
                        v.wait_ge(S("mb_cv"), 4 * it - 4 + j)
                    for t in range(XT):
                        if b < 2:
                            src, dst = cX[:, t, c0 + j:c0 + j + n], xcs[:, t, 0:n]
                        else:
                            src = cX[:, t, EX:WX_].rearrange("p (s k) -> p s k", k=STEP + 3)[:, :, j:j + STEP]
                            dst = xcs[:, t, 0:n].rearrange("p (s k) -> p s k", k=STEP)
                        if j == 0:
                            m = ts(dst, src, V("conv_w", t), V("conv_b", t), ALU.mult, ALU.add)
                        else:
                            m = stt(dst, src, V("conv_w", j * XT + t), dst, ALU.mult, ALU.add)
                    m.then_inc(S("mb_cv"), 1)
                v.wait_ge(S("mb_ecb"), it)
                v.wait_ge(S("mb_tk3"), it)
                for h in range(HC):
                    m = ts(seg[rn, h, 0:n], B[h // 3][rn, (h % 3) * P:(h % 3) * P + n], tk3[rn, 1, h:h + 1], 0.0,
                           ALU.subtract, ALU.min)
                m.then_inc(S("mb_seg"), 1)
                v.wait_ge(S("mb_tB"), it)
                xt_ = B[2][rn, 0:HC * HD].rearrange("p (h c) -> p h c", c=HD)
                tt(xdt[rn, :, :], xt_, over(tk3[rn, 0, :], HD), ALU.mult)
                tt(xw[rn, :, :], xt_, over(tk3[rn, 2, :], HD), ALU.mult).then_inc(S("mb_xdt"), 1)
                v.wait_ge(S("mb_BC"), it)
                tt(cbm[rn, :, 0:n], bank(4, 2, n, rn), rep(C("causal8" if b == 2 else "causal", rows=rn), 2),
                   ALU.mult).then_inc(S("v_step"), 1)
                v.wait_ge(S("v_step"), own_count())
                v.wait_ge(S("mb_E"), it)
                for g in range(2):
                    m = tt(wts[rn, 3 * g:3 * g + 3, 0:n], seg[rn, 3 * g:3 * g + 3, 0:n], rep(cbm[rn, g, 0:n], 3), ALU.mult)
                m.then_inc(S("mb_wts"), 1)
                v.wait_ge(S("mb_y"), it)
                v.wait_ge(S("mb_xc"), it)
                for t in range(TC):
                    m = stt(yz[:, t, 0:n], xc[:, t, 0:n], V("d", t), B[5][:, t * P:t * P + n], ALU.mult, ALU.add)
                m.then_inc(S("v_step"), 1)
                v.wait_ge(S("v_step"), own_count())
                v.wait_ge(S("mb_zs"), it)
                tt(yz[:, :, 0:n], yz[:, :, 0:n], zs[:, :, 0:n], ALU.mult).then_inc(S("mb_y2"), 1)
                v.wait_ge(S("mb_ecb"), it)
                if b < 2:
                    v.wait_ge(S("zeroed"), l + 1)
                    if b > 0:
                        v.wait_ge(S("mb_S"), 2 * l + b)
                    st = smb_p[:, :].rearrange("p (h c) -> p h c", c=HD)
                    tt(st, st, ecb[:, :, n - 1:n].to_broadcast([P, HC, HD]), ALU.mult).then_inc(S("v_step"), 1)
                    v.wait_ge(S("v_step"), own_count())
                    v.wait_ge(S("mb_dS"), 2 * l + b + 1)
                    tt(smb_p[:, :], smb_p[:, :], B[0][:, 0:HC * HD], ALU.add).then_inc(S("mb_S"), 1)
                else:
                    for g in range(2):
                        for h in range(3):
                            last = ecb[:, 3 * g + h, STEP - 1:NSEQ * STEP:STEP]
                            st = smb[:, g, :, h, :]
                            m = tt(st, st, over(last, HD), ALU.mult)
                    m.then_inc(S("v_step"), 1)
                    v.wait_ge(S("v_step"), own_count())
                    for g in range(2):
                        v.wait_ge(S("mb_ds"), 2 * l + g + 1)
                        flat = smb[:, g, :, :, :].rearrange("p s h c -> p (s h c)")
                        for q in range(3):
                            f = flat[:, q * 512:(q + 1) * 512]
                            m = tt(f, f, B[q][:, :], ALU.add)
                        m.then_inc(S("mb_ds_used"), 1)
                v.wait_ge(S("mb_sd"), it)
                v.reciprocal(zs[:, 0, 0:n], zs[:, 0, 0:n]).then_inc(S("v_step"), 1)
                v.wait_ge(S("v_step"), own_count())
                v.wait_ge(S("mb_y2"), it)
                for t in range(TC):
                    m = stt(yz[:, t, 0:n], yz[:, t, 0:n], V("ssm_norm", t), zs[:, 0, 0:n], ALU.mult, ALU.mult)
                m.then_inc(S("mb_y3"), 1)
                v.wait_ge(S("mb_yh"), it)
                tt(hl[:, TA + TB:KT, c0:c0 + n], yz[:, :, 0:n], hh[:, TA + TB:KT, c0:c0 + n].bitcast(F32),
                   ALU.subtract).then_inc(S("mix_done"), 1)

            def router():
                v.memset(rt["l"][:, :, :], 0.0).then_inc(S("v_step"), 1)
                v.wait_ge(S("v_step"), own_count())
                v.wait_ge(S("lgT"), 1)
                for q, (c0, n) in enumerate(BLOCKS):
                    m = cp(rt["l"][0:n, q, :], B[7][0:n, q * NEXP:(q + 1) * NEXP])
                m.then_inc(S("v_step"), 1)
                v.wait_ge(S("v_step"), own_count())
                l_, e_, p_, rk, g_ = (rt[k][:, :, :] for k in ("l", "e", "p", "rank", "g"))
                v.tensor_reduce(rt1[:, :, 0], l_, AX.X, ALU.max).then_inc(S("v_step"), 1)
                v.wait_ge(S("v_step"), own_count())
                tt(l_, l_, over(rt1[:, :, 0], NEXP), ALU.subtract).then_inc(S("rt_lm"), 1)
                v.wait_ge(S("rt_ex"), 1)
                v.tensor_reduce(rt1[:, :, 1], e_, AX.X, ALU.add).then_inc(S("v_step"), 1)
                v.wait_ge(S("v_step"), own_count())
                v.reciprocal(rt1[:, :, 1], rt1[:, :, 1]).then_inc(S("v_step"), 1)
                v.wait_ge(S("v_step"), own_count())
                tt(p_, e_, over(rt1[:, :, 1], NEXP), ALU.mult).then_inc(S("v_step"), 1)
                v.wait_ge(S("v_step"), own_count())
                for q in range(3):
                    of_j, of_e = rep(rt["p"][:, q, :], NEXP), over(rt["p"][:, q, :], NEXP)
                    tt(cmp[:, q, :, :], of_j, of_e, ALU.is_gt)
                    m = tt(cmq[:, q, :, :], of_j, of_e, ALU.is_equal)
                m.then_inc(S("v_step"), 1)
                v.wait_ge(S("v_step"), own_count())
                for q in range(3):
                    m = tt(cmq[:, q, :, :], cmq[:, q, :, :], C("before").rearrange("p (e j) -> p e j", j=NEXP), ALU.mult)
                m.then_inc(S("v_step"), 1)
                v.wait_ge(S("v_step"), own_count())
                tt(cmp[:, :, :, :], cmp[:, :, :, :], cmq[:, :, :, :], ALU.add).then_inc(S("v_step"), 1)
                v.wait_ge(S("v_step"), own_count())
                for q in range(3):
                    m = v.tensor_reduce(rt["rank"][:, q, :], cmp[:, q, :, :], AX.X, ALU.add)
                m.then_inc(S("v_step"), 1)
                v.wait_ge(S("v_step"), own_count())
                stt(g_, rk, 1.5, p_, ALU.is_lt, ALU.mult).then_inc(S("v_step"), 1)
                v.wait_ge(S("v_step"), own_count())
                v.tensor_reduce(rt1[:, :, 2], g_, AX.X, ALU.add).then_inc(S("v_step"), 1)
                v.wait_ge(S("v_step"), own_count())
                v.reciprocal(rt1[:, :, 2], rt1[:, :, 2]).then_inc(S("v_step"), 1)
                v.wait_ge(S("v_step"), own_count())
                tt(g_, g_, over(rt1[:, :, 2], NEXP), ALU.mult).then_inc(S("gates"), 1)

            v.sem_inc(S("gu_free"), 2)
            v.sem_inc(S("dn_free"), KT)
            v.wait_ge(S("const_in"), 16)
            for g in range(HI):
                lo(g, g)
            for l in range(DEPTH):
                v.wait_ge(S("par_in"), 16 * (l + 1))
                norm(2 * l)
                for j in range(WIN):
                    lo(G_IN[l] + j + HI, G_IN[l] + j + HI)
                for b in range(3):
                    rwkv(l, b)
                for b in range(3):
                    retention(l, b)
                mamba_dt(l)
                for b in range(3):
                    mamba(l, b)
                for j in range(KT):
                    lo(G_OUT[l] + j + HI, G_OUT[l] + j + HI)
                    v.wait_ge(S("slot_used"), G_OUT[l] + j + 1)
                    tt(x[:, j, :], x[:, j, :], B[6 + j % 2][:, 0:T], ALU.add).then_inc(S("out_read"), 1)
                norm(2 * l + 1)
                v.wait_ge(S("st_out"), 16 * 8 * (l + 1))
                if l == DEPTH - 1:
                    lo(G_FFN[l] - 1 + HI, G_FFN[l] - 1 + HI)
                    router()

                def body(i, g, e):
                    def add(m_):
                        if m_ < KT - 1:
                            v.wait_ge(S("dn"), e * (KT - 1) + m_ + 1)
                        else:
                            v.wait_ge(S("slot_used"), g + EXP_SLOTS)
                        if l == 0:
                            v.wait_ge(S("dn_free"), e * KT + m_ + 1)
                            tt(x[:, m_, :], x[:, m_, :], B[4 + m_ % 4][:, 0:T], ALU.add).then_inc(S("dn_free"), 1)
                        else:
                            v.wait_ge(S("yt_free"), i * KT + m_ + 5)
                            gate = gbc[:, bass.ds(i, 1), :].rearrange("p o t -> p (o t)")
                            tt(yt[:, m_ % 4, :], B[4 + m_ % 4][:, 0:T], gate, ALU.mult).then_inc(S("dn_free"), 1)

                    ends = {2 * FT + (FT * m_ + FT - 1) // KT: m_ for m_ in range(KT)}
                    if l == DEPTH - 1:
                        pass
                    for j in range(EXP_SLOTS):
                        lo(g + j + HI, G_FFN[l] + j + HI)
                        f = j // 2
                        if j < 2 * FT and j % 2:
                            v.wait_ge(S("slot_used"), g + j + 1)
                            v.wait_ge(S("sil"), e * FT + f + 1)
                            tt(hid[:, f % 2, :], sil[:, f % 2, :], B[2 * (f % 2) + 1][:, 0:T], ALU.mult)\
                                .then_inc(S("gu_free"), 1)
                        elif 0 < j <= 2 * FT:
                            v.wait_ge(S("hid_hi"), e * FT + f)
                            tt(hidl[:, f - 1, :], hid[:, (f - 1) % 2, :], hidh[:, f - 1, :].bitcast(F32),
                               ALU.subtract).then_inc(S("hid_split"), 1)
                        if j in ends:
                            add(ends[j])
                if l == DEPTH - 1:
                    v.wait_ge(S("gbc"), NEXP)
                expert_loop(v, l, body)
            norm(2 * DEPTH)

        @block.gpsimd
        def _(gp):
            tt = gp.tensor_tensor

            def rwkv(l, b):
                it, (c0, n) = 3 * l + b + 1, BLOCKS[b]
                lv, rr = 15 * l + 6 * b, slice(0, chunks(b) * CH)
                gp.wait_ge(S("rw_kp"), it)
                tt(U["br"][:, :, 0:n], Dx[:, 0:3, 0:n], U["kp"][:, :, 0:n], ALU.mult).then_inc(S("rw_rk"), 1)
                gp.wait_ge(S("rw_rk"), it)
                tt(U["br"][:, :, 0:n], U["br"][:, :, 0:n], over(V("r_k", 0, 3), n), ALU.mult).then_inc(S("rw_br"), 1)
                gp.wait_ge(S("rw_AT"), it)
                for q in range(levels(b)):
                    if q >= 2:
                        gp.wait_ge(S("rw_W"), lv + q - 1)
                    m = C("lev").rearrange("p (q c) -> p q c", c=CH)[rr, q, :]
                    for o in range(2):
                        i_ = tt(AL[rr, q % 2, o * TA:(o + 1) * TA, :], AB[rr, o, 0, :, :], rep(m, TA), ALU.mult)
                    i_.then_inc(S("rw_AL"), 1)
                if b == 2:
                    gp.wait_ge(S("rw_tok"), 3 * it - 2)
                    gp.wait_ge(S("rw_SAc"), 5 * (l + 1))
                    for t in range(TA):
                        if t >= 1:
                            gp.wait_ge(S("rw_ds"), 3 * l + t)
                        tt(rwx[:, 1, :, :], rep(tok[0:CH, 0, t, :], NSEQ), over(C("seq", rows=slice(0, CH)), P),
                           ALU.mult).then_inc(S("rw_xv"), 1)

            def retention(l, b):
                it, (c0, n) = 3 * l + b + 1, BLOCKS[b]
                gp.wait_ge(S("mix_done"), 9 * l + 3 + b)
                tt(qk2[:, :, 0:n], cB[:, 0:4, c0:c0 + n], rep(C("cos", c0, n), 4), ALU.mult).then_inc(S("rt_q2"), 1)
                if b == 2:
                    gp.wait_ge(S("rt_tok"), it)
                    vt = vkt[0:CH, 0:2, :].rearrange("p a (h c) -> p (a h) c", c=HD)
                    for h in range(HB):
                        m = tt(vx[:, h, :, :], rep(vt[:, h, :], NSEQ), over(C("seq", rows=slice(0, CH)), HD), ALU.mult)
                    m.then_inc(S("rt_vx"), 1)

            def mamba(l, b):
                it, (c0, n) = 3 * l + b + 1, BLOCKS[b]
                gp.wait_ge(S("mb_ecb"), it)
                gp.wait_ge(S("mb_xc"), it)
                for g in range(2):
                    m = tt(cde[:, 3 * g:3 * g + 3, 0:n], ecb[:, 3 * g:3 * g + 3, 0:n], rep(xc[:, 5 + g, 0:n], 3), ALU.mult)
                m.then_inc(S("mb_cde"), 1)
                if b == 2:
                    gp.wait_ge(S("mb_xdt"), it)
                    for g in range(2):
                        if g:
                            gp.wait_ge(S("mb_ds"), 2 * l + 1)
                        tt(xwe[:, :, :, :].rearrange("p s h c -> p s (h c)"),
                           rep(xw[0:CH, 3 * g:3 * g + 3, :].rearrange("p h c -> p (h c)"), NSEQ),
                           over(C("seq", rows=slice(0, CH)), 3 * HD), ALU.mult).then_inc(S("mb_xwe"), 1)

            def out(dst, src):
                gp.dma_start(dst, src).then_inc(S("st_out"), 16)

            gp.sem_inc(S("yt_free"), KT)
            gp.dma_start(par[:, :], par_in[0]).then_inc(S("par_in"), 16)
            gp.wait_ge(S("const_in"), 16)
            for l in range(DEPTH):
                if l:
                    gp.wait_ge(S("h_split"), KT * 2 * l + 1)
                    gp.wait_ge(S("st_out"), 16 * 8 * l)
                gp.dma_start(sh_in[:, :, :], s_sh[l]).then_inc(S("ends_in"), 16)
                gp.dma_start(cv_in[:, :, :, :], s_cv[l]).then_inc(S("ends_in"), 16)
                gp.dma_start(srw[:, :, :, :], s_rw[l]).then_inc(S("srw_in"), 16)
                gp.memset(srw_p[:, :, :], 0.0)
                gp.memset(srt_p[:, :, :], 0.0)
                gp.memset(smb_p[:, :], 0.0).then_inc(S("zeroed"), 1)
                gp.memset(cR[:, :, 0:1], 0.0)
                gp.memset(cX[:, :, 0:3], 0.0)
                gp.wait_ge(S("ends_in"), 32 * (l + 1))
                rows = cR[:, :, EA:WA_].rearrange("p t (s k) -> p t s k", k=STEP + 1)
                xrows = cX[:, :, EX:WX_].rearrange("p t (s k) -> p t s k", k=STEP + 3)
                gp.tensor_copy(rows[:, :, :, 0], sh_in[:, :, :])
                gp.tensor_copy(xrows[:, :, :, 0:3], cv_in[:, :, :, :]).then_inc(S("ext_ready"), 1)
                gp.wait_ge(S("in_read"), WIN * (l + 1))
                gp.tensor_copy(sh_out[:, :, 0:1], cR[:, :, EA - 1:EA])
                gp.tensor_copy(sh_out[:, :, 1:], rows[:, :, :, STEP])
                gp.tensor_copy(cv_out[:, :, 0, :], cX[:, :, EX - 3:EX])
                gp.tensor_copy(cv_out[:, :, 1:, :], xrows[:, :, :, STEP:]).then_inc(S("ends"), 1)
                gp.wait_ge(S("ends"), l + 1)
                out(o_sh[l], sh_out[:, :, :])
                out(o_cv[l], cv_out[:, :, :, :])
                for b in range(3):
                    rwkv(l, b)
                gp.wait_ge(S("rw_Sbd"), 5 * (l + 1))
                out(p_rw[l], srw_p[:, :, :])
                gp.wait_ge(S("rw_sS"), 3 * (l + 1))
                out(o_rw[l], srw[:, :, :, :])
                gp.wait_ge(S("mix_done"), 9 * l + 3)
                gp.wait_ge(S("st_out"), 16 * (8 * l + 4))
                gp.dma_start(srt[:, :, :, :], s_rt[l]).then_inc(S("srt_in"), 16)
                for b in range(3):
                    retention(l, b)
                gp.wait_ge(S("rt_S"), 2 * (l + 1))
                out(p_rt[l], srt_p[:, :, :])
                gp.wait_ge(S("rt_sS"), l + 1)
                out(o_rt[l], srt[:, :, :, :])
                gp.wait_ge(S("mix_done"), 9 * l + 6)
                gp.wait_ge(S("st_out"), 16 * (8 * l + 6))
                gp.dma_start(smb[:, :, :, :, :], s_mb[l]).then_inc(S("smb_in"), 16)
                for b in range(3):
                    mamba(l, b)
                gp.wait_ge(S("mb_S"), 2 * (l + 1))
                out(p_mb[l], smb_p[:, :])
                gp.wait_ge(S("mb_ds_used"), 2 * (l + 1))
                out(o_mb[l], smb[:, :, :, :, :])
                if l + 1 < DEPTH:
                    gp.wait_ge(S("h_split"), KT * (2 * l + 2))
                    gp.dma_start(par[:, :], par_in[l + 1]).then_inc(S("par_in"), 16)
                else:
                    with gp.Fori(0, NEXP) as i:
                        for m_ in range(KT):
                            gp.wait_ge(S("dn_free"), i * KT + (N_E[0] * KT + KT + m_ + 1))
                            gp.wait_ge(S("yt_free"), i * KT + m_ + 1)
                            tt(x[:, m_, :], x[:, m_, :], yt[:, m_ % 4, :], ALU.add).then_inc(S("yt_free"), 1)
            gp.wait_ge(S("st_out"), 16 * 8 * DEPTH)



def tiles_of(m):
    a, b = m.shape
    return m.reshape(a // P, P, b // P, P).transpose(2, 1, 0, 3)


def slots_in(m):
    b = -(-m.shape[1] // P) * P
    pad = np.zeros((m.shape[0], b), m.dtype)
    pad[:, :m.shape[1]] = m
    return tiles_of(pad).reshape(b // P, P, D)


def slots_expert(wg, wu, wd):
    gu = np.stack([slots_in(wg), slots_in(wu)], 1).reshape(2 * FT, P, D)
    dn = tiles_of(wd).transpose(0, 2, 1, 3).reshape(KT * FT, P, P)
    return [gu, dn.reshape(FT, KT, P, P).transpose(0, 2, 1, 3).reshape(FT, P, D)]


def fm(a, axis=-1):
    return a.reshape(-1, P).T


def kernel(**inputs):
    import concourse.bacc as bacc
    from concourse.bass_utils import run_bass_kernel_spmd

    a = {k: np.asarray(v) for k, v in inputs.items()}
    f32 = np.float32
    xt = np.concatenate([a["x_prompt"].reshape(SEQ, D), a["x_sample"].reshape(NSEQ * STEP, D)], 0)
    x_in = xt.T.reshape(KT, P, T).transpose(1, 0, 2)

    stream = []
    for l in range(DEPTH):
        stream += [slots_in(a["w_in"][l]), slots_in(a["w_out"][l])]
        if l == 0:
            for h in range(2):
                c = slice(h * FE, (h + 1) * FE)
                stream += slots_expert(a["ffn_w_gate"][0][:, c], a["ffn_w_up"][0][:, c], a["ffn_w_down"][0][c])
        else:
            stream.append(slots_in(a["moe_router"][0]))
            for e in range(NEXP):
                stream += slots_expert(a["moe_w_gate"][0, e], a["moe_w_up"][0, e], a["moe_w_down"][0, e])
    stream.append(np.zeros((N_SLOTS - G_END, P, D), f32))
    w_in = np.concatenate(stream, 0)
    assert w_in.shape[0] == N_SLOTS

    par = np.zeros((DEPTH, P, NPAR), f32)

    def put(name, l, v):
        par[l, :v.shape[0], PAR[name]:PAR[name] + v.shape[1]] = v

    for l in range(DEPTH):
        for name, src in [("g_mix", a["norm_mix"][l]), ("g_ffn", a["norm_ffn"][l]), ("g_fin", a["norm_final"]),
                          ("mu", a["rwkv_mu"][l]), ("w0", a["rwkv_w0"][l]), ("a0", a["rwkv_a0"][l]),
                          ("k_k", a["rwkv_k_k"][l]), ("k_a", a["rwkv_k_a"][l]), ("r_k", a["rwkv_r_k"][l]),
                          ("ln_w", a["rwkv_ln_w"][l]), ("ln_b", a["rwkv_ln_b"][l]), ("ret_norm", a["ret_norm"][l]),
                          ("conv_b", a["ssm_conv_b"][l]), ("ssm_norm", a["ssm_norm"][l]),
                          ("d", np.repeat(a["ssm_d"][l], HD))]:
            put(name, l, fm(src.reshape(-1)))
        put("conv_w", l, np.concatenate([fm(a["ssm_conv_w"][l, j]) for j in range(CONV)], 1))
        put("dt_bias", l, a["ssm_dt_bias"][l][:, None])
        put("a_log", l, a["ssm_a_log"][l][:, None])
        put("wa_up", l, np.concatenate([a["rwkv_w_up"][l], a["rwkv_a_up"][l]], 0))
        put("g_up", l, a["rwkv_g_up"][l])

    rw = a["state_rwkv"].transpose(0, 2, 4, 1, 3).reshape(DEPTH, TA, P, NSEQ, HD).transpose(0, 2, 1, 3, 4)
    rt = a["state_ret"].transpose(0, 2, 3, 1, 4).reshape(DEPTH, TB, P, NSEQ, HD).transpose(0, 2, 1, 3, 4)
    mb = a["state_ssm"].transpose(0, 4, 1, 2, 3).reshape(DEPTH, NST, NSEQ, 2, 3, HD).transpose(0, 1, 3, 2, 4, 5)
    sh = a["state_shift"].transpose(0, 2, 1).reshape(DEPTH, A_TILES, P, NSEQ).transpose(0, 2, 1, 3)
    cv = a["state_conv"].transpose(0, 3, 1, 2).reshape(DEPTH, XT, P, NSEQ, 3).transpose(0, 2, 1, 3, 4)
    ins = [("x", x_in), ("w", w_in), ("consts", constants()[0]), ("par", par), ("s_rwkv", rw), ("s_ret", rt),
           ("s_ssm", mb), ("s_shift", sh), ("s_conv", cv)]
    outs = [("y", (P, KT, T)), ("p_rwkv", (DEPTH, P, TA, HD)), ("p_ret", (DEPTH, P, TB, HD)),
            ("p_ssm", (DEPTH, P, HC * HD)), ("o_rwkv", rw.shape), ("o_ret", rt.shape), ("o_ssm", mb.shape),
            ("o_shift", (DEPTH, P, A_TILES, 1 + NSEQ)), ("o_conv", (DEPTH, P, XT, 1 + NSEQ, 3))]

    nc = bacc.Bacc("TRN2", target_bir_lowering=False, num_devices=1)
    arrays, args = {}, []
    for name, v in ins:
        arrays["in_" + name] = np.ascontiguousarray(v)
        args.append(nc.dram_tensor("in_" + name, v.shape, F32, kind="ExternalInput").ap())
    for name, shape in outs:
        args.append(nc.dram_tensor("out_" + name, shape, F32, kind="ExternalOutput").ap())
    trunk(nc, *args)
    r = run_bass_kernel_spmd(nc, [arrays], core_ids=[0]).results[0]
    y, p_rw, p_rt, p_mb, o_rw, o_rt, o_mb, o_sh, o_cv = (np.asarray(r["out_" + name]) for name, _ in outs)

    y = y.transpose(2, 1, 0).reshape(T, D)

    def heads_rw(s):
        n = s.shape[3]
        return s.transpose(0, 2, 1, 3, 4).reshape(DEPTH, HA, HD, n, HD).transpose(0, 3, 1, 4, 2)

    def heads_rt(s):
        n = s.shape[3]
        return s.transpose(0, 2, 1, 3, 4).reshape(DEPTH, HB, HD, n, HD).transpose(0, 3, 1, 2, 4)

    p_ssm = p_mb.reshape(DEPTH, NST, HC, HD).transpose(0, 2, 3, 1)[:, None]
    s_ssm = o_mb.transpose(0, 3, 2, 4, 5, 1).reshape(DEPTH, NSEQ, HC, HD, NST)
    shift = o_sh.transpose(0, 3, 2, 1).reshape(DEPTH, 1 + NSEQ, COLS_A)
    conv = o_cv.transpose(0, 3, 4, 2, 1).reshape(DEPTH, 1 + NSEQ, 3, CONV_DIM)
    return (y[:SEQ].reshape(1, SEQ, D), y[SEQ:].reshape(NSEQ, STEP, D),
            heads_rw(p_rw[:, :, :, None]), shift[:, :1], heads_rt(p_rt[:, :, :, None]), p_ssm, conv[:, :1],
            heads_rw(o_rw), shift[:, 1:], heads_rt(o_rt), s_ssm, conv[:, 1:])
```

```python
from contextlib import ExitStack

import numpy as np
import concourse.bass as bass
from concourse import mybir

F32 = mybir.dt.float32
F32R = mybir.dt.float32r
ALU = mybir.AluOpType
ACT = mybir.ActivationFunctionType
AX = mybir.AxisListType

P = 128
D = 1024
SEQ = 256
DEPTH = 2
NSEQ = 8
STEP = 8
PAST = 2048
T = SEQ + NSEQ * STEP
KT = D // P
HD = 64
HA, HB, HC = 6, 4, 6
TA, TB, TC = HA // 2, HB // 2, HC // 2
COLS_A = 3 * HA * HD + 256
COLS_B = 4 * HB * HD
NST = 128
CONV = 4
CONV_DIM = HC * HD + 2 * 2 * NST
XT = CONV_DIM // P
FE = 1408
FT = FE // P
NEXP = 8
A_TILES = COLS_A // P
B_TILES = COLS_B // P
C_TILES = TC + XT
WIN = A_TILES + B_TILES + C_TILES + 1
EXP_SLOTS = 3 * FT
CHUNKS = [(4 * c, 4, 2) for c in range(FT // 2)] + [(2 * FT - 2, 2, 1)]
NC = len(CHUNKS)
ENDS = {j + n - 1: c for c, (j, n, _) in enumerate(CHUNKS)}
TURN = {j + n + 1: c for c, (j, n, _) in enumerate(CHUNKS)}
BLOCKS = [(0, 128), (128, 128), (256, 64)]
CH = 64
SQE = float(np.exp(-0.5))
EA, EX = 1 + SEQ, 3 + SEQ
WA_, WX_ = EA + NSEQ * (STEP + 1), EX + NSEQ * (STEP + 3)

RAW, HI = 11, 3
YR = 4
G_IN = [0, WIN + KT + 2 * EXP_SLOTS]
G_OUT = [g + WIN for g in G_IN]
G_FFN = [G_OUT[0] + KT, G_OUT[1] + KT + 1]
N_E = [2, NEXP]
E0 = [0, 2]
G_END = G_FFN[1] + NEXP * EXP_SLOTS
N_SLOTS = G_END + HI

PAR = {}


def _par(name, n, at=[0]):
    PAR[name] = at[0]
    at[0] += n
    return at[0]


for _n, _w in [("g_mix", 8), ("g_ffn", 8), ("g_fin", 8), ("mu", A_TILES), ("w0", 3), ("a0", 3), ("k_k", 3),
               ("k_a", 3), ("r_k", 3), ("ln_w", 3), ("ln_b", 3), ("ret_norm", 2), ("conv_w", 4 * XT),
               ("conv_b", XT), ("d", 3), ("ssm_norm", 3), ("dt_bias", 1), ("a_log", 1),
               ("wa_up", 384), ("g_up", 384)]:
    NPAR = _par(_n, _w)


def constants():
    i = np.arange(P)
    c = {}
    c["ident"] = np.eye(P)
    c["ones"] = np.ones((P, P))
    c["bd"] = (i[:, None] // HD == i[None, :] // HD) * 1.0
    c["swap"] = (i[:, None] == (i[None, :] ^ 32)) * 1.0
    pos = np.concatenate([np.arange(SEQ), np.tile(PAST + np.arange(STEP), NSEQ)]).astype(np.float32)
    theta = (1.0 / (np.float32(10000.0) ** np.linspace(0.0, 1.0, HD // 2, dtype=np.float32))).astype(np.float32)
    ang = (pos[None, :] * theta[i % 32][:, None]).astype(np.float32).astype(np.float64)
    c["cos"] = np.cos(ang)
    c["sin"] = np.sin(ang) * np.where(i % HD < 32, -1.0, 1.0)[:, None]
    gam = 1.0 - 2.0 ** (-5.0 - np.arange(HB))
    hb = (np.arange(TB)[None, :] * 2 + (i // HD)[:, None])
    g = gam[hb]
    at = np.concatenate([np.arange(SEQ) % P, np.tile(np.arange(STEP), NSEQ)])
    ln = np.concatenate([np.full(SEQ, P), np.full(NSEQ * STEP, STEP)])
    c["qdec"] = g[:, :, None] ** (at + 1)[None, None, :]
    c["kdec"] = g[:, :, None] ** (ln - 1 - at)[None, None, :]
    c["cdec"] = np.stack([g ** P, g ** STEP], 1)
    diff = i[None, :] - i[:, None]
    same8 = i[:, None] // STEP == i[None, :] // STEP
    gam = gam[[0, 2, 1, 3]]
    c["rmask"] = np.where((diff >= 0)[:, None], gam[None, :, None] ** np.maximum(diff, 0)[:, None], 0.0)
    c["rmask8"] = c["rmask"][:, :, :HD] * same8[:, None, :HD]
    c["causal"] = (diff >= 0) * 1.0
    c["causal8"] = ((diff >= 0) & same8)[:, :HD] * 1.0
    j = np.arange(CH)
    s, t = (i % CH)[:, None], j[None, :]
    s8 = s // STEP == t // STEP
    c["strict"], c["incl"] = (s < t) * 1.0, (s <= t) * 1.0
    c["strict8"], c["incl8"] = (s < t) & s8, (s <= t) & s8
    c["i64"] = (s == t) * 1.0
    c["lev"] = np.stack([(s >> (q + 1) == t >> (q + 1)) & (s >> q & 1 == 0) & (t >> q & 1 == 1)
                         for q in range(6)], 1)
    c["scan64"] = np.tile((np.arange(P) % CH != 0) * 1.0, (P, 1))
    c["scan8"] = np.tile((np.arange(CH) % STEP != 0) * 1.0, (P, 1))
    c["scanm"] = np.tile((at != 0) * 1.0, (P, 1))
    c["seq"] = (i[:, None] // STEP == np.arange(NSEQ)[None, :]) * 1.0
    c["sel"] = np.repeat(i[:, None] == np.arange(NEXP)[None, :], P, 1) * 1.0
    c["before"] = np.tile((np.arange(8)[None, :] < np.arange(8)[:, None]).reshape(1, 64), (P, 1)) * 1.0
    c["eps"] = np.tile(np.array([1e-6, 64e-5, 1e-5, 0.0]), (P, 1))
    cols, parts, n = {}, [], 0
    for k, v in c.items():
        v = np.asarray(v, np.float64).reshape(P, -1)
        cols[k] = (n, v.shape[1])
        parts.append(v)
        n += v.shape[1]
    return np.ascontiguousarray(np.concatenate(parts, 1).astype(np.float32)), cols


def trunk(nc, x_in, w_in, consts_in, par_in, s_rw, s_rt, s_mb, s_sh, s_cv,
          y_out, p_rw, p_rt, p_mb, o_rw, o_rt, o_mb, o_sh, o_cv):
    CC = constants()[1]
    NCONST = consts_in.shape[1]
    ctx = ExitStack()
    with ctx:
        sems = {}

        def S(name):
            if name not in sems:
                sems[name] = ctx.enter_context(nc.semaphore(name))
            return sems[name]

        base = (nc.sbuf_base + 63) // 64 * 64
        top = [base]

        def sb(name, shape, dt=F32, offset=None):
            size = int(np.prod(shape[1:])) * 4
            at = top[0] if offset is None else offset
            t = nc.alloc_sbuf_tensor_at(name, shape, dt, offset=at)
            if offset is None:
                top[0] = (at + size + 63) // 64 * 64
            return t

        raw_at = top[0]
        wraw = sb("wraw", [P, RAW, D])
        wlo = sb("wlo", [P, RAW, D], F32R, offset=raw_at)
        whi = sb("whi", [P, HI, D], F32R)
        x = sb("x", [P, KT, T])
        hh = sb("hh", [P, KT, T], F32R)
        hl = sb("hl", [P, KT, T], F32R)
        rstd = sb("rstd", [P, T])
        cst = sb("cst", [P, NCONST])
        par = sb("par", [P, NPAR])
        srw_p = sb("srw_p", [P, TA, HD])
        srt_p = sb("srt_p", [P, TB, HD])
        smb_p = sb("smb_p", [P, HC * HD])
        sh_out = sb("sh_out", [P, A_TILES, 1 + NSEQ])
        sh_in = sb("sh_in", [P, A_TILES, NSEQ])
        cv_in = sb("cv_in", [P, XT, NSEQ, 3])
        cv_out = sb("cv_out", [P, XT, 1 + NSEQ, 3])
        area = top[0]
        cR = sb("cR", [P, A_TILES, WA_])
        cB = sb("cB", [P, B_TILES, T])
        cZ = sb("cZ", [P, TC, T])
        cX = sb("cX", [P, XT, WX_])
        cD = sb("cD", [8, T])
        work = top[0]
        srw = sb("srw", [P, TA, NSEQ, HD])
        lent = top[0]
        TM, Wm = (sb(n, [P, HA, CH]) for n in ("TM", "Wm"))
        Sbd = sb("Sbd", [P, TA, P])
        AL = sb("AL", [P, 2, HA, CH])
        tw = sb("tw", [P, P])
        rwx = sb("rwx", [HD, 2, NSEQ, P], offset=lent)
        assert lent + 8 * 1024 == top[0]
        Dx = sb("Dx", [P, A_TILES, P])
        U = {k: sb("u_" + k, [P, TA, P]) for k in
             ("sg", "L", "P", "Pi", "Pm", "aa", "kr", "kp", "t1", "be", "rho", "g")}
        U["Lm"], U["sq"], U["br"], U["ka"] = U["sg"], U["rho"], U["t1"], U["Pi"]
        U["kk"], U["al"], U["bonus"] = U["kr"], U["Pm"], U["L"]
        gs = U["rho"][:, 0, :]
        tok = sb("tok", [P, 3, TA, P])
        AB, C12 = (sb(n, [P, 2, 2, TA, CH]) for n in ("AB", "C12"))
        TT = sb("TT", [P, HA, CH])
        Rs = sb("Rs", [P, HA, CH])
        Rs0 = Rs[:, 0:TA, :]
        SA = U["sg"][:, :, :].rearrange("p t (h c) -> p (t h) c", c=CH)
        rw_end = top[0]
        top[0] = work
        qk = sb("qk", [P, 4, P])
        qk2 = sb("qk2", [P, 4, P])
        qkd = sb("qkd", [P, 4, P])
        rsc = sb("rsc", [P, HB, P])
        vkt = sb("vkt", [P, 4, P])
        vx = sb("vx", [HD, HB, NSEQ, HD])
        ro = sb("ro", [P, TB, P])
        rsq = sb("rsq", [P, TB, P])
        rsg = sb("rsg", [P, TB, P])
        srt = sb("srt", [P, TB, NSEQ, HD])
        rt_end = top[0]
        top[0] = work
        smb = sb("smb", [P, 2, NSEQ, 3, HD])
        dd = {k: sb("d_" + k, [8, T]) for k in ("x", "e", "z", "z2", "p", "dt")}
        dd["dA"], dd["cum"], dd["lm"], dd["wk"] = dd["z"], dd["p"], dd["z2"], dd["e"]
        an = sb("an", [8, 1])
        xc = sb("xc", [P, XT, P])
        xwe = sb("xwe", [HD, NSEQ, 3, HD])
        xcs = sb("xcs", [P, XT, P], offset=top[0] - NSEQ * 3 * HD * 4)
        tk3 = sb("tk3", [P, 3, HC])
        ecb = sb("ecb", [P, HC, P])
        seg = sb("seg", [P, HC, P])
        xdt = sb("xdt", [P, HC, HD])
        xw = sb("xw", [P, HC, HD])
        Btk = sb("Btk", [P, 2, P])
        cbm = sb("cbm", [P, 2, P])
        wts = sb("wts", [P, HC, P])
        cde = sb("cde", [P, HC, P])
        yz = sb("yz", [P, TC, P])
        ysq = sb("ysq", [P, TC, P])
        zs = sb("zs", [P, TC, P])
        mb_end = top[0]
        mix_end = max(rw_end, rt_end, mb_end)
        htmp = sb("htmp", [P, 2, T], offset=mix_end - 4 * T * 4)
        sqb = sb("sqb", [P, 2, T], offset=mix_end - 2 * T * 4)
        top[0] = area
        hidh = sb("hidh", [P, FT, T], F32R)
        hidl = sb("hidl", [P, FT, T], F32R)
        sil_at = top[0]
        sil = sb("sil", [P, 2, T])
        hid = sb("hid", [P, 2, T])
        yt_at = top[0]
        yt = sb("yt", [P, YR, T])
        gbc = sb("gbc", [P, NEXP, T])
        place = sb("place", [P, NEXP, T], F32R, offset=top[0] - NEXP * T * 4)
        lg = sb("lg", [NEXP, T])
        rt = {k: sb("rt_" + k, [P, 3, NEXP]) for k in ("l", "e", "p", "rank", "g", "pos")}
        rt1 = sb("rt1", [P, 3, 4])
        slot_no = sb("slot_no", [P, 1])
        slot_gate = sb("slot_gate", [P, NEXP])
        n_most = sb("n_most", [1, 2])
        n_most_i = sb("n_most_i", [1, 1], mybir.dt.int32)
        count_up = sb("count_up", [P, P])
        htk = [sb("htk_" + k, [P, 3, D], F32R) for k in "hl"]
        pick = sb("pick", [P, NEXP + 1, 3, P], F32R)
        exp_end, top[0] = top[0], sil_at
        chosen, ones8, upto, pos1 = (sb(k, [NEXP, T]) for k in ("chosen", "ones8", "upto", "pos1"))
        assert top[0] <= yt_at
        top[0] = yt_at
        cmp = sb("cmp", [P, 3, NEXP, NEXP])
        cmq = sb("cmq", [P, 3, NEXP, NEXP])
        top[0] = exp_end
        assert max(mix_end, top[0]) <= nc.sbuf_usable_end, (mix_end, top[0], nc.sbuf_usable_end)

        B = [ctx.enter_context(nc.psum_tensor(f"bank{i}", [P, 512], F32)) for i in range(8)]

        def C(name, lo=0, n=None, rows=slice(0, P)):
            at, w = CC[name]
            return cst[rows, at + lo:at + (w if n is None else lo + n)]

        def V(name, i=0, n=1, rows=slice(0, P)):
            return par[rows, PAR[name] + i:PAR[name] + i + n]

        def over(ap, n):
            return ap.unsqueeze(2).to_broadcast([ap.shape[0], ap.shape[1], n])

        def rep(ap, n):
            return ap.unsqueeze(1).to_broadcast([ap.shape[0], n, ap.shape[1]])

        def bank(b, n_tiles, n, rows=slice(0, P)):
            return B[b][rows, 0:n_tiles * P].rearrange("p (a c) -> p a c", c=P)[:, :, 0:n]

        def b64(b, k, rows=slice(0, P)):
            return B[b][rows, 0:k * HD].rearrange("p (a c) -> p a c", c=HD)

        def halves(ap, q, odd):
            return ap.rearrange("p h (a o s) -> p h a o s", o=2, s=1 << q)[:, :, :, odd, :]

        def half1(ap, q, odd):
            return ap.rearrange("p (a o s) -> p a o s", o=2, s=1 << q)[:, :, odd, :]

        def c3(ap, q):
            return ap.rearrange("p h (a s) -> p h a s", s=1 << q)

        def ho(h):
            return (h % 2) * TA + h // 2

        def levels(b):
            return 3 if b == 2 else 6

        def chunks(b):
            return 1 if b == 2 else 2

        def expert_loop(eng, l, body):
            with eng.Fori(0, N_E[l]) as i:
                body(i, i * EXP_SLOTS + G_FFN[l], i + E0[l])

        block = ctx.enter_context(nc.Block())

        @block.sync
        def _(sp):
            def slot(g, ring):
                if not isinstance(g, int) or g >= RAW:
                    sp.wait_ge(S("slot_used"), g - RAW + 1)
                if isinstance(g, int):
                    sp.dma_start(wraw[:, ring % RAW, :], w_in[g, :, :]).then_inc(S(f"slot_in{ring % RAW}"), 16)
                else:
                    src = w_in[bass.ds(g, 1), :, :].rearrange("o p c -> (o p) c")
                    sp.dma_start(wraw[:, ring % RAW, :], src).then_inc(S(f"slot_in{ring % RAW}"), 16)

            sp.dma_start(x[:, :, :], x_in).then_inc(S("x_in"), 16)
            for l in range(DEPTH):
                for g in range(G_IN[l], G_FFN[l]):
                    slot(g, g)

                def body(i, g, e):
                    for j in range(EXP_SLOTS):
                        slot(g + j, G_FFN[l] + j)
                expert_loop(sp, l, body)
            for g in range(G_END, N_SLOTS):
                slot(g, g)
            sp.wait_ge(S("y_done"), 1)
            sp.dma_start(y_out, x[:, :, :]).then_inc(S("y_out"), 16)
            sp.wait_ge(S("y_out"), 16)

        @block.tensor
        def _(pe):
            mm = pe.matmul

            def mx(out, lhsT, rhs, start, stop):
                return pe.matmul(out, lhsT, rhs, start=start, stop=stop, skip_group_check=True)

            def three(out, k, slot_ring, rh, rl, first, last):
                hi = whi[:, slot_ring % HI, k * P:(k + 1) * P]
                lo = wlo[:, slot_ring % RAW, k * P:(k + 1) * P]
                mm(out, hi, rh, start=first, stop=False)
                mm(out, hi, rl, start=False, stop=False)
                return mm(out, lo, rh, start=False, stop=last)

            def full_slot(g, ring, out, h_from=None):
                pe.wait_ge(S("slot_split"), g + 1)
                for k in range(KT):
                    if h_from is not None:
                        pe.wait_ge(S("h_split"), h_from + k + 1)
                    m = three(out, k, ring, hh[:, k, :], hl[:, k, :], k == 0, k == KT - 1)
                m.then_inc(S("slot_used"), 1)

            def norm(i):
                for k in range(KT):
                    pe.wait_ge(S("sq_ready"), KT * i + k + 1)
                    m = mm(B[0][:, 0:T], C("ones"), sqb[:, k % 2, :], start=(k == 0), stop=(k == KT - 1))
                    m.then_inc(S("sq_used"), 1)

            def rwkv(l, b):
                it, n = 3 * l + b + 1, BLOCKS[b][1]
                nch, cb, lv = chunks(b), 5 * l + 2 * b, 15 * l + 6 * b
                pe.wait_ge(S("rw_lora"), it)
                for q, (rows, src, name) in enumerate([(slice(0, 64), tw[0:64, 0:n], "wa_up"),
                                                       (slice(64, P), Dx[64:P, 9, 0:n], "wa_up"),
                                                       (slice(0, P), gs[:, 0:n], "g_up")]):
                    for t in range(TA):
                        m = mm(B[q][:, t * P:t * P + n], V(name, t * P, P, rows), src, start=True, stop=True)
                    m.then_inc(S("rw_up"), 1)
                pe.wait_ge(S("rw_sq"), it)
                mm(bank(3, 3, n), C("bd"), U["sq"][:, :, 0:n], start=True, stop=True).then_inc(S("rw_ss"), 1)
                pe.wait_ge(S("rw_br"), it)
                mm(bank(4, 3, n), C("bd"), U["br"][:, :, 0:n], start=True, stop=True).then_inc(S("rw_bsum"), 1)
                pe.wait_ge(S("rw_ops"), it)
                pe.wait_ge(S("rw_sig"), 3 * it)
                for q, (bk, src) in enumerate([(5, Dx[:, 6:9, 0:n]), (0, U["be"][:, :, 0:n]), (1, U["ka"][:, :, 0:n])]):
                    for t in range(TA):
                        m = pe.transpose(B[bk][0:n, t * P:(t + 1) * P], src[:, t, :], C("ident"))
                    m.then_inc(S("rw_tr"), 1)
                pe.wait_ge(S("rw_ssm"), it)
                for q, bk in ((0, 2), (1, 4)):
                    if q == 1:
                        pe.wait_ge(S("rw_bonus"), it)
                        pe.wait_ge(S("rw_tok"), 3 * it)
                    for par_ in range(2):
                        r = slice(64 * par_, 64 * par_ + 64)
                        for z, lh in enumerate(("be", "ka")):
                            for t in range(TA):
                                for c in range(nch):
                                    lo = (z * TA + t) * CH
                                    m = mm(B[bk + par_][64 * c:64 * c + 64, lo:lo + CH],
                                           U[lh][r, t, c * CH:(c + 1) * CH],
                                           U[("al", "rho")[q]][r, t, c * CH:(c + 1) * CH], start=True, stop=True)
                        m.then_inc(S("rw_sc"), 1)
                for q in range(levels(b)):
                    pe.wait_ge(S("rw_T"), lv + q + it)
                    pe.wait_ge(S("rw_AL"), lv + q + 1)
                    for h in range(HA):
                        for c in range(nch):
                            r = slice(64 * c, 64 * c + 64)
                            m = mm(B[0][r, h * CH:(h + 1) * CH], AL[r, q % 2, h, :], TM[r, h, :], start=True, stop=True)
                    m.then_inc(S("rw_W"), 1)
                    pe.wait_ge(S("rw_Wc"), lv + q + 1)
                    if q == 0:
                        pe.wait_ge(S("rw_AT"), it)
                    for bk, odd in ((1, 0), (2, 1)):
                        for h in range(HA):
                            for c in range(nch):
                                r = slice(64 * c, 64 * c + 64)
                                out = B[bk][r, h * 32:(h + 1) * 32]
                                if odd:
                                    m = mm(out, Wm[r, h, :], half1(TT[r, h, :], q, 1), start=True, stop=True)
                                else:
                                    m = mm(out, TT[r, h, :], half1(Wm[r, h, :], q, 0), start=True, stop=True)
                    m.then_inc(S("rw_TW"), 1)
                pe.wait_ge(S("rw_T"), lv + levels(b) + it)
                pe.wait_ge(S("rw_C"), it)
                for c in range(nch):
                    r = slice(64 * c, 64 * c + 64)
                    cs = slice(c * CH, (c + 1) * CH)
                    vt, bt, kt = (tok[r, q, :, :].rearrange("p a c -> p (a c)") for q in range(3))
                    if b == 2:
                        pe.wait_ge(S("srw_in"), 16 * (l + 1))
                        for h in range(HA):
                            p = slice(64 * (h % 2), 64 * (h % 2) + 64)
                            for s in range(NSEQ):
                                m = mm(B[0][p, (h // 2) * CH + s * STEP:(h // 2) * CH + (s + 1) * STEP],
                                       srw[p, h // 2, s, :], U["al"][p, h // 2, s * STEP:(s + 1) * STEP],
                                       start=True, stop=True)
                        m.then_inc(S("rw_S0"), 1)
                        pe.wait_ge(S("rw_S0c"), l + 1)
                    else:
                        pe.wait_ge(S("rw_Sbd"), 5 * l + 2 * b + c + 1)
                    for t in range(TA):
                        pair = B[3][r, t * P:(t + 1) * P]
                        for o in range(2):
                            hs = slice(t * P + o * HD, t * P + (o + 1) * HD)
                            mx(B[3][r, hs], AB[r, o, 1, t, :], vt[:, hs], o == 0, False)
                        if b == 2:
                            m = mx(pair, Rs0[:, t, :], C("ident"), False, True)
                        else:
                            m = mx(pair, U["al"][:, t, cs], Sbd[:, t, :], False, True)
                    m.then_inc(S("rw_R"), 1)
                    pe.wait_ge(S("rw_Rc"), cb + c + 1)
                    for h in range(HA):
                        m = mm(B[4][r, h * HD:(h + 1) * HD], TT[r, ho(h), :], Rs[r, h, :], start=True, stop=True)
                    m.then_inc(S("rw_SA"), 1)
                    pe.wait_ge(S("rw_SAc"), cb + c + 1)
                    if b < 2:
                        for h in range(HA):
                            p = slice(64 * (h % 2), 64 * (h % 2) + 64)
                            out = B[0][p, (h // 2) * HD:(h // 2 + 1) * HD]
                            hs = slice(h * HD, (h + 1) * HD)
                            mx(out, bt[:, hs], SA[r, h, :], True, False)
                            m = mx(out, kt[:, hs], vt[:, hs], False, True)
                        m.then_inc(S("rw_dS"), 1)
                    for h in range(HA):
                        p = slice(64 * (h % 2), 64 * (h % 2) + 64)
                        lo = (h // 2) * P + c * CH
                        out = B[5][p, lo:lo + CH]
                        mx(out, SA[r, h, :], C12[r, h % 2, 0, h // 2, :], True, False)
                        m = mx(out, vt[:, h * HD:(h + 1) * HD], C12[r, h % 2, 1, h // 2, :], False, b == 2)
                        if b == 2:
                            for s in range(NSEQ):
                                t8 = slice(s * STEP, (s + 1) * STEP)
                                m = mm(B[0][p, (h // 2) * P + s * STEP:(h // 2) * P + (s + 1) * STEP], srw[p, h // 2, s, :],
                                       U["rho"][p, h // 2, t8], start=True, stop=True)
                        elif h % 2:
                            m = mx(B[5][:, lo:lo + CH], Sbd[:, h // 2, :], U["rho"][:, h // 2, cs], False, True)
                    m.then_inc(S("rw_y"), 1)
                if b == 2:
                    for t in range(TA):
                        pe.wait_ge(S("rw_xs"), 3 * l + t + 1)
                        pe.wait_ge(S("rw_xv"), 3 * l + t + 1)
                        for h in (2 * t, 2 * t + 1):
                            p = slice(64 * (h % 2), 64 * (h % 2) + 64)
                            o = slice((h % 2) * HD, (h % 2) * HD + HD)
                            hs = slice(h * HD, (h + 1) * HD)
                            mx(B[1 + t][p, :], bt[:, hs], rwx[:, 0, :, o], True, False)
                            m = mx(B[1 + t][p, :], kt[:, hs], rwx[:, 1, :, o], False, True)
                        m.then_inc(S("rw_ds"), 1)
                pe.wait_ge(S("rw_yc"), it)
                if b == 2:
                    pe.wait_ge(S("rw_sSa"), l + 1)
                mm(bank(3, 3, n), C("bd"), U["kr"][:, :, 0:n], start=True, stop=True).then_inc(S("rw_mean"), 1)
                pe.wait_ge(S("rw_ysq"), it)
                mm(bank(4, 3, n), C("bd"), U["sq"][:, :, 0:n], start=True, stop=True).then_inc(S("rw_var"), 1)

            def retention(l, b):
                it, (c0, n) = 3 * l + b + 1, BLOCKS[b]
                pe.wait_ge(S("mix_done"), 9 * l + 3 + b)
                mm(bank(0, 4, n), C("swap"), cB[:, 0:4, c0:c0 + n], start=True, stop=True).then_inc(S("rt_sw"), 1)
                pe.wait_ge(S("rt_qk"), it)
                for o in range(2):
                    p = slice(64 * o, 64 * o + 64)
                    for t in range(TB):
                        m = mm(B[(1, 5)[o]][0:n, t * P:t * P + n], qk[p, 2 + t, 0:n], qk[p, t, 0:n], start=True, stop=True)
                m.then_inc(S("rt_sc"), 1)
                pe.wait_ge(S("rt_dec"), it)
                for q in range(2):
                    pe.transpose(B[2][0:n, q * P:(q + 1) * P], cB[:, 4 + q, c0:c0 + n], C("ident"))
                for q in range(2):
                    m = pe.transpose(B[2][0:n, (2 + q) * P:(3 + q) * P], qkd[:, 2 + q, 0:n], C("ident"))
                m.then_inc(S("rt_tr"), 1)
                pe.wait_ge(S("rt_tok"), it)
                pe.wait_ge(S("rt_scm"), it)
                if b == 2:
                    pe.wait_ge(S("srt_in"), 16 * (l + 1))
                else:
                    pe.wait_ge(S("zeroed"), l + 1)
                    if b > 0:
                        pe.wait_ge(S("rt_S"), 2 * l + b)
                for h in range(HB):
                    p = slice(64 * (h % 2), 64 * (h % 2) + 64)
                    lo = (h // 2) * P
                    mx(B[3][p, lo:lo + n], vkt[0:n, h // 2, 64 * (h % 2):64 * (h % 2) + 64],
                       rsc[0:n, (h % 2) * TB + h // 2, 0:n], True, b == 2)
                    if b == 2:
                        for s in range(NSEQ):
                            m = mm(B[5][p, lo + s * STEP:lo + (s + 1) * STEP], srt[p, h // 2, s, :],
                                   qkd[p, h // 2, s * STEP:(s + 1) * STEP], start=True, stop=True)
                    else:
                        m = mx(B[3][p, lo:lo + n], srt_p[p, h // 2, :], qkd[p, h // 2, 0:n], False, True)
                m.then_inc(S("rt_o"), 1)
                if b == 2:
                    pe.wait_ge(S("rt_vx"), l + 1)
                for h in range(HB):
                    p = slice(64 * (h % 2), 64 * (h % 2) + 64)
                    kd = vkt[0:n, 2 + h // 2, 64 * (h % 2):64 * (h % 2) + 64]
                    if b == 2:
                        m = mm(B[(4, 1)[h // 2]][p, :], kd, vx[:, h, :, :], start=True, stop=True)
                    else:
                        m = mm(B[4][p, (h // 2) * HD:(h // 2 + 1) * HD], kd,
                               vkt[0:n, h // 2, 64 * (h % 2):64 * (h % 2) + 64], start=True, stop=True)
                m.then_inc(S("rt_dS"), 1)
                pe.wait_ge(S("rt_sq"), it)
                mm(bank(0, 2, n), C("bd"), rsq[:, :, 0:n], start=True, stop=True).then_inc(S("rt_ms"), 1)

            def mamba(l, b):
                it, (c0, n) = 3 * l + b + 1, BLOCKS[b]
                if b == 0:
                    pe.wait_ge(S("mb_dt"), 2 * l + 2)
                pe.wait_ge(S("mix_done"), 9 * l + 6 + b)
                for q, k in enumerate(("dt", "cum", "wk")):
                    m = pe.transpose(B[5][0:n, q * HC:(q + 1) * HC], dd[k][0:HC, c0:c0 + n], C("ident", 0, HC, slice(0, HC)))
                m.then_inc(S("mb_t3"), 1)
                for h in range(HC):
                    m = mm(B[h // 3][:, (h % 3) * P:(h % 3) * P + n], C("sel", h * P, P, slice(0, HC)),
                           dd["cum"][0:HC, c0:c0 + n], start=True, stop=True)
                m.then_inc(S("mb_cb"), 1)
                pe.wait_ge(S("mb_xc"), it)
                for q in range(3):
                    m = pe.transpose(B[2][0:n, q * P:(q + 1) * P], xc[:, q, 0:n], C("ident"))
                for q in range(2):
                    m = pe.transpose(B[3][0:n, q * P:(q + 1) * P], xc[:, 3 + q, 0:n], C("ident"))
                m.then_inc(S("mb_tB"), 1)
                for q in range(2):
                    m = mm(B[4][0:n, q * P:q * P + n], xc[:, 3 + q, 0:n], xc[:, 5 + q, 0:n], start=True, stop=True)
                m.then_inc(S("mb_BC"), 1)
                pe.wait_ge(S("mb_tk3"), it)
                pe.wait_ge(S("mb_xdt"), it)
                pe.wait_ge(S("mb_wts"), it)
                pe.wait_ge(S("mb_cde"), it)
                if b == 2:
                    pe.wait_ge(S("smb_in"), 16 * (l + 1))
                else:
                    pe.wait_ge(S("zeroed"), l + 1)
                    if b > 0:
                        pe.wait_ge(S("mb_S"), 2 * l + b)
                for h in range(HC):
                    p = slice(64 * (h % 2), 64 * (h % 2) + 64)
                    lo = (h // 2) * P
                    mx(B[5][p, lo:lo + n], xdt[0:n, h, :], wts[0:n, h, 0:n], True, False)
                    if b == 2:
                        for s in range(NSEQ):
                            m = mx(B[5][p, lo + s * STEP:lo + (s + 1) * STEP], smb[:, h // 3, s, h % 3, :],
                                   cde[:, h, s * STEP:(s + 1) * STEP], False, s == NSEQ - 1)
                    else:
                        m = mx(B[5][p, lo:lo + n], smb_p[:, h * HD:(h + 1) * HD], cde[:, h, 0:n], False, True)
                m.then_inc(S("mb_y"), 1)
                pe.wait_ge(S("mb_Btk"), it)
                if b == 2:
                    for g in range(2):
                        pe.wait_ge(S("mb_xwe"), 2 * l + g + 1)
                        if g == 1:
                            pe.wait_ge(S("mb_ds_used"), 2 * l + 1)
                        flat = xwe[:, :, :, :].rearrange("p s h d -> p (s h d)")
                        for q in range(3):
                            m = mm(B[q][:, :], Btk[0:n, g, :], flat[:, q * 512:(q + 1) * 512], start=True, stop=True)
                        m.then_inc(S("mb_ds"), 1)
                else:
                    for g in range(2):
                        m = mm(B[0][:, g * 192:(g + 1) * 192], Btk[0:n, g, :], xw[0:n, 3 * g:3 * g + 3, :],
                               start=True, stop=True)
                    m.then_inc(S("mb_dS"), 1)
                pe.wait_ge(S("mb_sq"), it)
                for q in range(3):
                    m = mm(B[4][:, 0:n], C("ones"), ysq[:, q, 0:n], start=(q == 0), stop=(q == 2))
                m.then_inc(S("mb_ms"), 1)

            def ffn(l):
                def body(i, g, e):
                    for f in range(FT):
                        pe.wait_ge(S("gu_free"), e * FT + f + 1)
                        full_slot(g + 2 * f, G_FFN[l] + 2 * f, B[2 * (f % 2)][:, 0:T])
                        full_slot(g + 2 * f + 1, G_FFN[l] + 2 * f + 1, B[2 * (f % 2) + 1][:, 0:T])
                    for m_ in range(KT):
                        pe.wait_ge(S("dn_free"), e * KT + m_ + 5)
                        for f in range(FT):
                            if m_ == 0:
                                pe.wait_ge(S("hid_split"), e * FT + f + 1)
                            j = m_ * FT + f
                            s = 2 * FT + j // KT
                            if j % KT == 0:
                                pe.wait_ge(S("slot_split"), g + s + 1)
                            m = three(B[4 + m_ % 4][:, 0:T], j % KT, G_FFN[l] + s, hidh[:, f, :], hidl[:, f, :],
                                      f == 0, f == FT - 1)
                            if j % KT == KT - 1:
                                m.then_inc(S("slot_used"), 1)
                            elif f == FT - 1:
                                m.then_inc(S("dn"), 1)
                expert_loop(pe, l, body)

            L = DEPTH - 1

            def router():
                full_slot(G_FFN[L] - 1, G_FFN[L] - 1, B[6][:, 0:T])
                pe.wait_ge(S("ro_act"), 1)
                for q, (c0, n) in enumerate(BLOCKS):
                    m = pe.transpose(B[7][0:n, q * NEXP:(q + 1) * NEXP], lg[:, c0:c0 + n],
                                     C("ident", 0, NEXP, slice(0, NEXP)))
                m.then_inc(S("ro_pe"), 1)
                for u in range(6):
                    if u >= 2:
                        pe.wait_ge(S("ro_act"), (2, 3, 5, 6)[u - 2])
                    c0, n = BLOCKS[u // 2]
                    for k in range(KT):
                        m = pe.transpose(B[2 * (u % 2) + k // 4][0:n, (k % 4) * P:(k % 4 + 1) * P],
                                         (hh, hl)[u % 2][:, k, c0:c0 + n].bitcast(F32), C("ident"))
                    m.then_inc(S("ro_pe"), 1)
                pe.wait_ge(S("ro_dve"), 2)
                for q, (c0, n) in enumerate(BLOCKS):
                    m = pe.transpose(B[5][0:NEXP, c0:c0 + n], rt["g"][0:n, q, :], C("ident", 0, n, slice(0, n)))
                m.then_inc(S("ro_pe"), 1)
                pe.wait_ge(S("ro_dve"), 3)
                for q, (c0, n) in enumerate(BLOCKS):
                    pe.transpose(B[7][0:n, q * NEXP:(q + 1) * NEXP], pos1[:, c0:c0 + n],
                                 C("ident", 0, NEXP, slice(0, NEXP)))
                pe.transpose(B[7][0:1, 32:32 + NEXP], upto[:, T - 1:T],
                             C("ident", 0, NEXP, slice(0, NEXP))).then_inc(S("ro_pe"), 1)

            def experts_dense():
                for e in range(NEXP):
                    if e >= 2:
                        pe.wait_ge(S("ro_act"), 9 + e - 1)
                    mm(B[e % 2][:, 0:T], C("sel", e * P, P, slice(0, NEXP)), lg[:, :],
                       start=True, stop=True).then_inc(S("ro_pe"), 1)
                pe.wait_ge(S("ro_act"), 9 + NEXP)

                def body(i, g, e):
                    pe.wait_ge(S("dn_free"), e * KT + KT)
                    for c, (j0, nj, nf) in enumerate(CHUNKS):
                        if c >= 2:
                            pe.wait_ge(S("gu_free"), e * FT + 2 * c)
                        for j in range(j0, j0 + nj):
                            pe.wait_ge(S("slot_split"), g + j + 1)
                            for t in range(2 * nf):
                                out = B[4 * (c % 2) + 2 * (t // nf) + t % nf][:, 0:T]
                                for kk in range(KT // nj):
                                    k = (j - j0) * (KT // nj) + kk
                                    m = three(out, kk * 2 * nf + t, G_FFN[L] + j, hh[:, k, :], hl[:, k, :],
                                              k == 0, k == KT - 1)
                            m.then_inc(S("slot_used"), 1)
                    pe.wait_ge(S("gu_free"), e * FT + FT + 2)
                    for f in range(FT):
                        pe.wait_ge(S("hid_split"), e * FT + f + 1)
                        pe.wait_ge(S("slot_split"), g + 2 * FT + f + 1)
                        for m_ in range(KT):
                            m = three(B[m_][:, 0:T], m_, G_FFN[L] + 2 * FT + f, hidh[:, f, :], hidl[:, f, :],
                                      f == 0, f == FT - 1)
                        m.then_inc(S("slot_used"), 1)
                expert_loop(pe, L, body)

            def gather(i):
                for z, bk in enumerate((6, 2)):
                    for k in range(KT):
                        for q in range(3):
                            rhs = pick[:, i, q, :] if isinstance(i, int) else \
                                pick[:, bass.ds(i, 1), q, :].rearrange("p o c -> p (o c)")
                            m = mm(B[bk + k // 4][:, (k % 4) * P:(k % 4 + 1) * P], htk[z][:, q, k * P:(k + 1) * P],
                                   rhs, start=(q == 0), stop=(q == 2))
                    m.then_inc(S("taken"), 1)

            def experts_picked():
                pe.wait_ge(S("ro_dve"), 5)
                gather(0)
                for e in range(NEXP):
                    for q in range(3):
                        m = mm(B[5][:, e:e + 1], pick[:, e, q, :].bitcast(F32), rt["g"][:, q, e:e + 1],
                               start=(q == 0), stop=(q == 2))
                m.then_inc(S("ro_pe"), 1)
                for e in range(NEXP):
                    if e >= 2:
                        pe.wait_ge(S("ro_dve"), 6 + e - 1)
                    mm(B[e % 2][:, 0:T], C("sel", e * P, P, slice(0, NEXP)), pos1[:, :],
                       start=True, stop=True).then_inc(S("ro_pe"), 1)
                pe.wait_ge(S("ro_dve"), 5 + NEXP)
                pe.wait_ge(S("ro_act"), 10)

                def turn(i, c):
                    pe.wait_ge(S("gu_free"), i * NC + (N_E[0] * FT + 2 + c + 1))
                    if c >= 2:
                        pe.wait_ge(S("hid_split"), i * NC + (N_E[0] * FT + c - 1))
                    for t in range(CHUNKS[c][2]):
                        m = pe.transpose(B[2 + c % 2][:, t * P:(t + 1) * P], hid[:, c % 2, t * P:(t + 1) * P], C("ident"))
                    m.then_inc(S("hid_t"), 1)

                def body(i, g, e):
                    pe.wait_ge(S("taken_hi"), i + 1)
                    pe.wait_ge(S("taken_lo"), i + 1)
                    for c, (j0, nj, nf) in enumerate(CHUNKS):
                        for j in range(j0, j0 + nj):
                            r = G_FFN[L] + j
                            pe.wait_ge(S("slot_split"), g + j + 1)
                            for kk in range(KT // nj):
                                k, cols = (j - j0) * (KT // nj) + kk, slice(kk * 2 * nf * P, (kk + 1) * 2 * nf * P)
                                out = B[c % 2][:, 0:2 * nf * P]
                                mm(out, hh[:, k, 0:P], whi[:, r % HI, cols], start=(k == 0), stop=False)
                                mm(out, hl[:, k, 0:P], whi[:, r % HI, cols], start=False, stop=False)
                                m = mm(out, hh[:, k, 0:P], wlo[:, r % RAW, cols], start=False, stop=(k == KT - 1))
                            m.then_inc(S("slot_used"), 1)
                            if j in TURN:
                                turn(i, TURN[j])
                    pe.wait_ge(S("put_free"), i * 4 + 4)
                    pe.wait_ge(S("dn_free"), i * 4 + KT * (1 + N_E[0]))
                    for f in range(FT):
                        if f % 2 == 0:
                            pe.wait_ge(S("hid_split"), i * NC + (N_E[0] * FT + f // 2 + 1))
                        pe.wait_ge(S("slot_split"), g + 2 * FT + f + 1)
                        r = G_FFN[L] + 2 * FT + f
                        for q, (h_, w_) in enumerate(((hidh, whi[:, r % HI, :]), (hidh, wlo[:, r % RAW, :]),
                                                      (hidl, whi[:, r % HI, :]))):
                            for z in range(2):
                                m = mm(B[4 + z][:, :], h_[:, f, 0:P], w_[:, z * 512:(z + 1) * 512],
                                       start=(f == 0 and q == 0), stop=(f == FT - 1 and q == 2))
                        m.then_inc(S("slot_used"), 1)
                        if 2 * FT + f in TURN:
                            turn(i, TURN[2 * FT + f])
                    gather(i + 1)
                    for m_ in range(KT):
                        if m_ < 2:
                            pe.wait_ge(S("y_lo"), 2 * i + m_ + 1)
                        elif m_ == 2:
                            pe.wait_ge(S("taken_hi"), i + 2)
                        elif m_ in (4, 6):
                            pe.wait_ge(S("put_free"), i * 4 + m_ // 2 + 3)
                        elif m_ in (5, 7):
                            pe.wait_ge(S("dn_free"), i * 4 + (KT * (1 + N_E[0]) + (m_ - 3) // 2))
                        to = place[:, bass.ds(i, 1), :].rearrange("p o t -> p (o t)")
                        mm(B[4 + m_ % 4][:, 0:T], hidh[:, m_, P:2 * P], to, start=True, stop=False)
                        mm(B[4 + m_ % 4][:, 0:T], hidl[:, m_, P:2 * P], to, start=False, stop=True)\
                            .then_inc(S("put"), 1)
                expert_loop(pe, L, body)

            pe.wait_ge(S("const_in"), 16)
            for l in range(DEPTH):
                pe.wait_ge(S("par_in"), 16 * (l + 1))
                norm(2 * l)
                for j in range(WIN):
                    if j >= 2:
                        pe.wait_ge(S("in_read"), WIN * l + j - 1)
                    full_slot(G_IN[l] + j, G_IN[l] + j, B[6 + j % 2][:, 0:T], KT * 2 * l if j == 0 else None)
                for b in range(3):
                    rwkv(l, b)
                for b in range(3):
                    retention(l, b)
                for b in range(3):
                    mamba(l, b)
                pe.wait_ge(S("mix_done"), 9 * (l + 1))
                for j in range(KT):
                    if j >= 2:
                        pe.wait_ge(S("out_read"), KT * l + j - 1)
                    full_slot(G_OUT[l] + j, G_OUT[l] + j, B[6 + j % 2][:, 0:T])
                norm(2 * l + 1)
                pe.wait_ge(S("h_split"), KT * (2 * l + 2))
                if l == DEPTH - 1:
                    router()
                    pe.wait_ge(S("ro_dve"), 4)
                    most = pe.value_load(n_most_i[0:1, 0:1], min_val=0, max_val=T)
                    with pe.If(most <= P):
                        experts_picked()
                    with pe.Else():
                        experts_dense()
                else:
                    ffn(l)
            norm(2 * DEPTH)

        @block.scalar
        def _(act):
            af = act.activation

            def hi(g, ring, rounds):
                act.wait_ge(S(f"slot_in{ring % RAW}"), 16 * rounds)
                if not isinstance(g, int) or g >= HI:
                    act.wait_ge(S("slot_used"), g - HI + 1)
                af(whi[:, ring % HI, :], wraw[:, ring % RAW, :], ACT.Copy).then_inc(S("slot_hi"), 1)

            def hi_ahead(g):
                hi(g + HI, g + HI, (g + HI) // RAW + 1)

            def norm(i):
                for k in range(KT):
                    l = i // 2
                    if i == 0:
                        act.wait_ge(S("x_in"), 16)
                    elif i % 2:
                        act.wait_ge(S("out_read"), KT * l + k + 1)
                    elif i < 2 * DEPTH:
                        act.wait_ge(S("dn_free"), KT + KT * (N_E[0] - 1) + k + 1)
                    if KT * i + k >= 2:
                        act.wait_ge(S("sq_used"), KT * i + k - 1)
                    af(sqb[:, k % 2, :], x[:, k, :], ACT.Square).then_inc(S("sq_ready"), 1)
                act.wait_ge(S("sq_used"), KT * (i + 1))
                af(rstd[:, :], B[0][:, 0:T], ACT.Sqrt, scale=1.0 / D, bias=C("eps", 0, 1)).then_inc(S("nrm_sd"), 1)
                if i == 2 * DEPTH:
                    return
                for k in range(KT):
                    act.wait_ge(S("h_k"), KT * i + k + 1)
                    af(hh[:, k, :], htmp[:, k % 2, :], ACT.Copy).then_inc(S("hh_k"), 1)

            def evac_in(l, j):
                act.wait_ge(S("slot_used"), G_IN[l] + j + 1)
                src = B[6 + j % 2]
                smp = src[:, SEQ:T].rearrange("p (s k) -> p s k", k=STEP)
                if j < A_TILES:
                    af(cR[:, j, 1:EA], src[:, 0:SEQ], ACT.Copy)
                    m = af(cR[:, j, EA:WA_].rearrange("p (s k) -> p s k", k=STEP + 1)[:, :, 1:], smp, ACT.Copy)
                elif j < A_TILES + B_TILES:
                    m = af(cB[:, j - A_TILES, :], src[:, 0:T], ACT.Copy)
                elif j < A_TILES + B_TILES + TC:
                    m = af(cZ[:, j - A_TILES - B_TILES, :], src[:, 0:T], ACT.Copy)
                elif j < WIN - 1:
                    t = j - A_TILES - B_TILES - TC
                    af(cX[:, t, 3:EX], src[:, 0:SEQ], ACT.Copy)
                    m = af(cX[:, t, EX:WX_].rearrange("p (s k) -> p s k", k=STEP + 3)[:, :, 3:], smp, ACT.Copy)
                else:
                    m = af(cD[0:HC, :], src[0:HC, 0:T], ACT.Copy)
                m.then_inc(S("in_read"), 1)

            def rwkv(l, b):
                it, (c0, n) = 3 * l + b + 1, BLOCKS[b]
                nch, cb = chunks(b), 5 * l + 2 * b
                act.wait_ge(S("rw_xm"), it)
                af(tw[0:64, 0:n], Dx[0:64, 9, 0:n], ACT.Tanh)
                af(gs[:, 0:n], Dx[:, 10, 0:n], ACT.Sigmoid).then_inc(S("rw_lora"), 1)
                for q, dst, bias in ((0, "sg", "w0"), (1, "aa", "a0")):
                    act.wait_ge(S("rw_up"), 3 * it - 2 + q)
                    for t in range(TA):
                        m = af(U[dst][:, t, 0:n], B[q][:, t * P:t * P + n], ACT.Sigmoid, bias=V(bias, t))
                    m.then_inc(S("rw_sig"), 1)
                act.wait_ge(S("rw_up"), 3 * it)
                af(U["g"][:, :, 0:n], bank(2, 3, n), ACT.Copy).then_inc(S("rw_sig"), 1)
                act.wait_ge(S("rw_kr"), it)
                af(U["sq"][:, :, 0:n], U["kr"][:, :, 0:n], ACT.Square).then_inc(S("rw_sq"), 1)
                act.wait_ge(S("rw_scan"), it)
                af(U["P"][:, :, 0:n], U["L"][:, :, 0:n], ACT.Exp, scale=-SQE)
                af(U["Pi"][:, :, 0:n], U["L"][:, :, 0:n], ACT.Exp, scale=SQE)
                act.wait_ge(S("rw_lm"), it)
                af(U["Pm"][:, :, 0:n], U["Lm"][:, :, 0:n], ACT.Exp, scale=-SQE).then_inc(S("rw_exp"), 1)
                act.wait_ge(S("rw_ssm"), it)
                af(U["be"][:, :, 0:n], U["be"][:, :, 0:n], ACT.Sqrt).then_inc(S("rw_sd"), 1)
                for q, bk in enumerate((5, 0, 1)):
                    act.wait_ge(S("rw_tr"), 3 * it - 2 + q)
                    af(tok[0:n, q, :, :], bank(bk, 3, P, slice(0, n)), ACT.Copy).then_inc(S("rw_tok"), 1)
                for c in range(nch):
                    r = slice(64 * c, 64 * c + 64)
                    if b == 2:
                        act.wait_ge(S("rw_S0"), l + 1)
                        af(Rs0[:, :, :], b64(0, TA), ACT.Copy).then_inc(S("rw_S0c"), 1)
                    act.wait_ge(S("rw_SA"), cb + c + 1)
                    af(SA[r, :, :], b64(4, HA, r), ACT.Copy).then_inc(S("rw_SAc"), 1)
                act.wait_ge(S("rw_y"), cb + nch)
                af(U["kr"][:, :, 0:n], bank(5, 3, n), ACT.Copy).then_inc(S("rw_y5" if b == 2 else "rw_yc"), 1)
                act.wait_ge(S("rw_yd"), it)
                af(U["sq"][:, :, 0:n], U["kp"][:, :, 0:n], ACT.Square).then_inc(S("rw_ysq"), 1)
                act.wait_ge(S("rw_var"), it)
                af(U["be"][:, :, 0:n], bank(4, 3, n), ACT.Sqrt, scale=1.0 / HD, bias=C("eps", 1, 1)).then_inc(S("rw_ysd"), 1)
                act.wait_ge(S("rw_yf"), it)
                af(hh[:, 0:TA, c0:c0 + n], U["kp"][:, :, 0:n], ACT.Copy).then_inc(S("rw_yh"), 1)

            def retention(l, b):
                it, (c0, n) = 3 * l + b + 1, BLOCKS[b]
                act.wait_ge(S("rt_tr"), it)
                af(vkt[0:n, :, :], bank(2, 4, P, slice(0, n)), ACT.Copy).then_inc(S("rt_tok"), 1)
                act.wait_ge(S("rt_o"), it)
                af(ro[:, :, 0:n], bank(3, 2, n), ACT.Copy).then_inc(S("rt_oc"), 1)
                if b == 2:
                    act.wait_ge(S("rt_o2"), l + 1)
                else:
                    act.wait_ge(S("rt_oc"), it)
                af(rsq[:, :, 0:n], ro[:, :, 0:n], ACT.Square).then_inc(S("rt_sq"), 1)
                af(rsg[:, :, 0:n], cB[:, 6:8, c0:c0 + n], ACT.Silu).then_inc(S("rt_sg"), 1)
                act.wait_ge(S("rt_ms"), it)
                af(rsq[:, :, 0:n], bank(0, 2, n), ACT.Sqrt, scale=1.0 / HD, bias=C("eps", 0, 1)).then_inc(S("rt_sd"), 1)
                act.wait_ge(S("rt_y"), it)
                af(hh[:, TA:TA + TB, c0:c0 + n], ro[:, :, 0:n], ACT.Copy).then_inc(S("rt_yh"), 1)

            def mamba_dt(l):
                r = slice(0, HC)
                act.wait_ge(S("mix_done"), 9 * l + 6)
                act.wait_ge(S("st_out"), 16 * (8 * l + 6))
                af(an[r, :], V("a_log", rows=r), ACT.Exp)
                af(dd["x"][r, :], cD[r, :], ACT.Identity, bias=V("dt_bias", rows=r))
                af(dd["e"][r, :], cD[r, :], ACT.Abs, bias=V("dt_bias", rows=r)).then_inc(S("mb_e"), 1)
                act.wait_ge(S("mb_e"), 3 * l + 1)
                af(dd["e"][r, :], dd["e"][r, :], ACT.Exp, scale=-1.0).then_inc(S("mb_e"), 1)
                act.wait_ge(S("mb_dt"), 2 * l + 1)
                af(dd["wk"][r, :], dd["lm"][r, :], ACT.Exp).then_inc(S("mb_e"), 1)

            def mamba(l, b):
                it, (c0, n) = 3 * l + b + 1, BLOCKS[b]
                act.wait_ge(S("mb_cv"), 4 * it)
                af(xc[:, :, 0:n], xcs[:, :, 0:n], ACT.Silu).then_inc(S("mb_xc"), 1)
                af(zs[:, :, 0:n], cZ[:, :, c0:c0 + n], ACT.Silu).then_inc(S("mb_zs"), 1)
                act.wait_ge(S("mb_t3"), it)
                af(tk3[0:n, :, :], B[5][0:n, 0:3 * HC].rearrange("p (a c) -> p a c", c=HC), ACT.Copy).then_inc(S("mb_tk3"), 1)
                act.wait_ge(S("mb_cb"), it)
                af(ecb[:, 0:3, 0:n], bank(0, 3, n), ACT.Exp)
                af(ecb[:, 3:6, 0:n], bank(1, 3, n), ACT.Exp).then_inc(S("mb_ecb"), 1)
                act.wait_ge(S("mb_seg"), it)
                af(seg[0:n, :, 0:n], seg[0:n, :, 0:n], ACT.Exp).then_inc(S("mb_E"), 1)
                act.wait_ge(S("mb_tB"), it)
                af(Btk[0:n, :, :], bank(3, 2, P, slice(0, n)), ACT.Copy).then_inc(S("mb_Btk"), 1)
                act.wait_ge(S("mb_y2"), it)
                af(ysq[:, :, 0:n], yz[:, :, 0:n], ACT.Square).then_inc(S("mb_sq"), 1)
                act.wait_ge(S("mb_ms"), it)
                af(zs[:, 0, 0:n], B[4][:, 0:n], ACT.Sqrt, scale=1.0 / (HC * HD), bias=C("eps", 2, 1)).then_inc(S("mb_sd"), 1)
                act.wait_ge(S("mb_y3"), it)
                af(hh[:, TA + TB:KT, c0:c0 + n], yz[:, :, 0:n], ACT.Copy).then_inc(S("mb_yh"), 1)

            L = DEPTH - 1

            def next_hi(l, i, g, j):
                r = G_FFN[l] + j + HI
                hi(g + j + HI, r, i * (EXP_SLOTS // RAW) + r // RAW + 1)

            def hidden_hi(f, e):
                act.wait_ge(S("gu_free"), e * FT + f + 3)
                af(hidh[:, f, :], hid[:, f % 2, :], ACT.Copy).then_inc(S("hid_hi"), 1)

            def ffn(l):
                def body(i, g, e):
                    for j in range(EXP_SLOTS):
                        next_hi(l, i, g, j)
                        f = j // 2
                        if j < 2 * FT and j % 2:
                            act.wait_ge(S("slot_used"), g + 2 * f + 1)
                            af(sil[:, f % 2, :], B[2 * (f % 2)][:, 0:T], ACT.Silu).then_inc(S("sil"), 1)
                        elif 0 < j <= 2 * FT:
                            hidden_hi(f - 1, e)
                expert_loop(act, l, body)

            def router():
                act.wait_ge(S("slot_used"), G_FFN[L])
                act.wait_ge(S("st_out"), 16 * 8 * (L + 1))
                af(lg[:, :], B[6][0:NEXP, 0:T], ACT.Copy).then_inc(S("ro_act"), 1)
                for u in range(6):
                    if u == 2:
                        act.wait_ge(S("ro_dve"), 1)
                        af(rt["e"][:, :, :], rt["l"][:, :, :], ACT.Exp).then_inc(S("ro_act"), 1)
                    act.wait_ge(S("ro_pe"), u + 2)
                    n = BLOCKS[u // 2][1]
                    if n < P:
                        af(htk[u % 2][n:P, u // 2, :], cst[n:P, 0:D], ACT.Copy, scale=0.0)
                    for z in range(2):
                        m = af(htk[u % 2][0:n, u // 2, z * 512:(z + 1) * 512], B[2 * (u % 2) + z][0:n, :], ACT.Copy)
                    m.then_inc(S("ro_act"), 1)
                act.wait_ge(S("ro_pe"), 8)
                af(lg[:, :], B[5][0:NEXP, 0:T], ACT.Copy).then_inc(S("ro_act"), 1)

            def experts_dense():
                for e in range(NEXP):
                    act.wait_ge(S("ro_pe"), 9 + e + 1)
                    af(gbc[:, e, :], B[e % 2][:, 0:T], ACT.Copy).then_inc(S("ro_act"), 1)

                def body(i, g, e):
                    for j in range(EXP_SLOTS):
                        next_hi(L, i, g, j)
                        if j in ENDS:
                            c = ENDS[j]
                            act.wait_ge(S("slot_used"), g + j + 1)
                            tiles = range(2 * c, 2 * c + CHUNKS[c][2])
                            for f in tiles:
                                af(sil[:, f % 2, :], B[4 * (c % 2) + f % 2][:, 0:T], ACT.Silu).then_inc(S("sil"), 1)
                            for f in tiles:
                                hidden_hi(f, e)
                expert_loop(act, L, body)
                act.wait_ge(S("yt_free"), KT + KT * NEXP)

            def taken_hi(i):
                act.wait_ge(S("taken"), 2 * i + 1)
                for z in range(2):
                    m = af(hh[:, 4 * z:4 * z + 4, 0:P], bank(6 + z, 4, P), ACT.Copy)
                m.then_inc(S("taken_hi"), 1)

            def experts_picked():
                taken_hi(0)
                act.wait_ge(S("ro_pe"), 10)
                af(slot_gate[:, :], B[5][:, 0:NEXP], ACT.Copy).then_inc(S("ro_act"), 1)
                act.wait_ge(S("ro_act"), 10)

                def gated(i, g):
                    act.wait_ge(S("slot_used"), g + EXP_SLOTS)
                    for z in range(2):
                        af(hidh[:, 4 * z:4 * z + 4, P:2 * P], bank(4 + z, 4, P), ACT.Copy,
                           scale=slot_gate[:, bass.ds(i, 1)]).then_inc(S("y_hi"), 1)

                def body(i, g, e):
                    for j in range(EXP_SLOTS):
                        if j == EXP_SLOTS - 1:
                            gated(i, g)
                        next_hi(L, i, g, j)
                        if j in ENDS:
                            c, n = ENDS[j], CHUNKS[ENDS[j]][2] * P
                            act.wait_ge(S("slot_used"), g + j + 1)
                            af(sil[:, c % 2, 0:n], B[c % 2][:, 0:n], ACT.Silu).then_inc(S("sil"), 1)
                        if j in TURN:
                            c, n = TURN[j], CHUNKS[TURN[j]][2]
                            act.wait_ge(S("hid_t"), i * NC + c + 1)
                            af(hidh[:, 2 * c:2 * c + n, 0:P], bank(2 + c % 2, n, P), ACT.Copy).then_inc(S("hid_hi"), 1)
                    taken_hi(i + 1)
                    for m_ in range(0, KT, 2):
                        act.wait_ge(S("put"), i * KT + m_ + 1)
                        act.wait_ge(S("yt_free"), i * 4 + (KT - 3 + m_ // 2))
                        af(yt[:, m_ // 2, :], B[4 + m_ % 4][:, 0:T], ACT.Copy).then_inc(S("put_free"), 1)
                expert_loop(act, L, body)
                act.wait_ge(S("yt_free"), KT + 4 * NEXP)
                act.wait_ge(S("dn_free"), KT * (1 + N_E[0]) + 4 * NEXP)

            act.dma_start(cst[:, :], consts_in).then_inc(S("const_in"), 16)
            act.wait_ge(S("const_in"), 16)
            for g in range(HI):
                hi(g, g, 1)
            for l in range(DEPTH):
                act.wait_ge(S("par_in"), 16 * (l + 1))
                norm(2 * l)
                for j in range(WIN):
                    hi_ahead(G_IN[l] + j)
                    evac_in(l, j)
                for b in range(3):
                    rwkv(l, b)
                for b in range(3):
                    retention(l, b)
                mamba_dt(l)
                for b in range(3):
                    mamba(l, b)
                for j in range(KT):
                    hi_ahead(G_OUT[l] + j)
                norm(2 * l + 1)
                if l == DEPTH - 1:
                    hi_ahead(G_FFN[l] - 1)
                    router()
                    act.wait_ge(S("ro_dve"), 4)
                    most = act.value_load(n_most_i[0:1, 0:1], min_val=0, max_val=T)
                    with act.If(most <= P):
                        experts_picked()
                    with act.Else():
                        experts_dense()
                else:
                    act.wait_ge(S("st_out"), 16 * 8 * (l + 1))
                    ffn(l)
            norm(2 * DEPTH)

        @block.vector
        def _(v):
            tt, ts, stt, cp = v.tensor_tensor, v.tensor_scalar, v.scalar_tensor_tensor, v.tensor_copy
            own = [0]

            def own_count():
                own[0] += 1
                return own[0]

            def lo(g, ring):
                v.wait_ge(S("slot_hi"), g + 1)
                tt(wlo[:, ring % RAW, :], wraw[:, ring % RAW, :], whi[:, ring % HI, :].bitcast(F32),
                   ALU.subtract).then_inc(S("slot_split"), 1)

            def norm(i):
                v.wait_ge(S("nrm_sd"), i + 1)
                v.reciprocal(rstd[:, :], rstd[:, :]).then_inc(S("v_step"), 1)
                v.wait_ge(S("v_step"), own_count())
                if i == 2 * DEPTH:
                    for k in range(KT):
                        m = stt(x[:, k, :], x[:, k, :], V("g_fin", k), rstd[:, :], ALU.mult, ALU.mult)
                    m.then_inc(S("y_done"), 1)
                    return
                gain = "g_ffn" if i % 2 else "g_mix"

                def scaled(k):
                    stt(htmp[:, k % 2, :], x[:, k, :], V(gain, k), rstd[:, :], ALU.mult, ALU.mult).then_inc(S("h_k"), 1)
                scaled(0)
                scaled(1)
                for k in range(KT):
                    v.wait_ge(S("hh_k"), KT * i + k + 1)
                    tt(hl[:, k, :], htmp[:, k % 2, :], hh[:, k, :].bitcast(F32), ALU.subtract).then_inc(S("h_split"), 1)
                    if k + 2 < KT:
                        if k >= 0:
                            v.wait_ge(S("h_split"), KT * i + k + 1)
                        scaled(k + 2)

            def rwkv(l, b):
                it, (c0, n) = 3 * l + b + 1, BLOCKS[b]
                nch, cb, lv = chunks(b), 5 * l + 2 * b, 15 * l + 6 * b
                nn = nch * CH
                u = {k: t[:, :, 0:n] for k, t in U.items()}
                rr = slice(0, nn)
                if b == 0:
                    v.wait_ge(S("in_read"), WIN * (l + 1))
                    v.wait_ge(S("ext_ready"), l + 1)
                if b < 2:
                    now, prev = cR[:, :, c0 + 1:c0 + 1 + n], cR[:, :, c0:c0 + n]
                    d3 = Dx[:, :, 0:n]
                else:
                    e3 = cR[:, :, EA:WA_].rearrange("p t (s k) -> p t s k", k=STEP + 1)
                    now, prev = e3[:, :, :, 1:], e3[:, :, :, 0:STEP]
                    d3 = Dx[:, :, 0:n].rearrange("p t (s k) -> p t s k", k=STEP)
                tt(d3, prev, now, ALU.subtract).then_inc(S("v_step"), 1)
                v.wait_ge(S("v_step"), own_count())
                for t in range(A_TILES):
                    m = stt(d3[:, t], d3[:, t], V("mu", t), now[:, t], ALU.mult, ALU.add)
                m.then_inc(S("rw_xm"), 1)
                v.wait_ge(S("rw_xm"), it)
                r_, k_, v_ = Dx[:, 0:3, 0:n], Dx[:, 3:6, 0:n], Dx[:, 6:9, 0:n]
                tt(u["kr"], k_, over(V("k_k", 0, 3), n), ALU.mult).then_inc(S("rw_kr"), 1)
                v.wait_ge(S("rw_sig"), 3 * it - 2)
                for t in range(TA):
                    m = v.tensor_tensor_scan(U["L"][:, t, 0:n], C("scan8" if b == 2 else "scan64", 0, n),
                                             U["sg"][:, t, 0:n], 0.0, ALU.mult, ALU.add)
                m.then_inc(S("rw_scan"), 1)
                v.wait_ge(S("rw_scan"), it)
                tt(u["Lm"], u["L"], u["sg"], ALU.subtract).then_inc(S("rw_lm"), 1)
                v.wait_ge(S("rw_sig"), 3 * it - 1)
                stt(u["t1"], u["aa"], -1.0, over(V("k_a", 0, 3), n), ALU.add, ALU.mult).then_inc(S("v_step"), 1)
                v.wait_ge(S("v_step"), own_count())
                stt(u["kp"], u["t1"], 1.0, k_, ALU.add, ALU.mult).then_inc(S("rw_kp"), 1)
                v.wait_ge(S("rw_ss"), it)
                ts(u["be"], bank(3, 3, n), 1e-24, None, ALU.max).then_inc(S("rw_ssm"), 1)
                v.wait_ge(S("rw_sd"), it)
                v.reciprocal(u["be"], u["be"]).then_inc(S("v_step"), 1)
                v.wait_ge(S("v_step"), own_count())
                tt(u["kk"], u["kr"], u["be"], ALU.mult).then_inc(S("v_step"), 1)
                v.wait_ge(S("v_step"), own_count())
                v.wait_ge(S("rw_exp"), it)
                stt(u["al"], u["Pm"], -1.0, u["kk"], ALU.mult, ALU.mult)
                tt(u["be"], u["kk"], u["aa"], ALU.mult).then_inc(S("v_step"), 1)
                v.wait_ge(S("v_step"), own_count())
                tt(u["be"], u["be"], u["Pi"], ALU.mult)
                v.wait_ge(S("rw_kp"), it)
                tt(u["ka"], u["kp"], u["Pi"], ALU.mult)
                tt(u["rho"], u["P"], r_, ALU.mult).then_inc(S("rw_ops"), 1)
                v.wait_ge(S("rw_bsum"), it)
                tt(u["bonus"], bank(4, 3, n), v_, ALU.mult).then_inc(S("rw_bonus"), 1)
                cp(TM[rr, :, :], rep(C("i64", rows=rr), HA))
                cp(TT[rr, :, :], rep(C("i64", rows=rr), HA)).then_inc(S("rw_T"), 1)
                sfx = "8" if b == 2 else ""
                for q, (dst, mask) in enumerate(((AB, "strict"), (C12, "incl"))):
                    for o in range(2):
                        v.wait_ge(S("rw_sc"), 4 * it - 3 + 2 * q + o)
                        m = tt(dst[rr, o, :, :, :].rearrange("p z t c -> p (z t) c"), b64(2 + 2 * q + o, 2 * TA, rr),
                               rep(C(mask + sfx, rows=rr), 2 * TA), ALU.mult)
                    m.then_inc(S(("rw_AT", "rw_C")[q]), 1)
                for q in range(levels(b)):
                    v.wait_ge(S("rw_W"), lv + q + 1)
                    cp(Wm[rr, :, :], b64(0, HA, rr)).then_inc(S("rw_Wc"), 1)
                    v.wait_ge(S("rw_TW"), lv + q + 1)
                    v.wait_ge(S("rw_T"), lv + q + it)
                    for bk, mt, odd in ((1, TM, 0), (2, TT, 1)):
                        got = B[bk][rr, 0:HA * 32].rearrange("p (x s) -> p x s", s=1 << q)
                        part = mt[rr, :, :].rearrange("p h (a o s) -> p (h a) o s", o=2, s=1 << q)[:, :, odd, :]
                        m = tt(part, part, got, ALU.add)
                    m.then_inc(S("rw_T"), 1)
                for c in range(nch):
                    r = slice(64 * c, 64 * c + 64)
                    if b < 2 and c == 0:
                        if b == 0:
                            v.memset(Sbd[:, :, :], 0.0).then_inc(S("rw_Sbd"), 1)
                    v.wait_ge(S("rw_R"), cb + c + 1)
                    cp(Rs[r, :, :], b64(3, HA, r)).then_inc(S("rw_Rc"), 1)
                    if b < 2:
                        v.wait_ge(S("rw_dS"), 4 * l + 2 * b + c + 1)
                        v.wait_ge(S("zeroed"), l + 1)
                        v.wait_ge(S("rw_Sbd"), 5 * l + 2 * b + c + 1)
                        v.wait_ge(S("rw_y"), cb + c + 1)
                        tt(srw_p[:, :, :], srw_p[:, :, :], b64(0, TA), ALU.add).then_inc(S("v_step"), 1)
                        v.wait_ge(S("v_step"), own_count())
                        last = U["P"][:, :, c * CH + CH - 1:c * CH + CH]
                        tt(srw_p[:, :, :], srw_p[:, :, :], last.to_broadcast([P, TA, HD]), ALU.mult).then_inc(S("v_step"), 1)
                        v.wait_ge(S("v_step"), own_count())
                        for o in range(2):
                            p = slice(64 * o, 64 * o + 64)
                            m = cp(Sbd[p, :, 64 * o:64 * o + 64], srw_p[p, :, :])
                        m.then_inc(S("rw_Sbd"), 1)
                if b == 2:
                    v.wait_ge(S("rw_SAc"), cb + 1)
                    for t in range(TA):
                        if t >= 1:
                            v.wait_ge(S("rw_ds"), 3 * l + t)
                        tt(rwx[:, 0, :, :], rep(SA[0:CH, 2 * t:2 * t + 2, :].rearrange("p h c -> p (h c)"), NSEQ),
                           over(C("seq", rows=slice(0, CH)), P), ALU.mult).then_inc(S("rw_xs"), 1)
                    for t in range(TA):
                        v.wait_ge(S("rw_ds"), 3 * l + t + 1)
                        st = srw[:, t, :, :]
                        m = tt(st, st, B[1 + t][:, :].rearrange("p (s c) -> p s c", c=HD), ALU.add)
                        if t == TA - 1:
                            m.then_inc(S("rw_sSa"), 1)
                            v.wait_ge(S("rw_sSa"), l + 1)
                        else:
                            m.then_inc(S("v_step"), 1)
                            v.wait_ge(S("v_step"), own_count())
                        last = U["P"][:, t, STEP - 1:NSEQ * STEP:STEP]
                        tt(st, st, over(last, HD), ALU.mult).then_inc(S("rw_sS"), 1)
                    v.wait_ge(S("rw_y5"), l + 1)
                    tt(u["kr"], u["kr"], bank(0, 3, n), ALU.add).then_inc(S("rw_yc"), 1)
                    v.wait_ge(S("rw_yc"), it)
                v.wait_ge(S("rw_mean"), it)
                stt(u["kp"], bank(3, 3, n), -1.0 / HD, u["kr"], ALU.mult, ALU.add).then_inc(S("rw_yd"), 1)
                v.wait_ge(S("rw_ysd"), it)
                v.reciprocal(u["be"], u["be"]).then_inc(S("v_step"), 1)
                v.wait_ge(S("v_step"), own_count())
                tt(u["kp"], u["kp"], u["be"], ALU.mult).then_inc(S("v_step"), 1)
                v.wait_ge(S("v_step"), own_count())
                for t in range(TA):
                    m = ts(U["kp"][:, t, 0:n], U["kp"][:, t, 0:n], V("ln_w", t), V("ln_b", t), ALU.mult, ALU.add)
                m.then_inc(S("v_step"), 1)
                v.wait_ge(S("v_step"), own_count())
                v.wait_ge(S("rw_bonus"), it)
                tt(u["kp"], u["kp"], u["bonus"], ALU.add).then_inc(S("v_step"), 1)
                v.wait_ge(S("v_step"), own_count())
                v.wait_ge(S("rw_sig"), 3 * it)
                tt(u["kp"], u["kp"], u["g"], ALU.mult).then_inc(S("rw_yf"), 1)
                v.wait_ge(S("rw_yh"), it)
                tt(hl[:, 0:TA, c0:c0 + n], u["kp"], hh[:, 0:TA, c0:c0 + n].bitcast(F32), ALU.subtract)\
                    .then_inc(S("mix_done"), 1)

            def retention(l, b):
                it, (c0, n) = 3 * l + b + 1, BLOCKS[b]
                q_ = qk[:, :, 0:n]
                if b == 0:
                    v.wait_ge(S("st_out"), 16 * (8 * l + 4))
                v.wait_ge(S("rt_sw"), it)
                tt(q_, bank(0, 4, n), rep(C("sin", c0, n), 4), ALU.mult).then_inc(S("v_step"), 1)
                v.wait_ge(S("v_step"), own_count())
                v.wait_ge(S("rt_q2"), it)
                tt(q_, q_, qk2[:, :, 0:n], ALU.add).then_inc(S("v_step"), 1)
                v.wait_ge(S("v_step"), own_count())
                ts(qk[:, 2:4, 0:n], qk[:, 2:4, 0:n], HD ** -0.5, None, ALU.mult).then_inc(S("rt_qk"), 1)
                v.wait_ge(S("rt_qk"), it)
                for q, nm in enumerate(("qdec", "kdec")):
                    dec = C(nm).rearrange("p (t c) -> p t c", c=T)[:, :, c0:c0 + n]
                    m = tt(qkd[:, 2 * q:2 * q + 2, 0:n], qk[:, 2 * q:2 * q + 2, 0:n], dec, ALU.mult)
                m.then_inc(S("rt_dec"), 1)
                v.wait_ge(S("rt_sc"), it)
                mask = C("rmask8" if b == 2 else "rmask", rows=slice(0, n)).rearrange("p (h c) -> p h c", h=HB)
                for o in range(2):
                    hs = slice(o * TB, (o + 1) * TB)
                    m = tt(rsc[0:n, hs, 0:n], bank((1, 5)[o], TB, n, slice(0, n)), mask[:, hs, :], ALU.mult)
                m.then_inc(S("rt_scm"), 1)
                v.wait_ge(S("rt_dS"), it)
                if b < 2:
                    v.wait_ge(S("zeroed"), l + 1)
                    if b > 0:
                        v.wait_ge(S("rt_S"), 2 * l + b)
                for t in range(TB):
                    if b < 2:
                        m = stt(srt_p[:, t, :], srt_p[:, t, :], C("cdec", t, 1), B[4][:, t * HD:(t + 1) * HD],
                                ALU.mult, ALU.add)
                    else:
                        st = srt[:, t, :, :].rearrange("p s c -> p (s c)")
                        m = stt(st, st, C("cdec", TB + t, 1), B[(4, 1)[t]][:, :], ALU.mult, ALU.add)
                m.then_inc(S("rt_S" if b < 2 else "rt_sS"), 1)
                if b == 2:
                    v.wait_ge(S("rt_oc"), it)
                    tt(ro[:, :, 0:n], ro[:, :, 0:n], bank(5, TB, n), ALU.add).then_inc(S("rt_o2"), 1)
                    v.wait_ge(S("rt_o2"), l + 1)
                v.wait_ge(S("rt_sd"), it)
                v.reciprocal(rsq[:, :, 0:n], rsq[:, :, 0:n]).then_inc(S("v_step"), 1)
                v.wait_ge(S("v_step"), own_count())
                v.wait_ge(S("rt_oc"), it)
                for t in range(TB):
                    m = stt(ro[:, t, 0:n], ro[:, t, 0:n], V("ret_norm", t), rsq[:, t, 0:n], ALU.mult, ALU.mult)
                m.then_inc(S("v_step"), 1)
                v.wait_ge(S("v_step"), own_count())
                v.wait_ge(S("rt_sg"), it)
                tt(ro[:, :, 0:n], ro[:, :, 0:n], rsg[:, :, 0:n], ALU.mult).then_inc(S("rt_y"), 1)
                v.wait_ge(S("rt_yh"), it)
                tt(hl[:, TA:TA + TB, c0:c0 + n], ro[:, :, 0:n], hh[:, TA:TA + TB, c0:c0 + n].bitcast(F32),
                   ALU.subtract).then_inc(S("mix_done"), 1)

            def mamba_dt(l):
                r = slice(0, HC)
                d = {k: t[r, :] for k, t in dd.items()}
                coef = [1.0 / k for k in (13, 11, 9, 7, 5, 3)]
                v.wait_ge(S("mb_e"), 3 * l + 2)
                ts(d["z"], d["e"], 2.0, None, ALU.add).then_inc(S("v_step"), 1)
                v.wait_ge(S("v_step"), own_count())
                v.reciprocal(d["z"], d["z"]).then_inc(S("v_step"), 1)
                v.wait_ge(S("v_step"), own_count())
                tt(d["z"], d["z"], d["e"], ALU.mult).then_inc(S("v_step"), 1)
                v.wait_ge(S("v_step"), own_count())
                tt(d["z2"], d["z"], d["z"], ALU.mult).then_inc(S("v_step"), 1)
                v.wait_ge(S("v_step"), own_count())
                ts(d["p"], d["z2"], 1.0 / 15, None, ALU.mult).then_inc(S("v_step"), 1)
                v.wait_ge(S("v_step"), own_count())
                for c in coef:
                    stt(d["p"], d["p"], c, d["z2"], ALU.add, ALU.mult).then_inc(S("v_step"), 1)
                    v.wait_ge(S("v_step"), own_count())
                stt(d["p"], d["p"], 1.0, d["z"], ALU.add, ALU.mult).then_inc(S("v_step"), 1)
                v.wait_ge(S("v_step"), own_count())
                ts(d["x"], d["x"], 0.0, None, ALU.max).then_inc(S("v_step"), 1)
                v.wait_ge(S("v_step"), own_count())
                stt(d["dt"], d["p"], 2.0, d["x"], ALU.mult, ALU.add).then_inc(S("v_step"), 1)
                v.wait_ge(S("v_step"), own_count())
                ts(d["dA"], d["dt"], an[r, :], -1.0, ALU.mult, ALU.mult).then_inc(S("v_step"), 1)
                v.wait_ge(S("v_step"), own_count())
                v.tensor_tensor_scan(d["cum"], C("scanm", rows=r), d["dA"], 0.0, ALU.mult, ALU.add).then_inc(S("v_step"), 1)
                v.wait_ge(S("v_step"), own_count())
                for lo_, n_, k_ in ((0, 2, P), (SEQ, NSEQ, STEP)):
                    c3_ = d["cum"][:, lo_:lo_ + n_ * k_].rearrange("p (a k) -> p a k", k=k_)
                    o3 = d["lm"][:, lo_:lo_ + n_ * k_].rearrange("p (a k) -> p a k", k=k_)
                    m = tt(o3, c3_[:, :, k_ - 1:k_].to_broadcast([HC, n_, k_]), c3_, ALU.subtract)
                m.then_inc(S("mb_dt"), 1)
                v.wait_ge(S("mb_e"), 3 * l + 3)
                tt(d["wk"], d["wk"], d["dt"], ALU.mult).then_inc(S("mb_dt"), 1)

            def mamba(l, b):
                it, (c0, n) = 3 * l + b + 1, BLOCKS[b]
                rn = slice(0, n)
                for j in range(CONV):
                    if j:
                        v.wait_ge(S("mb_cv"), 4 * it - 4 + j)
                    for t in range(XT):
                        if b < 2:
                            src, dst = cX[:, t, c0 + j:c0 + j + n], xcs[:, t, 0:n]
                        else:
                            src = cX[:, t, EX:WX_].rearrange("p (s k) -> p s k", k=STEP + 3)[:, :, j:j + STEP]
                            dst = xcs[:, t, 0:n].rearrange("p (s k) -> p s k", k=STEP)
                        if j == 0:
                            m = ts(dst, src, V("conv_w", t), V("conv_b", t), ALU.mult, ALU.add)
                        else:
                            m = stt(dst, src, V("conv_w", j * XT + t), dst, ALU.mult, ALU.add)
                    m.then_inc(S("mb_cv"), 1)
                v.wait_ge(S("mb_ecb"), it)
                v.wait_ge(S("mb_tk3"), it)
                for h in range(HC):
                    m = ts(seg[rn, h, 0:n], B[h // 3][rn, (h % 3) * P:(h % 3) * P + n], tk3[rn, 1, h:h + 1], 0.0,
                           ALU.subtract, ALU.min)
                m.then_inc(S("mb_seg"), 1)
                v.wait_ge(S("mb_tB"), it)
                xt_ = B[2][rn, 0:HC * HD].rearrange("p (h c) -> p h c", c=HD)
                tt(xdt[rn, :, :], xt_, over(tk3[rn, 0, :], HD), ALU.mult)
                tt(xw[rn, :, :], xt_, over(tk3[rn, 2, :], HD), ALU.mult).then_inc(S("mb_xdt"), 1)
                v.wait_ge(S("mb_BC"), it)
                tt(cbm[rn, :, 0:n], bank(4, 2, n, rn), rep(C("causal8" if b == 2 else "causal", rows=rn), 2),
                   ALU.mult).then_inc(S("v_step"), 1)
                v.wait_ge(S("v_step"), own_count())
                v.wait_ge(S("mb_E"), it)
                for g in range(2):
                    m = tt(wts[rn, 3 * g:3 * g + 3, 0:n], seg[rn, 3 * g:3 * g + 3, 0:n], rep(cbm[rn, g, 0:n], 3), ALU.mult)
                m.then_inc(S("mb_wts"), 1)
                v.wait_ge(S("mb_y"), it)
                v.wait_ge(S("mb_xc"), it)
                for t in range(TC):
                    m = stt(yz[:, t, 0:n], xc[:, t, 0:n], V("d", t), B[5][:, t * P:t * P + n], ALU.mult, ALU.add)
                m.then_inc(S("v_step"), 1)
                v.wait_ge(S("v_step"), own_count())
                v.wait_ge(S("mb_zs"), it)
                tt(yz[:, :, 0:n], yz[:, :, 0:n], zs[:, :, 0:n], ALU.mult).then_inc(S("mb_y2"), 1)
                v.wait_ge(S("mb_ecb"), it)
                if b < 2:
                    v.wait_ge(S("zeroed"), l + 1)
                    if b > 0:
                        v.wait_ge(S("mb_S"), 2 * l + b)
                    st = smb_p[:, :].rearrange("p (h c) -> p h c", c=HD)
                    tt(st, st, ecb[:, :, n - 1:n].to_broadcast([P, HC, HD]), ALU.mult).then_inc(S("v_step"), 1)
                    v.wait_ge(S("v_step"), own_count())
                    v.wait_ge(S("mb_dS"), 2 * l + b + 1)
                    tt(smb_p[:, :], smb_p[:, :], B[0][:, 0:HC * HD], ALU.add).then_inc(S("mb_S"), 1)
                else:
                    for g in range(2):
                        for h in range(3):
                            last = ecb[:, 3 * g + h, STEP - 1:NSEQ * STEP:STEP]
                            st = smb[:, g, :, h, :]
                            m = tt(st, st, over(last, HD), ALU.mult)
                    m.then_inc(S("v_step"), 1)
                    v.wait_ge(S("v_step"), own_count())
                    for g in range(2):
                        v.wait_ge(S("mb_ds"), 2 * l + g + 1)
                        flat = smb[:, g, :, :, :].rearrange("p s h c -> p (s h c)")
                        for q in range(3):
                            f = flat[:, q * 512:(q + 1) * 512]
                            m = tt(f, f, B[q][:, :], ALU.add)
                        m.then_inc(S("mb_ds_used"), 1)
                v.wait_ge(S("mb_sd"), it)
                v.reciprocal(zs[:, 0, 0:n], zs[:, 0, 0:n]).then_inc(S("v_step"), 1)
                v.wait_ge(S("v_step"), own_count())
                v.wait_ge(S("mb_y2"), it)
                for t in range(TC):
                    m = stt(yz[:, t, 0:n], yz[:, t, 0:n], V("ssm_norm", t), zs[:, 0, 0:n], ALU.mult, ALU.mult)
                m.then_inc(S("mb_y3"), 1)
                v.wait_ge(S("mb_yh"), it)
                tt(hl[:, TA + TB:KT, c0:c0 + n], yz[:, :, 0:n], hh[:, TA + TB:KT, c0:c0 + n].bitcast(F32),
                   ALU.subtract).then_inc(S("mix_done"), 1)

            def router():
                v.tensor_tensor_scan(count_up[:, :], C("ones"), C("ones"), 0.0, ALU.mult, ALU.add)
                v.tensor_reduce(slot_no[:, :], C("causal"), AX.X, ALU.add)
                v.memset(rt["pos"][:, :, :], 0.0)
                v.memset(rt["l"][:, :, :], 0.0).then_inc(S("v_step"), 1)
                v.wait_ge(S("v_step"), own_count())
                ts(slot_no[:, :], slot_no[:, :], -1.0, P + 1.0, ALU.mult, ALU.add)
                v.wait_ge(S("ro_pe"), 1)
                for q, (c0, n) in enumerate(BLOCKS):
                    m = cp(rt["l"][0:n, q, :], B[7][0:n, q * NEXP:(q + 1) * NEXP])
                m.then_inc(S("v_step"), 1)
                v.wait_ge(S("v_step"), own_count())
                l_, e_, p_, rk, g_ = (rt[k][:, :, :] for k in ("l", "e", "p", "rank", "g"))
                v.tensor_reduce(rt1[:, :, 0], l_, AX.X, ALU.max).then_inc(S("v_step"), 1)
                v.wait_ge(S("v_step"), own_count())
                tt(l_, l_, over(rt1[:, :, 0], NEXP), ALU.subtract).then_inc(S("ro_dve"), 1)
                v.wait_ge(S("ro_act"), 4)
                v.tensor_reduce(rt1[:, :, 1], e_, AX.X, ALU.add).then_inc(S("v_step"), 1)
                v.wait_ge(S("v_step"), own_count())
                v.reciprocal(rt1[:, :, 1], rt1[:, :, 1]).then_inc(S("v_step"), 1)
                v.wait_ge(S("v_step"), own_count())
                tt(p_, e_, over(rt1[:, :, 1], NEXP), ALU.mult).then_inc(S("v_step"), 1)
                v.wait_ge(S("v_step"), own_count())
                for q in range(3):
                    of_j, of_e = rep(rt["p"][:, q, :], NEXP), over(rt["p"][:, q, :], NEXP)
                    tt(cmp[:, q, :, :], of_j, of_e, ALU.is_gt)
                    m = tt(cmq[:, q, :, :], of_j, of_e, ALU.is_equal)
                m.then_inc(S("v_step"), 1)
                v.wait_ge(S("v_step"), own_count())
                for q in range(3):
                    m = tt(cmq[:, q, :, :], cmq[:, q, :, :], C("before").rearrange("p (e j) -> p e j", j=NEXP), ALU.mult)
                m.then_inc(S("v_step"), 1)
                v.wait_ge(S("v_step"), own_count())
                tt(cmp[:, :, :, :], cmp[:, :, :, :], cmq[:, :, :, :], ALU.add).then_inc(S("v_step"), 1)
                v.wait_ge(S("v_step"), own_count())
                for q in range(3):
                    m = v.tensor_reduce(rt["rank"][:, q, :], cmp[:, q, :, :], AX.X, ALU.add)
                m.then_inc(S("v_step"), 1)
                v.wait_ge(S("v_step"), own_count())
                stt(g_, rk, 1.5, p_, ALU.is_lt, ALU.mult).then_inc(S("v_step"), 1)
                v.wait_ge(S("v_step"), own_count())
                v.tensor_reduce(rt1[:, :, 2], g_, AX.X, ALU.add).then_inc(S("v_step"), 1)
                v.wait_ge(S("v_step"), own_count())
                v.reciprocal(rt1[:, :, 2], rt1[:, :, 2]).then_inc(S("v_step"), 1)
                v.wait_ge(S("v_step"), own_count())
                tt(g_, g_, over(rt1[:, :, 2], NEXP), ALU.mult).then_inc(S("v_step"), 1)
                v.wait_ge(S("v_step"), own_count())
                last = BLOCKS[2][1]
                v.memset(rt["g"][last:P, 2, :], 0.0).then_inc(S("ro_dve"), 1)
                v.wait_ge(S("ro_act"), 9)
                ts(chosen[:, :], lg[:, :], 0.0, None, ALU.is_gt)
                ts(ones8[:, :], lg[:, :], 0.0, None, ALU.is_ge).then_inc(S("v_step"), 1)
                v.wait_ge(S("v_step"), own_count())
                v.tensor_tensor_scan(upto[:, :], ones8[:, :], chosen[:, :], 0.0, ALU.mult, ALU.add).then_inc(S("v_step"), 1)
                v.wait_ge(S("v_step"), own_count())
                tt(pos1[:, :], upto[:, :], chosen[:, :], ALU.mult).then_inc(S("ro_dve"), 1)
                v.wait_ge(S("ro_pe"), 9)
                for q, (c0, n) in enumerate(BLOCKS):
                    cp(rt["pos"][0:n, q, :], B[7][0:n, q * NEXP:(q + 1) * NEXP])
                v.tensor_reduce(n_most[:, 0:1], B[7][0:1, 32:32 + NEXP], AX.X, ALU.max).then_inc(S("v_step"), 1)
                v.wait_ge(S("v_step"), own_count())
                cp(n_most_i[:, :], n_most[:, 0:1]).then_inc(S("ro_dve"), 1)

            L = DEPTH - 1

            def times_up(f, e, bk):
                v.wait_ge(S("sil"), e * FT + f + 1)
                tt(hid[:, f % 2, :], sil[:, f % 2, :], B[bk][:, 0:T], ALU.mult).then_inc(S("gu_free"), 1)

            def hidden_lo(f, e):
                v.wait_ge(S("hid_hi"), e * FT + f + 1)
                tt(hidl[:, f, :], hid[:, f % 2, :], hidh[:, f, :].bitcast(F32), ALU.subtract).then_inc(S("hid_split"), 1)

            def ffn(l):
                ends = {2 * FT + (FT * m_ + FT - 1) // KT: m_ for m_ in range(KT)}

                def body(i, g, e):
                    for j in range(EXP_SLOTS):
                        lo(g + j + HI, G_FFN[l] + j + HI)
                        if j < 2 * FT and j % 2:
                            v.wait_ge(S("slot_used"), g + j + 1)
                            times_up(j // 2, e, 2 * (j // 2 % 2) + 1)
                        elif 0 < j <= 2 * FT:
                            hidden_lo(j // 2 - 1, e)
                        if j in ends:
                            m_ = ends[j]
                            if m_ < KT - 1:
                                v.wait_ge(S("dn"), e * (KT - 1) + m_ + 1)
                            else:
                                v.wait_ge(S("slot_used"), g + EXP_SLOTS)
                            v.wait_ge(S("dn_free"), e * KT + m_ + 1)
                            tt(x[:, m_, :], x[:, m_, :], B[4 + m_ % 4][:, 0:T], ALU.add).then_inc(S("dn_free"), 1)
                expert_loop(v, l, body)

            def experts_dense():
                v.wait_ge(S("ro_act"), 9 + NEXP)

                def body(i, g, e):
                    for j in range(EXP_SLOTS):
                        lo(g + j + HI, G_FFN[L] + j + HI)
                        if j in ENDS:
                            c = ENDS[j]
                            v.wait_ge(S("slot_used"), g + j + 1)
                            tiles = range(2 * c, 2 * c + CHUNKS[c][2])
                            v.wait_ge(S("hid_split"), e * FT + 2 * c)
                            for f in tiles:
                                times_up(f, e, 4 * (c % 2) + 2 + f % 2)
                            for f in tiles:
                                hidden_lo(f, e)
                    v.wait_ge(S("slot_used"), g + EXP_SLOTS)
                    for m_ in range(KT):
                        v.wait_ge(S("yt_free"), i * KT + m_ + KT - YR + 1)
                        gate = gbc[:, bass.ds(i, 1), :].rearrange("p o t -> p (o t)")
                        tt(yt[:, m_ % YR, :], B[m_][:, 0:T], gate, ALU.mult).then_inc(S("dn_free"), 1)
                expert_loop(v, L, body)

            def taken_lo(i):
                v.wait_ge(S("taken"), 2 * i + 2)
                for z in range(2):
                    m = cp(hl[:, 4 * z:4 * z + 4, 0:P], bank(2 + z, 4, P))
                m.then_inc(S("taken_lo"), 1)

            def experts_picked():
                for q in range(3):
                    tt(pick[:, 0:NEXP, q, :], rep(count_up[:, :], NEXP), over(rt["pos"][:, q, :], P), ALU.is_equal)
                    m = ts(pick[:, NEXP, q, :], count_up[:, :], 0.0, None, ALU.mult)
                m.then_inc(S("ro_dve"), 1)
                taken_lo(0)
                for e in range(NEXP):
                    v.wait_ge(S("ro_pe"), 10 + e + 1)
                    ts(place[:, e, :], B[e % 2][:, 0:T], slot_no[:, :], None, ALU.is_equal).then_inc(S("ro_dve"), 1)
                v.wait_ge(S("ro_act"), 10)

                def body(i, g, e):
                    for j in range(EXP_SLOTS):
                        if j == EXP_SLOTS - 1:
                            for z in range(2):
                                v.wait_ge(S("y_hi"), 2 * i + z + 1)
                                stt(hidl[:, 4 * z:4 * z + 4, P:2 * P], bank(4 + z, 4, P), slot_gate[:, bass.ds(i, 1)],
                                    hidh[:, 4 * z:4 * z + 4, P:2 * P].bitcast(F32), ALU.mult, ALU.subtract)\
                                    .then_inc(S("y_lo"), 1)
                        lo(g + j + HI, G_FFN[L] + j + HI)
                        if j in ENDS:
                            c, n = ENDS[j], CHUNKS[ENDS[j]][2] * P
                            v.wait_ge(S("sil"), i * NC + (N_E[0] * FT + c + 1))
                            tt(hid[:, c % 2, 0:n], sil[:, c % 2, 0:n], B[c % 2][:, n:2 * n], ALU.mult)\
                                .then_inc(S("gu_free"), 1)
                        if j in TURN:
                            c, n = TURN[j], CHUNKS[TURN[j]][2]
                            v.wait_ge(S("hid_hi"), i * NC + (N_E[0] * FT + c + 1))
                            tt(hidl[:, 2 * c:2 * c + n, 0:P], bank(2 + c % 2, n, P),
                               hidh[:, 2 * c:2 * c + n, 0:P].bitcast(F32), ALU.subtract).then_inc(S("hid_split"), 1)
                    taken_lo(i + 1)
                    v.wait_ge(S("dn_free"), i * 4 + KT * (1 + N_E[0]))
                    for m_ in range(1, KT, 2):
                        v.wait_ge(S("put"), i * KT + m_ + 1)
                        tt(x[:, m_, :], x[:, m_, :], B[4 + m_ % 4][:, 0:T], ALU.add).then_inc(S("dn_free"), 1)
                expert_loop(v, L, body)

            v.sem_inc(S("gu_free"), 2)
            v.sem_inc(S("dn_free"), KT)
            v.sem_inc(S("put_free"), 4)
            v.wait_ge(S("const_in"), 16)
            for g in range(HI):
                lo(g, g)
            for l in range(DEPTH):
                v.wait_ge(S("par_in"), 16 * (l + 1))
                norm(2 * l)
                for j in range(WIN):
                    lo(G_IN[l] + j + HI, G_IN[l] + j + HI)
                for b in range(3):
                    rwkv(l, b)
                for b in range(3):
                    retention(l, b)
                mamba_dt(l)
                for b in range(3):
                    mamba(l, b)
                for j in range(KT):
                    lo(G_OUT[l] + j + HI, G_OUT[l] + j + HI)
                    v.wait_ge(S("slot_used"), G_OUT[l] + j + 1)
                    tt(x[:, j, :], x[:, j, :], B[6 + j % 2][:, 0:T], ALU.add).then_inc(S("out_read"), 1)
                norm(2 * l + 1)
                v.wait_ge(S("st_out"), 16 * 8 * (l + 1))
                if l == DEPTH - 1:
                    lo(G_FFN[l] - 1 + HI, G_FFN[l] - 1 + HI)
                    router()
                    v.wait_ge(S("ro_dve"), 4)
                    most = v.value_load(n_most_i[0:1, 0:1], min_val=0, max_val=T)
                    with v.If(most <= P):
                        experts_picked()
                    with v.Else():
                        experts_dense()
                else:
                    ffn(l)
            norm(2 * DEPTH)

        @block.gpsimd
        def _(gp):
            tt = gp.tensor_tensor

            def rwkv(l, b):
                it, (c0, n) = 3 * l + b + 1, BLOCKS[b]
                lv, rr = 15 * l + 6 * b, slice(0, chunks(b) * CH)
                gp.wait_ge(S("rw_kp"), it)
                tt(U["br"][:, :, 0:n], Dx[:, 0:3, 0:n], U["kp"][:, :, 0:n], ALU.mult).then_inc(S("rw_rk"), 1)
                gp.wait_ge(S("rw_rk"), it)
                tt(U["br"][:, :, 0:n], U["br"][:, :, 0:n], over(V("r_k", 0, 3), n), ALU.mult).then_inc(S("rw_br"), 1)
                gp.wait_ge(S("rw_AT"), it)
                for q in range(levels(b)):
                    if q >= 2:
                        gp.wait_ge(S("rw_W"), lv + q - 1)
                    m = C("lev").rearrange("p (q c) -> p q c", c=CH)[rr, q, :]
                    for o in range(2):
                        i_ = tt(AL[rr, q % 2, o * TA:(o + 1) * TA, :], AB[rr, o, 0, :, :], rep(m, TA), ALU.mult)
                    i_.then_inc(S("rw_AL"), 1)
                if b == 2:
                    gp.wait_ge(S("rw_tok"), 3 * it - 2)
                    gp.wait_ge(S("rw_SAc"), 5 * (l + 1))
                    for t in range(TA):
                        if t >= 1:
                            gp.wait_ge(S("rw_ds"), 3 * l + t)
                        tt(rwx[:, 1, :, :], rep(tok[0:CH, 0, t, :], NSEQ), over(C("seq", rows=slice(0, CH)), P),
                           ALU.mult).then_inc(S("rw_xv"), 1)

            def retention(l, b):
                it, (c0, n) = 3 * l + b + 1, BLOCKS[b]
                gp.wait_ge(S("mix_done"), 9 * l + 3 + b)
                tt(qk2[:, :, 0:n], cB[:, 0:4, c0:c0 + n], rep(C("cos", c0, n), 4), ALU.mult).then_inc(S("rt_q2"), 1)
                if b == 2:
                    gp.wait_ge(S("rt_tok"), it)
                    vt = vkt[0:CH, 0:2, :].rearrange("p a (h c) -> p (a h) c", c=HD)
                    for h in range(HB):
                        m = tt(vx[:, h, :, :], rep(vt[:, h, :], NSEQ), over(C("seq", rows=slice(0, CH)), HD), ALU.mult)
                    m.then_inc(S("rt_vx"), 1)

            def mamba(l, b):
                it, (c0, n) = 3 * l + b + 1, BLOCKS[b]
                gp.wait_ge(S("mb_ecb"), it)
                gp.wait_ge(S("mb_xc"), it)
                for g in range(2):
                    m = tt(cde[:, 3 * g:3 * g + 3, 0:n], ecb[:, 3 * g:3 * g + 3, 0:n], rep(xc[:, 5 + g, 0:n], 3), ALU.mult)
                m.then_inc(S("mb_cde"), 1)
                if b == 2:
                    gp.wait_ge(S("mb_xdt"), it)
                    for g in range(2):
                        if g:
                            gp.wait_ge(S("mb_ds"), 2 * l + 1)
                        tt(xwe[:, :, :, :].rearrange("p s h c -> p s (h c)"),
                           rep(xw[0:CH, 3 * g:3 * g + 3, :].rearrange("p h c -> p (h c)"), NSEQ),
                           over(C("seq", rows=slice(0, CH)), 3 * HD), ALU.mult).then_inc(S("mb_xwe"), 1)

            def out(dst, src):
                gp.dma_start(dst, src).then_inc(S("st_out"), 16)

            gp.sem_inc(S("yt_free"), KT)
            gp.dma_start(par[:, :], par_in[0]).then_inc(S("par_in"), 16)
            gp.wait_ge(S("const_in"), 16)
            for l in range(DEPTH):
                if l:
                    gp.wait_ge(S("h_split"), KT * 2 * l + 1)
                    gp.wait_ge(S("st_out"), 16 * 8 * l)
                gp.dma_start(sh_in[:, :, :], s_sh[l]).then_inc(S("ends_in"), 16)
                gp.dma_start(cv_in[:, :, :, :], s_cv[l]).then_inc(S("ends_in"), 16)
                gp.dma_start(srw[:, :, :, :], s_rw[l]).then_inc(S("srw_in"), 16)
                gp.memset(srw_p[:, :, :], 0.0)
                gp.memset(srt_p[:, :, :], 0.0)
                gp.memset(smb_p[:, :], 0.0).then_inc(S("zeroed"), 1)
                gp.memset(cR[:, :, 0:1], 0.0)
                gp.memset(cX[:, :, 0:3], 0.0)
                gp.wait_ge(S("ends_in"), 32 * (l + 1))
                rows = cR[:, :, EA:WA_].rearrange("p t (s k) -> p t s k", k=STEP + 1)
                xrows = cX[:, :, EX:WX_].rearrange("p t (s k) -> p t s k", k=STEP + 3)
                gp.tensor_copy(rows[:, :, :, 0], sh_in[:, :, :])
                gp.tensor_copy(xrows[:, :, :, 0:3], cv_in[:, :, :, :]).then_inc(S("ext_ready"), 1)
                gp.wait_ge(S("in_read"), WIN * (l + 1))
                gp.tensor_copy(sh_out[:, :, 0:1], cR[:, :, EA - 1:EA])
                gp.tensor_copy(sh_out[:, :, 1:], rows[:, :, :, STEP])
                gp.tensor_copy(cv_out[:, :, 0, :], cX[:, :, EX - 3:EX])
                gp.tensor_copy(cv_out[:, :, 1:, :], xrows[:, :, :, STEP:]).then_inc(S("ends"), 1)
                gp.wait_ge(S("ends"), l + 1)
                out(o_sh[l], sh_out[:, :, :])
                out(o_cv[l], cv_out[:, :, :, :])
                for b in range(3):
                    rwkv(l, b)
                gp.wait_ge(S("rw_Sbd"), 5 * (l + 1))
                out(p_rw[l], srw_p[:, :, :])
                gp.wait_ge(S("rw_sS"), 3 * (l + 1))
                out(o_rw[l], srw[:, :, :, :])
                gp.wait_ge(S("mix_done"), 9 * l + 3)
                gp.wait_ge(S("st_out"), 16 * (8 * l + 4))
                gp.dma_start(srt[:, :, :, :], s_rt[l]).then_inc(S("srt_in"), 16)
                for b in range(3):
                    retention(l, b)
                gp.wait_ge(S("rt_S"), 2 * (l + 1))
                out(p_rt[l], srt_p[:, :, :])
                gp.wait_ge(S("rt_sS"), l + 1)
                out(o_rt[l], srt[:, :, :, :])
                gp.wait_ge(S("mix_done"), 9 * l + 6)
                gp.wait_ge(S("st_out"), 16 * (8 * l + 6))
                gp.dma_start(smb[:, :, :, :, :], s_mb[l]).then_inc(S("smb_in"), 16)
                for b in range(3):
                    mamba(l, b)
                gp.wait_ge(S("mb_S"), 2 * (l + 1))
                out(p_mb[l], smb_p[:, :])
                gp.wait_ge(S("mb_ds_used"), 2 * (l + 1))
                out(o_mb[l], smb[:, :, :, :, :])
                if l + 1 < DEPTH:
                    gp.wait_ge(S("h_split"), KT * (2 * l + 2))
                    gp.dma_start(par[:, :], par_in[l + 1]).then_inc(S("par_in"), 16)
                else:
                    gp.wait_ge(S("ro_dve"), 4)
                    most = gp.value_load(n_most_i[0:1, 0:1], min_val=0, max_val=T)
                    with gp.If(most <= P):
                        with gp.Fori(0, NEXP) as i:
                            for m_ in range(0, KT, 2):
                                gp.wait_ge(S("put_free"), i * 4 + m_ // 2 + 5)
                                gp.wait_ge(S("yt_free"), i * 4 + (KT - 3 + m_ // 2))
                                tt(x[:, m_, :], x[:, m_, :], yt[:, m_ // 2, :], ALU.add).then_inc(S("yt_free"), 1)
                    with gp.Else():
                        with gp.Fori(0, NEXP) as i:
                            for m_ in range(KT):
                                gp.wait_ge(S("dn_free"), i * KT + (N_E[0] * KT + KT + m_ + 1))
                                gp.wait_ge(S("yt_free"), i * KT + m_ + 1)
                                tt(x[:, m_, :], x[:, m_, :], yt[:, m_ % YR, :], ALU.add).then_inc(S("yt_free"), 1)
            gp.wait_ge(S("st_out"), 16 * 8 * DEPTH)



def tiles_of(m):
    a, b = m.shape
    return m.reshape(a // P, P, b // P, P).transpose(2, 1, 0, 3)


def slots_in(m):
    b = -(-m.shape[1] // P) * P
    pad = np.zeros((m.shape[0], b), m.dtype)
    pad[:, :m.shape[1]] = m
    return tiles_of(pad).reshape(b // P, P, D)


def slots_by_row(wg, wu, wd):
    out = []
    for j, n, nf in CHUNKS:
        c = slice(j * P // 2, j * P // 2 + nf * P)
        m = np.concatenate([wg[:, c], wu[:, c]], 1)
        out.append(m.reshape(n, KT // n, P, 2 * nf * P).transpose(0, 2, 1, 3).reshape(n, P, D))
    return out + [wd.reshape(FT, P, D)]


def slots_expert(wg, wu, wd):
    gu = np.stack([slots_in(wg), slots_in(wu)], 1).reshape(2 * FT, P, D)
    dn = tiles_of(wd).transpose(0, 2, 1, 3).reshape(KT * FT, P, P)
    return [gu, dn.reshape(FT, KT, P, P).transpose(0, 2, 1, 3).reshape(FT, P, D)]


def fm(a, axis=-1):
    return a.reshape(-1, P).T


def kernel(**inputs):
    import concourse.bacc as bacc
    from concourse.bass_utils import run_bass_kernel_spmd

    a = {k: np.asarray(v) for k, v in inputs.items()}
    f32 = np.float32
    xt = np.concatenate([a["x_prompt"].reshape(SEQ, D), a["x_sample"].reshape(NSEQ * STEP, D)], 0)
    x_in = xt.T.reshape(KT, P, T).transpose(1, 0, 2)

    stream = []
    for l in range(DEPTH):
        stream += [slots_in(a["w_in"][l]), slots_in(a["w_out"][l])]
        if l == 0:
            for h in range(2):
                c = slice(h * FE, (h + 1) * FE)
                stream += slots_expert(a["ffn_w_gate"][0][:, c], a["ffn_w_up"][0][:, c], a["ffn_w_down"][0][c])
        else:
            stream.append(slots_in(a["moe_router"][0]))
            for e in range(NEXP):
                stream += slots_by_row(a["moe_w_gate"][0, e], a["moe_w_up"][0, e], a["moe_w_down"][0, e])
    stream.append(np.zeros((N_SLOTS - G_END, P, D), f32))
    w_in = np.concatenate(stream, 0)
    assert w_in.shape[0] == N_SLOTS

    par = np.zeros((DEPTH, P, NPAR), f32)

    def put(name, l, v):
        par[l, :v.shape[0], PAR[name]:PAR[name] + v.shape[1]] = v

    for l in range(DEPTH):
        for name, src in [("g_mix", a["norm_mix"][l]), ("g_ffn", a["norm_ffn"][l]), ("g_fin", a["norm_final"]),
                          ("mu", a["rwkv_mu"][l]), ("w0", a["rwkv_w0"][l]), ("a0", a["rwkv_a0"][l]),
                          ("k_k", a["rwkv_k_k"][l]), ("k_a", a["rwkv_k_a"][l]), ("r_k", a["rwkv_r_k"][l]),
                          ("ln_w", a["rwkv_ln_w"][l]), ("ln_b", a["rwkv_ln_b"][l]), ("ret_norm", a["ret_norm"][l]),
                          ("conv_b", a["ssm_conv_b"][l]), ("ssm_norm", a["ssm_norm"][l]),
                          ("d", np.repeat(a["ssm_d"][l], HD))]:
            put(name, l, fm(src.reshape(-1)))
        put("conv_w", l, np.concatenate([fm(a["ssm_conv_w"][l, j]) for j in range(CONV)], 1))
        put("dt_bias", l, a["ssm_dt_bias"][l][:, None])
        put("a_log", l, a["ssm_a_log"][l][:, None])
        put("wa_up", l, np.concatenate([a["rwkv_w_up"][l], a["rwkv_a_up"][l]], 0))
        put("g_up", l, a["rwkv_g_up"][l])

    rw = a["state_rwkv"].transpose(0, 2, 4, 1, 3).reshape(DEPTH, TA, P, NSEQ, HD).transpose(0, 2, 1, 3, 4)
    rt = a["state_ret"].transpose(0, 2, 3, 1, 4).reshape(DEPTH, TB, P, NSEQ, HD).transpose(0, 2, 1, 3, 4)
    mb = a["state_ssm"].transpose(0, 4, 1, 2, 3).reshape(DEPTH, NST, NSEQ, 2, 3, HD).transpose(0, 1, 3, 2, 4, 5)
    sh = a["state_shift"].transpose(0, 2, 1).reshape(DEPTH, A_TILES, P, NSEQ).transpose(0, 2, 1, 3)
    cv = a["state_conv"].transpose(0, 3, 1, 2).reshape(DEPTH, XT, P, NSEQ, 3).transpose(0, 2, 1, 3, 4)
    ins = [("x", x_in), ("w", w_in), ("consts", constants()[0]), ("par", par), ("s_rwkv", rw), ("s_ret", rt),
           ("s_ssm", mb), ("s_shift", sh), ("s_conv", cv)]
    outs = [("y", (P, KT, T)), ("p_rwkv", (DEPTH, P, TA, HD)), ("p_ret", (DEPTH, P, TB, HD)),
            ("p_ssm", (DEPTH, P, HC * HD)), ("o_rwkv", rw.shape), ("o_ret", rt.shape), ("o_ssm", mb.shape),
            ("o_shift", (DEPTH, P, A_TILES, 1 + NSEQ)), ("o_conv", (DEPTH, P, XT, 1 + NSEQ, 3))]

    nc = bacc.Bacc("TRN2", target_bir_lowering=False, num_devices=1)
    arrays, args = {}, []
    for name, v in ins:
        arrays["in_" + name] = np.ascontiguousarray(v)
        args.append(nc.dram_tensor("in_" + name, v.shape, F32, kind="ExternalInput").ap())
    for name, shape in outs:
        args.append(nc.dram_tensor("out_" + name, shape, F32, kind="ExternalOutput").ap())
    trunk(nc, *args)
    r = run_bass_kernel_spmd(nc, [arrays], core_ids=[0]).results[0]
    y, p_rw, p_rt, p_mb, o_rw, o_rt, o_mb, o_sh, o_cv = (np.asarray(r["out_" + name]) for name, _ in outs)

    y = y.transpose(2, 1, 0).reshape(T, D)

    def heads_rw(s):
        n = s.shape[3]
        return s.transpose(0, 2, 1, 3, 4).reshape(DEPTH, HA, HD, n, HD).transpose(0, 3, 1, 4, 2)

    def heads_rt(s):
        n = s.shape[3]
        return s.transpose(0, 2, 1, 3, 4).reshape(DEPTH, HB, HD, n, HD).transpose(0, 3, 1, 2, 4)

    p_ssm = p_mb.reshape(DEPTH, NST, HC, HD).transpose(0, 2, 3, 1)[:, None]
    s_ssm = o_mb.transpose(0, 3, 2, 4, 5, 1).reshape(DEPTH, NSEQ, HC, HD, NST)
    shift = o_sh.transpose(0, 3, 2, 1).reshape(DEPTH, 1 + NSEQ, COLS_A)
    conv = o_cv.transpose(0, 3, 4, 2, 1).reshape(DEPTH, 1 + NSEQ, 3, CONV_DIM)
    return (y[:SEQ].reshape(1, SEQ, D), y[SEQ:].reshape(NSEQ, STEP, D),
            heads_rw(p_rw[:, :, :, None]), shift[:, :1], heads_rt(p_rt[:, :, :, None]), p_ssm, conv[:, :1],
            heads_rw(o_rw), shift[:, 1:], heads_rt(o_rt), s_ssm, conv[:, 1:])
```

```python
from contextlib import ExitStack

import numpy as np
import concourse.bass as bass
from concourse import mybir

F32 = mybir.dt.float32
F32R = mybir.dt.float32r
ALU = mybir.AluOpType
ACT = mybir.ActivationFunctionType
AX = mybir.AxisListType

P = 128
D = 1024
SEQ = 256
DEPTH = 2
NSEQ = 8
STEP = 8
PAST = 2048
T = SEQ + NSEQ * STEP
KT = D // P
HD = 64
HA, HB, HC = 6, 4, 6
TA, TB, TC = HA // 2, HB // 2, HC // 2
COLS_A = 3 * HA * HD + 256
COLS_B = 4 * HB * HD
NST = 128
CONV = 4
CONV_DIM = HC * HD + 2 * 2 * NST
XT = CONV_DIM // P
FE = 1408
FT = FE // P
NEXP = 8
A_TILES = COLS_A // P
B_TILES = COLS_B // P
C_TILES = TC + XT
WIN = A_TILES + B_TILES + C_TILES + 1
EXP_SLOTS = 3 * FT
CHUNKS = [(4 * c, 4, 2) for c in range(FT // 2)] + [(2 * FT - 2, 2, 1)]
NC = len(CHUNKS)
ENDS = {j + n - 1: c for c, (j, n, _) in enumerate(CHUNKS)}
TURN = {j + n + 1: c for c, (j, n, _) in enumerate(CHUNKS)}
BLOCKS = [(0, 128), (128, 128), (256, 64)]
CH = 64
SQE = float(np.exp(-0.5))
EA, EX = 1 + SEQ, 3 + SEQ
WA_, WX_ = EA + NSEQ * (STEP + 1), EX + NSEQ * (STEP + 3)

RAW, HI = 11, 3
YR = 4
G_IN = [0, WIN + KT + 2 * EXP_SLOTS]
G_OUT = [g + WIN for g in G_IN]
G_FFN = [G_OUT[0] + KT, G_OUT[1] + KT + 1]
N_E = [2, NEXP]
E0 = [0, 2]
G_END = G_FFN[1] + NEXP * EXP_SLOTS
N_SLOTS = G_END + HI

PAR = {}


def _par(name, n, at=[0]):
    PAR[name] = at[0]
    at[0] += n
    return at[0]


for _n, _w in [("g_mix", 8), ("g_ffn", 8), ("g_fin", 8), ("mu", A_TILES), ("w0", 3), ("a0", 3), ("k_k", 3),
               ("k_a", 3), ("r_k", 3), ("ln_w", 3), ("ln_b", 3), ("ret_norm", 2), ("conv_w", 4 * XT),
               ("conv_b", XT), ("d", 3), ("ssm_norm", 3), ("dt_bias", 1), ("a_log", 1),
               ("wa_up", 384), ("g_up", 384)]:
    NPAR = _par(_n, _w)


LEVELS = [6, 6, 3]
CHUNKS_OF = [2, 2, 1]
RW_CH = [8 + 2 * LEVELS[b] for b in range(3)]
RW_END = [RW_CH[b] + 4 * CHUNKS_OF[b] + (b == 2) for b in range(3)]
RW_AT = [sum(RW_END[:b]) + 6 * b for b in range(3)]
RT_AT = [10 * b for b in range(3)]
MB_AT = [30 + 14 * b for b in range(3)]
DENSE, SPARSE = 0.95, 0.55
BG, _at = [], 0.0
for _b in range(3):
    for _s in range(RW_END[_b] + 6):
        while len(BG) <= _at:
            BG.append(RW_AT[_b] + _s)
        _at += DENSE if 9 <= _s < RW_END[_b] else SPARSE
BG += [RW_AT[2] + RW_END[2] + 6] * 99
SHIFT_AT = [0, RW_AT[0] + 12, RW_AT[1] + 12]


def weave(*parts):
    at = [next(p, None) for p in parts]
    while any(a is not None for a in at):
        i = min((a, i) for i, a in enumerate(at) if a is not None)[1]
        at[i] = next(parts[i], None)


def constants():
    i = np.arange(P)
    c = {}
    c["ident"] = np.eye(P)
    c["ones"] = np.ones((P, P))
    c["bd"] = (i[:, None] // HD == i[None, :] // HD) * 1.0
    c["swap"] = (i[:, None] == (i[None, :] ^ 32)) * 1.0
    pos = np.concatenate([np.arange(SEQ), np.tile(PAST + np.arange(STEP), NSEQ)]).astype(np.float32)
    theta = (1.0 / (np.float32(10000.0) ** np.linspace(0.0, 1.0, HD // 2, dtype=np.float32))).astype(np.float32)
    ang = (pos[None, :] * theta[i % 32][:, None]).astype(np.float32).astype(np.float64)
    c["cos"] = np.cos(ang)
    c["sin"] = np.sin(ang) * np.where(i % HD < 32, -1.0, 1.0)[:, None]
    gam = 1.0 - 2.0 ** (-5.0 - np.arange(HB))
    hb = (np.arange(TB)[None, :] * 2 + (i // HD)[:, None])
    g = gam[hb]
    at = np.concatenate([np.arange(SEQ) % P, np.tile(np.arange(STEP), NSEQ)])
    ln = np.concatenate([np.full(SEQ, P), np.full(NSEQ * STEP, STEP)])
    c["qdec"] = g[:, :, None] ** (at + 1)[None, None, :]
    c["kdec"] = g[:, :, None] ** (ln - 1 - at)[None, None, :]
    c["cdec"] = np.stack([g ** P, g ** STEP], 1)
    diff = i[None, :] - i[:, None]
    same8 = i[:, None] // STEP == i[None, :] // STEP
    gam = gam[[0, 2, 1, 3]]
    c["rmask"] = np.where((diff >= 0)[:, None], gam[None, :, None] ** np.maximum(diff, 0)[:, None], 0.0)
    c["rmask8"] = c["rmask"][:, :, :HD] * same8[:, None, :HD]
    c["causal"] = (diff >= 0) * 1.0
    c["causal8"] = ((diff >= 0) & same8)[:, :HD] * 1.0
    j = np.arange(CH)
    s, t = (i % CH)[:, None], j[None, :]
    s8 = s // STEP == t // STEP
    c["strict"], c["incl"] = (s < t) * 1.0, (s <= t) * 1.0
    c["strict8"], c["incl8"] = (s < t) & s8, (s <= t) & s8
    c["i64"] = (s == t) * 1.0
    c["lev"] = np.stack([(s >> (q + 1) == t >> (q + 1)) & (s >> q & 1 == 0) & (t >> q & 1 == 1)
                         for q in range(6)], 1)
    c["scan64"] = np.tile((np.arange(P) % CH != 0) * 1.0, (P, 1))
    c["scan8"] = np.tile((np.arange(CH) % STEP != 0) * 1.0, (P, 1))
    c["scanm"] = np.tile((at != 0) * 1.0, (P, 1))
    c["seq"] = (i[:, None] // STEP == np.arange(NSEQ)[None, :]) * 1.0
    c["sel"] = np.repeat(i[:, None] == np.arange(NEXP)[None, :], P, 1) * 1.0
    c["before"] = np.tile((np.arange(8)[None, :] < np.arange(8)[:, None]).reshape(1, 64), (P, 1)) * 1.0
    c["eps"] = np.tile(np.array([1e-6, 64e-5, 1e-5, 0.0]), (P, 1))
    cols, parts, n = {}, [], 0
    for k, v in c.items():
        v = np.asarray(v, np.float64).reshape(P, -1)
        cols[k] = (n, v.shape[1])
        parts.append(v)
        n += v.shape[1]
    return np.ascontiguousarray(np.concatenate(parts, 1).astype(np.float32)), cols


def trunk(nc, x_in, w_in, consts_in, par_in, s_rw, s_rt, s_mb, s_sh, s_cv,
          y_out, p_rw, p_rt, p_mb, o_rw, o_rt, o_mb, o_sh, o_cv):
    CC = constants()[1]
    NCONST = consts_in.shape[1]
    ctx = ExitStack()
    with ctx:
        sems = {}

        def S(name):
            if name not in sems:
                sems[name] = ctx.enter_context(nc.semaphore(name))
            return sems[name]

        base = (nc.sbuf_base + 63) // 64 * 64
        top = [base]

        def sb(name, shape, dt=F32, offset=None):
            size = int(np.prod(shape[1:])) * 4
            at = top[0] if offset is None else offset
            t = nc.alloc_sbuf_tensor_at(name, shape, dt, offset=at)
            if offset is None:
                top[0] = (at + size + 63) // 64 * 64
            return t

        raw_at = top[0]
        wraw = sb("wraw", [P, RAW, D])
        wlo = sb("wlo", [P, RAW, D], F32R, offset=raw_at)
        whi = sb("whi", [P, HI, D], F32R)
        rings_end = top[0]
        x = sb("x", [P, KT, T])
        hh = sb("hh", [P, KT, T], F32R)
        hl = sb("hl", [P, KT, T], F32R)
        rstd = sb("rstd", [P, T])
        cst = sb("cst", [P, NCONST])
        par = sb("par", [P, NPAR])
        srw_p = sb("srw_p", [P, TA, HD])
        srt_p = sb("srt_p", [P, TB, HD])
        smb_p = sb("smb_p", [P, HC * HD])
        sh_out = sb("sh_out", [P, A_TILES, 1 + NSEQ])
        sh_in = sb("sh_in", [P, A_TILES, NSEQ])
        cv_in = sb("cv_in", [P, XT, NSEQ, 3])
        cv_out = sb("cv_out", [P, XT, 1 + NSEQ, 3])
        area = top[0]
        cR = sb("cR", [P, A_TILES, WA_])
        cB = sb("cB", [P, B_TILES, T])
        cZ = sb("cZ", [P, TC, T])
        cX = sb("cX", [P, XT, WX_])
        cD = sb("cD", [8, T])
        work = top[0]
        srw = sb("srw", [P, TA, NSEQ, HD])
        lent = top[0]
        TM, Wm = (sb(n, [P, HA, CH]) for n in ("TM", "Wm"))
        Sbd = sb("Sbd", [P, TA, P])
        AL = sb("AL", [P, 2, HA, CH])
        tw = sb("tw", [P, P])
        rwx = sb("rwx", [HD, 2, NSEQ, P], offset=lent)
        assert lent + 8 * 1024 == top[0]
        Dx = sb("Dx", [P, A_TILES, P])
        U = {k: sb("u_" + k, [P, TA, P]) for k in
             ("sg", "L", "P", "Pi", "Pm", "aa", "kr", "kp", "t1", "be", "rho", "g")}
        U["Lm"], U["sq"], U["br"], U["ka"] = U["sg"], U["rho"], U["t1"], U["Pi"]
        U["kk"], U["al"], U["bonus"] = U["kr"], U["Pm"], U["L"]
        tok = sb("tok", [P, 3, TA, P])
        AB, C12 = (sb(n, [P, 2, 2, TA, CH]) for n in ("AB", "C12"))
        TT = sb("TT", [P, HA, CH])
        Rs = sb("Rs", [P, HA, CH])
        Rs0 = Rs[:, 0:TA, :]
        SA = U["sg"][:, :, :].rearrange("p t (h c) -> p (t h) c", c=CH)
        rw_end = top[0]
        top[0] = raw_at
        qk = sb("qk", [P, 4, P])
        qk2 = sb("qk2", [P, 4, P])
        qkd = sb("qkd", [P, 4, P])
        rsc = sb("rsc", [P, HB, P])
        vkt = sb("vkt", [P, 4, P])
        vx = sb("vx", [HD, HB, NSEQ, HD])
        ro = sb("ro", [P, TB, P])
        rsq = sb("rsq", [P, TB, P])
        rsg = sb("rsg", [P, TB, P])
        srt = sb("srt", [P, TB, NSEQ, HD])
        rt_end = top[0]
        top[0] = raw_at
        xc = sb("xc", [P, XT, P])
        xwe = sb("xwe", [HD, NSEQ, 3, HD])
        xcs = sb("xcs", [P, XT, P], offset=top[0] - NSEQ * 3 * HD * 4)
        tk3 = sb("tk3", [P, 3, HC])
        ecb = sb("ecb", [P, HC, P])
        seg = sb("seg", [P, HC, P])
        xdt = sb("xdt", [P, HC, HD])
        xw = sb("xw", [P, HC, HD])
        Btk = sb("Btk", [P, 2, P])
        cbm = sb("cbm", [P, 2, P])
        wts = sb("wts", [P, HC, P])
        cde = sb("cde", [P, HC, P])
        yz = sb("yz", [P, TC, P])
        ysq = sb("ysq", [P, TC, P])
        zs = sb("zs", [P, TC, P])
        assert top[0] >= rt_end
        smb = sb("smb", [P, 2, NSEQ, 3, HD])
        dd = {k: sb("d_" + k, [8, T]) for k in ("x", "e", "z", "z2", "p", "dt")}
        dd["dA"], dd["cum"], dd["lm"], dd["wk"] = dd["z"], dd["p"], dd["z2"], dd["e"]
        an = sb("an", [8, 1])
        gs = sb("gs", [P, P])
        assert top[0] <= rings_end
        mix_end = rw_end
        htmp = sb("htmp", [P, 2, T], offset=mix_end - 4 * T * 4)
        sqb = sb("sqb", [P, 2, T], offset=mix_end - 2 * T * 4)
        top[0] = area
        hidh = sb("hidh", [P, FT, T], F32R)
        hidl = sb("hidl", [P, FT, T], F32R)
        sil_at = top[0]
        sil = sb("sil", [P, 2, T])
        hid = sb("hid", [P, 2, T])
        yt_at = top[0]
        yt = sb("yt", [P, YR, T])
        gbc = sb("gbc", [P, NEXP, T])
        place = sb("place", [P, NEXP, T], F32R, offset=top[0] - NEXP * T * 4)
        lg = sb("lg", [NEXP, T])
        rt = {k: sb("rt_" + k, [P, 3, NEXP]) for k in ("l", "e", "p", "rank", "g", "pos")}
        rt1 = sb("rt1", [P, 3, 4])
        slot_no = sb("slot_no", [P, 1])
        slot_gate = sb("slot_gate", [P, NEXP])
        n_most = sb("n_most", [1, 2])
        n_most_i = sb("n_most_i", [1, 1], mybir.dt.int32)
        count_up = sb("count_up", [P, P])
        htk = [sb("htk_" + k, [P, 3, D], F32R) for k in "hl"]
        pick = sb("pick", [P, NEXP + 1, 3, P], F32R)
        exp_end, top[0] = top[0], sil_at
        chosen, ones8, upto, pos1 = (sb(k, [NEXP, T]) for k in ("chosen", "ones8", "upto", "pos1"))
        assert top[0] <= yt_at
        top[0] = yt_at
        cmp = sb("cmp", [P, 3, NEXP, NEXP])
        cmq = sb("cmq", [P, 3, NEXP, NEXP])
        top[0] = exp_end
        assert max(mix_end, top[0]) <= nc.sbuf_usable_end, (mix_end, top[0], nc.sbuf_usable_end)

        B = [ctx.enter_context(nc.psum_tensor(f"bank{i}", [P, 512], F32)) for i in range(8)]

        def C(name, lo=0, n=None, rows=slice(0, P)):
            at, w = CC[name]
            return cst[rows, at + lo:at + (w if n is None else lo + n)]

        def V(name, i=0, n=1, rows=slice(0, P)):
            return par[rows, PAR[name] + i:PAR[name] + i + n]

        def over(ap, n):
            return ap.unsqueeze(2).to_broadcast([ap.shape[0], ap.shape[1], n])

        def rep(ap, n):
            return ap.unsqueeze(1).to_broadcast([ap.shape[0], n, ap.shape[1]])

        def bank(b, n_tiles, n, rows=slice(0, P)):
            return B[b][rows, 0:n_tiles * P].rearrange("p (a c) -> p a c", c=P)[:, :, 0:n]

        def b64(b, k, rows=slice(0, P)):
            return B[b][rows, 0:k * HD].rearrange("p (a c) -> p a c", c=HD)

        def halves(ap, q, odd):
            return ap.rearrange("p h (a o s) -> p h a o s", o=2, s=1 << q)[:, :, :, odd, :]

        def half1(ap, q, odd):
            return ap.rearrange("p (a o s) -> p a o s", o=2, s=1 << q)[:, :, odd, :]

        def c3(ap, q):
            return ap.rearrange("p h (a s) -> p h a s", s=1 << q)

        def ho(h):
            return (h % 2) * TA + h // 2

        def levels(b):
            return LEVELS[b]

        def chunks(b):
            return CHUNKS_OF[b]

        def expert_loop(eng, l, body):
            with eng.Fori(0, N_E[l]) as i:
                body(i, i * EXP_SLOTS + G_FFN[l], i + E0[l])

        block = ctx.enter_context(nc.Block())

        @block.sync
        def _(sp):
            def slot(g, ring):
                if not isinstance(g, int) or g >= RAW:
                    sp.wait_ge(S("slot_used"), g - RAW + 1)
                if isinstance(g, int):
                    sp.dma_start(wraw[:, ring % RAW, :], w_in[g, :, :]).then_inc(S(f"slot_in{ring % RAW}"), 16)
                else:
                    src = w_in[bass.ds(g, 1), :, :].rearrange("o p c -> (o p) c")
                    sp.dma_start(wraw[:, ring % RAW, :], src).then_inc(S(f"slot_in{ring % RAW}"), 16)

            sp.dma_start(x[:, :, :], x_in).then_inc(S("x_in"), 16)
            slot(0, 0)
            for l in range(DEPTH):
                for g in range(G_IN[l], G_FFN[l]):
                    if g == G_OUT[l]:
                        sp.wait_ge(S("rings_free"), l + 1)
                    if g == HI:
                        sp.wait_ge(S("const_in"), 16)
                    if g > 0:
                        slot(g, g)

                def body(i, g, e):
                    for j in range(EXP_SLOTS):
                        slot(g + j, G_FFN[l] + j)
                expert_loop(sp, l, body)
            for g in range(G_END, N_SLOTS):
                slot(g, g)
            sp.wait_ge(S("y_done"), 1)
            sp.dma_start(y_out, x[:, :, :]).then_inc(S("y_out"), 16)
            sp.wait_ge(S("y_out"), 16)

        @block.tensor
        def _(pe):
            mm = pe.matmul

            def mx(out, lhsT, rhs, start, stop):
                return pe.matmul(out, lhsT, rhs, start=start, stop=stop, skip_group_check=True)

            def three(out, k, slot_ring, rh, rl, first, last):
                hi = whi[:, slot_ring % HI, k * P:(k + 1) * P]
                lo = wlo[:, slot_ring % RAW, k * P:(k + 1) * P]
                mm(out, hi, rh, start=first, stop=False)
                mm(out, hi, rl, start=False, stop=False)
                return mm(out, lo, rh, start=False, stop=last)

            def full_slot(g, ring, out, h_from=None):
                pe.wait_ge(S("slot_split"), g + 1)
                for k in range(KT):
                    if h_from is not None:
                        pe.wait_ge(S("h_split"), h_from + k + 1)
                    m = three(out, k, ring, hh[:, k, :], hl[:, k, :], k == 0, k == KT - 1)
                m.then_inc(S("slot_used"), 1)

            def norm(i, tiles=range(KT)):
                for k in tiles:
                    pe.wait_ge(S("sq_ready"), KT * i + k + 1)
                    m = mm(B[0][:, 0:T], C("ones"), sqb[:, k % 2, :], start=(k == 0), stop=(k == KT - 1))
                    m.then_inc(S("sq_used"), 1)

            def shift(l):
                for b in range(3):
                    it, n = 3 * l + b + 1, BLOCKS[b][1]
                    yield RW_AT[b] - 3 if b else 2
                    pe.wait_ge(S("rw_lora"), it)
                    if b > 0:
                        pe.wait_ge(S("rw_Sbd"), 5 * l + 2 * b + 1)
                    for q, (rows, src, name) in enumerate([(slice(0, 64), tw[0:64, 0:n], "wa_up"),
                                                           (slice(64, P), Dx[64:P, 9, 0:n], "wa_up"),
                                                           (slice(0, P), gs[:, 0:n], "g_up")]):
                        for t in range(TA):
                            m = mm(B[q][:, t * P:t * P + n], V(name, t * P, P, rows), src, start=True, stop=True)
                        m.then_inc(S("rw_up"), 1)

            def rwkv(l, b):
                it, n = 3 * l + b + 1, BLOCKS[b][1]
                nch, cb, lv, s0 = chunks(b), 5 * l + 2 * b, 15 * l + 6 * b, RW_AT[b]
                lw = 12 * l + 5 * b
                yield s0 + 3
                pe.wait_ge(S("rw_sq"), it)
                mm(bank(3, 3, n), C("bd"), U["sq"][:, :, 0:n], start=True, stop=True).then_inc(S("rw_ss"), 1)
                yield s0 + 4
                pe.wait_ge(S("rw_br"), it)
                mm(bank(4, 3, n), C("bd"), U["br"][:, :, 0:n], start=True, stop=True).then_inc(S("rw_bsum"), 1)
                yield s0 + 6
                pe.wait_ge(S("rw_ops"), it)
                pe.wait_ge(S("rw_sig"), 3 * it)
                for q, (bk, src) in enumerate([(5, Dx[:, 6:9, 0:n]), (0, U["be"][:, :, 0:n]), (1, U["ka"][:, :, 0:n])]):
                    for t in range(TA):
                        m = pe.transpose(B[bk][0:n, t * P:(t + 1) * P], src[:, t, :], C("ident"))
                    m.then_inc(S("rw_tr"), 1)
                pe.wait_ge(S("rw_ssm"), it)
                for q, bk in ((0, 2), (1, 4)):
                    if q == 1:
                        pe.wait_ge(S("rw_bonus"), it)
                        pe.wait_ge(S("rw_tok"), 3 * it)
                    for par_ in range(2):
                        r = slice(64 * par_, 64 * par_ + 64)
                        for z, lh in enumerate(("be", "ka")):
                            for t in range(TA):
                                for c in range(nch):
                                    lo = (z * TA + t) * CH
                                    m = mm(B[bk + par_][64 * c:64 * c + 64, lo:lo + CH],
                                           U[lh][r, t, c * CH:(c + 1) * CH],
                                           U[("al", "rho")[q]][r, t, c * CH:(c + 1) * CH], start=True, stop=True)
                        m.then_inc(S("rw_sc"), 1)
                yield s0 + 9
                pe.wait_ge(S("rw_AL"), lv + 1)
                for h in range(HA):
                    for c in range(nch):
                        r = slice(64 * c, 64 * c + 64)
                        m = mm(B[0][r, h * CH:(h + 1) * CH], AL[r, 0, h, :], C("i64", rows=r), start=True, stop=True)
                m.then_inc(S("rw_W"), 1)
                for q in range(1, levels(b)):
                    yield s0 + 8 + 2 * q
                    pe.wait_ge(S("rw_T"), lv + q)
                    pe.wait_ge(S("rw_AL"), lv + q + 1)
                    for h in range(HA):
                        for c in range(nch):
                            r = slice(64 * c, 64 * c + 64)
                            m = mm(B[0][r, h * CH:(h + 1) * CH], AL[r, q % 2, h, :], TM[r, h, :], start=True, stop=True)
                    m.then_inc(S("rw_W"), 1)
                    yield s0 + 9 + 2 * q
                    pe.wait_ge(S("rw_Wc"), lw + q)
                    if q == 1:
                        pe.wait_ge(S("rw_AT"), it)
                    for bk, odd in ((1, 0), (2, 1)):
                        for h in range(HA):
                            for c in range(nch):
                                r = slice(64 * c, 64 * c + 64)
                                out = B[bk][r, h * 32:(h + 1) * 32]
                                if odd:
                                    m = mm(out, Wm[r, h, :], half1(TT[r, h, :], q, 1), start=True, stop=True)
                                else:
                                    m = mm(out, TT[r, h, :], half1(Wm[r, h, :], q, 0), start=True, stop=True)
                    m.then_inc(S("rw_TW"), 1)
                yield s0 + RW_CH[b]
                pe.wait_ge(S("rw_T"), lv + levels(b))
                pe.wait_ge(S("rw_C"), it)
                for c in range(nch):
                    yield s0 + RW_CH[b] + 4 * c
                    r = slice(64 * c, 64 * c + 64)
                    cs = slice(c * CH, (c + 1) * CH)
                    vt, bt, kt = (tok[r, q, :, :].rearrange("p a c -> p (a c)") for q in range(3))
                    if b == 2:
                        pe.wait_ge(S("srw_in"), 16 * (l + 1))
                        for h in range(HA):
                            p = slice(64 * (h % 2), 64 * (h % 2) + 64)
                            for s in range(NSEQ):
                                m = mm(B[0][p, (h // 2) * CH + s * STEP:(h // 2) * CH + (s + 1) * STEP],
                                       srw[p, h // 2, s, :], U["al"][p, h // 2, s * STEP:(s + 1) * STEP],
                                       start=True, stop=True)
                        m.then_inc(S("rw_S0"), 1)
                        pe.wait_ge(S("rw_S0c"), l + 1)
                    else:
                        pe.wait_ge(S("rw_Sbd"), 5 * l + 2 * b + c + 1)
                    for t in range(TA):
                        pair = B[3][r, t * P:(t + 1) * P]
                        for o in range(2):
                            hs = slice(t * P + o * HD, t * P + (o + 1) * HD)
                            mx(B[3][r, hs], AB[r, o, 1, t, :], vt[:, hs], o == 0, False)
                        if b == 2:
                            m = mx(pair, Rs0[:, t, :], C("ident"), False, True)
                        else:
                            m = mx(pair, U["al"][:, t, cs], Sbd[:, t, :], False, True)
                    m.then_inc(S("rw_R"), 1)
                    yield s0 + RW_CH[b] + 4 * c + 1
                    pe.wait_ge(S("rw_Rc"), cb + c + 1)
                    for h in range(HA):
                        m = mm(B[4][r, h * HD:(h + 1) * HD], TT[r, ho(h), :], Rs[r, h, :], start=True, stop=True)
                    m.then_inc(S("rw_SA"), 1)
                    yield s0 + RW_CH[b] + 4 * c + 2
                    pe.wait_ge(S("rw_SAc"), cb + c + 1)
                    if b < 2:
                        for h in range(HA):
                            p = slice(64 * (h % 2), 64 * (h % 2) + 64)
                            out = B[0][p, (h // 2) * HD:(h // 2 + 1) * HD]
                            hs = slice(h * HD, (h + 1) * HD)
                            mx(out, bt[:, hs], SA[r, h, :], True, False)
                            m = mx(out, kt[:, hs], vt[:, hs], False, True)
                        m.then_inc(S("rw_dS"), 1)
                    yield s0 + RW_CH[b] + 4 * c + 3
                    for h in range(HA):
                        p = slice(64 * (h % 2), 64 * (h % 2) + 64)
                        lo = (h // 2) * P + c * CH
                        out = B[5][p, lo:lo + CH]
                        mx(out, SA[r, h, :], C12[r, h % 2, 0, h // 2, :], True, False)
                        m = mx(out, vt[:, h * HD:(h + 1) * HD], C12[r, h % 2, 1, h // 2, :], False, b == 2)
                        if b == 2:
                            for s in range(NSEQ):
                                t8 = slice(s * STEP, (s + 1) * STEP)
                                m = mm(B[0][p, (h // 2) * P + s * STEP:(h // 2) * P + (s + 1) * STEP], srw[p, h // 2, s, :],
                                       U["rho"][p, h // 2, t8], start=True, stop=True)
                        elif h % 2:
                            m = mx(B[5][:, lo:lo + CH], Sbd[:, h // 2, :], U["rho"][:, h // 2, cs], False, True)
                    m.then_inc(S("rw_y"), 1)
                if b == 2:
                    yield s0 + RW_END[b] - 1
                    for t in range(TA):
                        pe.wait_ge(S("rw_xs"), 3 * l + t + 1)
                        pe.wait_ge(S("rw_xv"), 3 * l + t + 1)
                        for h in (2 * t, 2 * t + 1):
                            p = slice(64 * (h % 2), 64 * (h % 2) + 64)
                            o = slice((h % 2) * HD, (h % 2) * HD + HD)
                            hs = slice(h * HD, (h + 1) * HD)
                            mx(B[1 + t][p, :], bt[:, hs], rwx[:, 0, :, o], True, False)
                            m = mx(B[1 + t][p, :], kt[:, hs], rwx[:, 1, :, o], False, True)
                        m.then_inc(S("rw_ds"), 1)
                yield s0 + RW_END[b]
                pe.wait_ge(S("rw_yc"), it)
                if b == 2:
                    pe.wait_ge(S("rw_sSa"), l + 1)
                mm(bank(3, 3, n), C("bd"), U["kr"][:, :, 0:n], start=True, stop=True).then_inc(S("rw_mean"), 1)
                yield s0 + RW_END[b] + 2
                pe.wait_ge(S("rw_ysq"), it)
                mm(bank(4, 3, n), C("bd"), U["sq"][:, :, 0:n], start=True, stop=True).then_inc(S("rw_var"), 1)

            def retention(l, b):
                it, (c0, n), s0 = 3 * l + b + 1, BLOCKS[b], RT_AT[b]
                yield BG[s0]
                if b == 0:
                    pe.wait_ge(S("in_read"), WIN * (l + 1))
                else:
                    pe.wait_ge(S("mix_done"), 6 * l + b)
                mm(bank(6, 4, n), C("swap"), cB[:, 0:4, c0:c0 + n], start=True, stop=True).then_inc(S("rt_sw"), 1)
                yield BG[s0 + 2]
                pe.wait_ge(S("rt_qk"), it)
                for o in range(2):
                    p = slice(64 * o, 64 * o + 64)
                    for t in range(TB):
                        m = mm(B[6 + o][0:n, t * P:t * P + n], qk[p, 2 + t, 0:n], qk[p, t, 0:n], start=True, stop=True)
                m.then_inc(S("rt_sc"), 1)
                yield BG[s0 + 4]
                pe.wait_ge(S("rt_dec"), it)
                pe.wait_ge(S("rt_scm"), it)
                for q in range(2):
                    pe.transpose(B[6][0:n, q * P:(q + 1) * P], cB[:, 4 + q, c0:c0 + n], C("ident"))
                for q in range(2):
                    m = pe.transpose(B[6][0:n, (2 + q) * P:(3 + q) * P], qkd[:, 2 + q, 0:n], C("ident"))
                m.then_inc(S("rt_tr"), 1)
                yield BG[s0 + 5]
                pe.wait_ge(S("rt_tok"), it)
                if b == 2:
                    pe.wait_ge(S("srt_in"), 16 * (l + 1))
                else:
                    pe.wait_ge(S("zeroed"), l + 1)
                    if b > 0:
                        pe.wait_ge(S("rt_S"), 3 * l + b)
                for h in range(HB):
                    p = slice(64 * (h % 2), 64 * (h % 2) + 64)
                    lo = (h // 2) * P
                    mx(B[7][p, lo:lo + n], vkt[0:n, h // 2, 64 * (h % 2):64 * (h % 2) + 64],
                       rsc[0:n, (h % 2) * TB + h // 2, 0:n], True, b == 2)
                    if b == 2:
                        for s in range(NSEQ):
                            m = mm(B[6][p, lo + s * STEP:lo + (s + 1) * STEP], srt[p, h // 2, s, :],
                                   qkd[p, h // 2, s * STEP:(s + 1) * STEP], start=True, stop=True)
                    else:
                        m = mx(B[7][p, lo:lo + n], srt_p[p, h // 2, :], qkd[p, h // 2, 0:n], False, True)
                m.then_inc(S("rt_o"), 1)
                yield BG[s0 + 6]
                if b == 2:
                    pe.wait_ge(S("rt_vx"), l + 1)
                    pe.wait_ge(S("rt_o2"), l + 1)
                for h in range(HB):
                    p = slice(64 * (h % 2), 64 * (h % 2) + 64)
                    kd = vkt[0:n, 2 + h // 2, 64 * (h % 2):64 * (h % 2) + 64]
                    if b == 2:
                        m = mm(B[6 + h // 2][p, :], kd, vx[:, h, :, :], start=True, stop=True)
                    else:
                        m = mm(B[6][p, (h // 2) * HD:(h // 2 + 1) * HD], kd,
                               vkt[0:n, h // 2, 64 * (h % 2):64 * (h % 2) + 64], start=True, stop=True)
                m.then_inc(S("rt_dS"), 1)
                yield BG[s0 + 7]
                pe.wait_ge(S("rt_sq"), it)
                if b == 2:
                    pe.wait_ge(S("rt_S"), 3 * (l + 1))
                mm(bank(7, 2, n), C("bd"), rsq[:, :, 0:n], start=True, stop=True).then_inc(S("rt_ms"), 1)

            def mamba(l, b):
                it, (c0, n), s0 = 3 * l + b + 1, BLOCKS[b], MB_AT[b]
                yield BG[s0 + 1]
                if b == 0:
                    pe.wait_ge(S("mb_dt"), 2 * l + 2)
                pe.wait_ge(S("mix_done"), 6 * l + 3 + b)
                for q, k in enumerate(("dt", "cum", "wk")):
                    m = pe.transpose(B[6][0:n, q * HC:(q + 1) * HC], dd[k][0:HC, c0:c0 + n], C("ident", 0, HC, slice(0, HC)))
                m.then_inc(S("mb_t3"), 1)
                yield BG[s0 + 2]
                pe.wait_ge(S("mb_tk3"), it)
                for h in range(HC):
                    m = mm(B[7 - h // 3][:, (h % 3) * P:(h % 3) * P + n], C("sel", h * P, P, slice(0, HC)),
                           dd["cum"][0:HC, c0:c0 + n], start=True, stop=True)
                m.then_inc(S("mb_cb"), 1)
                yield BG[s0 + 5]
                pe.wait_ge(S("mb_xc"), it)
                pe.wait_ge(S("mb_seg"), it)
                for q in range(3):
                    m = pe.transpose(B[6][0:n, q * P:(q + 1) * P], xc[:, q, 0:n], C("ident"))
                for q in range(2):
                    m = pe.transpose(B[7][0:n, q * P:(q + 1) * P], xc[:, 3 + q, 0:n], C("ident"))
                m.then_inc(S("mb_tB"), 1)
                yield BG[s0 + 7]
                pe.wait_ge(S("mb_Btk"), it)
                for q in range(2):
                    m = mm(B[7][0:n, q * P:q * P + n], xc[:, 3 + q, 0:n], xc[:, 5 + q, 0:n], start=True, stop=True)
                m.then_inc(S("mb_BC"), 1)
                yield BG[s0 + 9]
                pe.wait_ge(S("mb_xdt"), it)
                pe.wait_ge(S("mb_wts"), it)
                pe.wait_ge(S("mb_cde"), it)
                if b == 2:
                    pe.wait_ge(S("smb_in"), 16 * (l + 1))
                else:
                    pe.wait_ge(S("zeroed"), l + 1)
                    if b > 0:
                        pe.wait_ge(S("mb_S"), 2 * l + b)
                for h in range(HC):
                    p = slice(64 * (h % 2), 64 * (h % 2) + 64)
                    lo = (h // 2) * P
                    mx(B[6][p, lo:lo + n], xdt[0:n, h, :], wts[0:n, h, 0:n], True, False)
                    if b == 2:
                        for s in range(NSEQ):
                            m = mx(B[6][p, lo + s * STEP:lo + (s + 1) * STEP], smb[:, h // 3, s, h % 3, :],
                                   cde[:, h, s * STEP:(s + 1) * STEP], False, s == NSEQ - 1)
                    else:
                        m = mx(B[6][p, lo:lo + n], smb_p[:, h * HD:(h + 1) * HD], cde[:, h, 0:n], False, True)
                m.then_inc(S("mb_y"), 1)
                if b == 2:
                    flat = xwe[:, :, :, :].rearrange("p s h d -> p (s h d)")
                    for k, at in enumerate((9, 11, 11, 13, 13, 14)):
                        yield BG[s0 + at]
                        pe.wait_ge(S("mb_xwe"), 2 * l + k // 3 + 1)
                        if k == 1:
                            pe.wait_ge(S("mb_y2"), it)
                        elif k >= 2:
                            pe.wait_ge(S("mb_ds_used"), 6 * l + k - 1)
                        mm(B[7 - k % 2][:, :], Btk[0:n, k // 3, :], flat[:, k % 3 * 512:(k % 3 + 1) * 512],
                           start=True, stop=True).then_inc(S("mb_ds"), 1)
                    yield BG[s0 + 15]
                    pe.wait_ge(S("mb_ds_used"), 6 * (l + 1))
                else:
                    for g in range(2):
                        m = mm(B[7][:, g * 192:(g + 1) * 192], Btk[0:n, g, :], xw[0:n, 3 * g:3 * g + 3, :],
                               start=True, stop=True)
                    m.then_inc(S("mb_dS"), 1)
                    yield BG[s0 + 11]
                    pe.wait_ge(S("mb_S"), 2 * l + b + 1)
                pe.wait_ge(S("mb_sq"), it)
                for q in range(3):
                    m = mm(B[7][:, 0:n], C("ones"), ysq[:, q, 0:n], start=(q == 0), stop=(q == 2))
                m.then_inc(S("mb_ms"), 1)

            def rwkv_all(l):
                for b in range(3):
                    yield from rwkv(l, b)

            def others(l):
                for b in range(3):
                    yield from retention(l, b)
                for b in range(3):
                    yield from mamba(l, b)

            def ffn(l):
                def body(i, g, e):
                    for f in range(FT):
                        pe.wait_ge(S("gu_free"), e * FT + f + 1)
                        full_slot(g + 2 * f, G_FFN[l] + 2 * f, B[2 * (f % 2)][:, 0:T])
                        full_slot(g + 2 * f + 1, G_FFN[l] + 2 * f + 1, B[2 * (f % 2) + 1][:, 0:T])
                    for m_ in range(KT):
                        pe.wait_ge(S("dn_free"), e * KT + m_ + 5)
                        for f in range(FT):
                            if m_ == 0:
                                pe.wait_ge(S("hid_split"), e * FT + f + 1)
                            j = m_ * FT + f
                            s = 2 * FT + j // KT
                            if j % KT == 0:
                                pe.wait_ge(S("slot_split"), g + s + 1)
                            m = three(B[4 + m_ % 4][:, 0:T], j % KT, G_FFN[l] + s, hidh[:, f, :], hidl[:, f, :],
                                      f == 0, f == FT - 1)
                            if j % KT == KT - 1:
                                m.then_inc(S("slot_used"), 1)
                            elif f == FT - 1:
                                m.then_inc(S("dn"), 1)
                expert_loop(pe, l, body)

            L = DEPTH - 1

            def router():
                full_slot(G_FFN[L] - 1, G_FFN[L] - 1, B[6][:, 0:T])
                pe.wait_ge(S("ro_act"), 1)
                for q, (c0, n) in enumerate(BLOCKS):
                    m = pe.transpose(B[7][0:n, q * NEXP:(q + 1) * NEXP], lg[:, c0:c0 + n],
                                     C("ident", 0, NEXP, slice(0, NEXP)))
                m.then_inc(S("ro_pe"), 1)
                for u in range(6):
                    if u >= 2:
                        pe.wait_ge(S("ro_act"), (2, 3, 5, 6)[u - 2])
                    c0, n = BLOCKS[u // 2]
                    for k in range(KT):
                        m = pe.transpose(B[2 * (u % 2) + k // 4][0:n, (k % 4) * P:(k % 4 + 1) * P],
                                         (hh, hl)[u % 2][:, k, c0:c0 + n].bitcast(F32), C("ident"))
                    m.then_inc(S("ro_pe"), 1)
                pe.wait_ge(S("ro_dve"), 2)
                for q, (c0, n) in enumerate(BLOCKS):
                    m = pe.transpose(B[5][0:NEXP, c0:c0 + n], rt["g"][0:n, q, :], C("ident", 0, n, slice(0, n)))
                m.then_inc(S("ro_pe"), 1)
                pe.wait_ge(S("ro_dve"), 3)
                for q, (c0, n) in enumerate(BLOCKS):
                    pe.transpose(B[7][0:n, q * NEXP:(q + 1) * NEXP], pos1[:, c0:c0 + n],
                                 C("ident", 0, NEXP, slice(0, NEXP)))
                pe.transpose(B[7][0:1, 32:32 + NEXP], upto[:, T - 1:T],
                             C("ident", 0, NEXP, slice(0, NEXP))).then_inc(S("ro_pe"), 1)

            def experts_dense():
                for e in range(NEXP):
                    if e >= 2:
                        pe.wait_ge(S("ro_act"), 9 + e - 1)
                    mm(B[e % 2][:, 0:T], C("sel", e * P, P, slice(0, NEXP)), lg[:, :],
                       start=True, stop=True).then_inc(S("ro_pe"), 1)
                pe.wait_ge(S("ro_act"), 9 + NEXP)

                def body(i, g, e):
                    pe.wait_ge(S("dn_free"), e * KT + KT)
                    for c, (j0, nj, nf) in enumerate(CHUNKS):
                        if c >= 2:
                            pe.wait_ge(S("gu_free"), e * FT + 2 * c)
                        for j in range(j0, j0 + nj):
                            pe.wait_ge(S("slot_split"), g + j + 1)
                            for t in range(2 * nf):
                                out = B[4 * (c % 2) + 2 * (t // nf) + t % nf][:, 0:T]
                                for kk in range(KT // nj):
                                    k = (j - j0) * (KT // nj) + kk
                                    m = three(out, kk * 2 * nf + t, G_FFN[L] + j, hh[:, k, :], hl[:, k, :],
                                              k == 0, k == KT - 1)
                            m.then_inc(S("slot_used"), 1)
                    pe.wait_ge(S("gu_free"), e * FT + FT + 2)
                    for f in range(FT):
                        pe.wait_ge(S("hid_split"), e * FT + f + 1)
                        pe.wait_ge(S("slot_split"), g + 2 * FT + f + 1)
                        for m_ in range(KT):
                            m = three(B[m_][:, 0:T], m_, G_FFN[L] + 2 * FT + f, hidh[:, f, :], hidl[:, f, :],
                                      f == 0, f == FT - 1)
                        m.then_inc(S("slot_used"), 1)
                expert_loop(pe, L, body)

            def gather(i):
                for z, bk in enumerate((6, 2)):
                    for k in range(KT):
                        for q in range(3):
                            rhs = pick[:, i, q, :] if isinstance(i, int) else \
                                pick[:, bass.ds(i, 1), q, :].rearrange("p o c -> p (o c)")
                            m = mm(B[bk + k // 4][:, (k % 4) * P:(k % 4 + 1) * P], htk[z][:, q, k * P:(k + 1) * P],
                                   rhs, start=(q == 0), stop=(q == 2))
                    m.then_inc(S("taken"), 1)

            def experts_picked():
                pe.wait_ge(S("ro_dve"), 5)
                gather(0)
                for e in range(NEXP):
                    for q in range(3):
                        m = mm(B[5][:, e:e + 1], pick[:, e, q, :].bitcast(F32), rt["g"][:, q, e:e + 1],
                               start=(q == 0), stop=(q == 2))
                m.then_inc(S("ro_pe"), 1)
                for e in range(NEXP):
                    if e >= 2:
                        pe.wait_ge(S("ro_dve"), 6 + e - 1)
                    mm(B[e % 2][:, 0:T], C("sel", e * P, P, slice(0, NEXP)), pos1[:, :],
                       start=True, stop=True).then_inc(S("ro_pe"), 1)
                pe.wait_ge(S("ro_dve"), 5 + NEXP)
                pe.wait_ge(S("ro_act"), 10)

                def turn(i, c):
                    pe.wait_ge(S("gu_free"), i * NC + (N_E[0] * FT + 2 + c + 1))
                    if c >= 2:
                        pe.wait_ge(S("hid_split"), i * NC + (N_E[0] * FT + c - 1))
                    for t in range(CHUNKS[c][2]):
                        m = pe.transpose(B[2 + c % 2][:, t * P:(t + 1) * P], hid[:, c % 2, t * P:(t + 1) * P], C("ident"))
                    m.then_inc(S("hid_t"), 1)

                def body(i, g, e):
                    pe.wait_ge(S("taken_hi"), i + 1)
                    pe.wait_ge(S("taken_lo"), i + 1)
                    for c, (j0, nj, nf) in enumerate(CHUNKS):
                        for j in range(j0, j0 + nj):
                            r = G_FFN[L] + j
                            pe.wait_ge(S("slot_split"), g + j + 1)
                            for kk in range(KT // nj):
                                k, cols = (j - j0) * (KT // nj) + kk, slice(kk * 2 * nf * P, (kk + 1) * 2 * nf * P)
                                out = B[c % 2][:, 0:2 * nf * P]
                                mm(out, hh[:, k, 0:P], whi[:, r % HI, cols], start=(k == 0), stop=False)
                                mm(out, hl[:, k, 0:P], whi[:, r % HI, cols], start=False, stop=False)
                                m = mm(out, hh[:, k, 0:P], wlo[:, r % RAW, cols], start=False, stop=(k == KT - 1))
                            m.then_inc(S("slot_used"), 1)
                            if j in TURN:
                                turn(i, TURN[j])
                    pe.wait_ge(S("put_free"), i * 4 + 4)
                    pe.wait_ge(S("dn_free"), i * 4 + KT * (1 + N_E[0]))
                    for f in range(FT):
                        if f % 2 == 0:
                            pe.wait_ge(S("hid_split"), i * NC + (N_E[0] * FT + f // 2 + 1))
                        pe.wait_ge(S("slot_split"), g + 2 * FT + f + 1)
                        r = G_FFN[L] + 2 * FT + f
                        for q, (h_, w_) in enumerate(((hidh, whi[:, r % HI, :]), (hidh, wlo[:, r % RAW, :]),
                                                      (hidl, whi[:, r % HI, :]))):
                            for z in range(2):
                                m = mm(B[4 + z][:, :], h_[:, f, 0:P], w_[:, z * 512:(z + 1) * 512],
                                       start=(f == 0 and q == 0), stop=(f == FT - 1 and q == 2))
                        m.then_inc(S("slot_used"), 1)
                        if 2 * FT + f in TURN:
                            turn(i, TURN[2 * FT + f])
                    gather(i + 1)
                    for m_ in range(KT):
                        if m_ < 2:
                            pe.wait_ge(S("y_lo"), 2 * i + m_ + 1)
                        elif m_ == 2:
                            pe.wait_ge(S("taken_hi"), i + 2)
                        elif m_ in (4, 6):
                            pe.wait_ge(S("put_free"), i * 4 + m_ // 2 + 3)
                        elif m_ in (5, 7):
                            pe.wait_ge(S("dn_free"), i * 4 + (KT * (1 + N_E[0]) + (m_ - 3) // 2))
                        to = place[:, bass.ds(i, 1), :].rearrange("p o t -> p (o t)")
                        mm(B[4 + m_ % 4][:, 0:T], hidh[:, m_, P:2 * P], to, start=True, stop=False)
                        mm(B[4 + m_ % 4][:, 0:T], hidl[:, m_, P:2 * P], to, start=False, stop=True)\
                            .then_inc(S("put"), 1)
                expert_loop(pe, L, body)

            pe.wait_ge(S("const_in"), 16)
            for l in range(DEPTH):
                pe.wait_ge(S("par_in"), 16 * (l + 1))
                norm(2 * l)
                for j in range(WIN):
                    if j >= 2:
                        pe.wait_ge(S("in_read"), WIN * l + j - 1)
                    full_slot(G_IN[l] + j, G_IN[l] + j, B[6 + j % 2][:, 0:T], KT * 2 * l if j == 0 else None)
                weave(rwkv_all(l), shift(l), others(l))
                pe.wait_ge(S("rw_done"), 3 * (l + 1))
                pe.wait_ge(S("mix_done"), 6 * (l + 1))
                for j in range(KT):
                    if j >= 2:
                        pe.wait_ge(S("out_read"), KT * l + j - 1)
                    full_slot(G_OUT[l] + j, G_OUT[l] + j, B[6 + j % 2][:, 0:T])
                    if j >= 2:
                        norm(2 * l + 1, [j - 2])
                norm(2 * l + 1, range(KT - 2, KT))
                pe.wait_ge(S("h_split"), KT * (2 * l + 2))
                if l == DEPTH - 1:
                    router()
                    pe.wait_ge(S("ro_dve"), 4)
                    most = pe.value_load(n_most_i[0:1, 0:1], min_val=0, max_val=T)
                    with pe.If(most <= P):
                        experts_picked()
                    with pe.Else():
                        experts_dense()
                else:
                    ffn(l)
            norm(2 * DEPTH)

        @block.scalar
        def _(act):
            af = act.activation

            def hi(g, ring, rounds):
                act.wait_ge(S(f"slot_in{ring % RAW}"), 16 * rounds)
                if not isinstance(g, int) or g >= HI:
                    act.wait_ge(S("slot_used"), g - HI + 1)
                af(whi[:, ring % HI, :], wraw[:, ring % RAW, :], ACT.Copy).then_inc(S("slot_hi"), 1)

            def hi_ahead(g):
                hi(g + HI, g + HI, (g + HI) // RAW + 1)

            def squares(i, tiles=range(KT)):
                for k in tiles:
                    l = i // 2
                    if i == 0:
                        act.wait_ge(S("x_in"), 16)
                    elif i % 2:
                        act.wait_ge(S("out_read"), KT * l + k + 1)
                    elif i < 2 * DEPTH:
                        act.wait_ge(S("dn_free"), KT + KT * (N_E[0] - 1) + k + 1)
                    if KT * i + k >= 2:
                        act.wait_ge(S("sq_used"), KT * i + k - 1)
                    af(sqb[:, k % 2, :], x[:, k, :], ACT.Square).then_inc(S("sq_ready"), 1)

            def norm(i):
                act.wait_ge(S("sq_used"), KT * (i + 1))
                act.wait_ge(S("const_in"), 16)
                af(rstd[:, :], B[0][:, 0:T], ACT.Sqrt, scale=1.0 / D, bias=C("eps", 0, 1)).then_inc(S("nrm_sd"), 1)
                if i == 2 * DEPTH:
                    return
                for k in range(KT):
                    act.wait_ge(S("h_k"), KT * i + k + 1)
                    af(hh[:, k, :], htmp[:, k % 2, :], ACT.Copy).then_inc(S("hh_k"), 1)

            def evac_in(l, j):
                act.wait_ge(S("slot_used"), G_IN[l] + j + 1)
                src = B[6 + j % 2]
                smp = src[:, SEQ:T].rearrange("p (s k) -> p s k", k=STEP)
                if j < A_TILES:
                    af(cR[:, j, 1:EA], src[:, 0:SEQ], ACT.Copy)
                    m = af(cR[:, j, EA:WA_].rearrange("p (s k) -> p s k", k=STEP + 1)[:, :, 1:], smp, ACT.Copy)
                elif j < A_TILES + B_TILES:
                    m = af(cB[:, j - A_TILES, :], src[:, 0:T], ACT.Copy)
                elif j < A_TILES + B_TILES + TC:
                    m = af(cZ[:, j - A_TILES - B_TILES, :], src[:, 0:T], ACT.Copy)
                elif j < WIN - 1:
                    t = j - A_TILES - B_TILES - TC
                    af(cX[:, t, 3:EX], src[:, 0:SEQ], ACT.Copy)
                    m = af(cX[:, t, EX:WX_].rearrange("p (s k) -> p s k", k=STEP + 3)[:, :, 3:], smp, ACT.Copy)
                else:
                    m = af(cD[0:HC, :], src[0:HC, 0:T], ACT.Copy)
                m.then_inc(S("in_read"), 1)

            def shift(l):
                for b in range(3):
                    it, n = 3 * l + b + 1, BLOCKS[b][1]
                    yield SHIFT_AT[b] + 1
                    act.wait_ge(S("rw_xm"), 2 * it - 1)
                    af(tw[0:64, 0:n], Dx[0:64, 9, 0:n], ACT.Tanh)
                    af(gs[:, 0:n], Dx[:, 10, 0:n], ACT.Sigmoid).then_inc(S("rw_lora"), 1)

            def rwkv(l, b):
                it, (c0, n) = 3 * l + b + 1, BLOCKS[b]
                nch, cb, s0 = chunks(b), 5 * l + 2 * b, RW_AT[b]
                yield s0 + 2
                for q, dst, bias in ((0, "sg", "w0"), (1, "aa", "a0")):
                    act.wait_ge(S("rw_up"), 3 * it - 2 + q)
                    for t in range(TA):
                        m = af(U[dst][:, t, 0:n], B[q][:, t * P:t * P + n], ACT.Sigmoid, bias=V(bias, t))
                    m.then_inc(S("rw_sig"), 1)
                act.wait_ge(S("rw_up"), 3 * it)
                af(U["g"][:, :, 0:n], bank(2, 3, n), ACT.Copy).then_inc(S("rw_sig"), 1)
                yield s0 + 3
                act.wait_ge(S("rw_kr"), it)
                af(U["sq"][:, :, 0:n], U["kr"][:, :, 0:n], ACT.Square).then_inc(S("rw_sq"), 1)
                act.wait_ge(S("rw_scan"), it)
                af(U["P"][:, :, 0:n], U["L"][:, :, 0:n], ACT.Exp, scale=-SQE)
                af(U["Pi"][:, :, 0:n], U["L"][:, :, 0:n], ACT.Exp, scale=SQE)
                act.wait_ge(S("rw_lm"), it)
                af(U["Pm"][:, :, 0:n], U["Lm"][:, :, 0:n], ACT.Exp, scale=-SQE).then_inc(S("rw_exp"), 1)
                yield s0 + 4
                act.wait_ge(S("rw_ssm"), it)
                af(U["be"][:, :, 0:n], U["be"][:, :, 0:n], ACT.Sqrt).then_inc(S("rw_sd"), 1)
                yield s0 + 6
                for q, bk in enumerate((5, 0, 1)):
                    act.wait_ge(S("rw_tr"), 3 * it - 2 + q)
                    af(tok[0:n, q, :, :], bank(bk, 3, P, slice(0, n)), ACT.Copy).then_inc(S("rw_tok"), 1)
                for c in range(nch):
                    yield s0 + RW_CH[b] + 4 * c
                    r = slice(64 * c, 64 * c + 64)
                    if b == 2:
                        act.wait_ge(S("rw_S0"), l + 1)
                        af(Rs0[:, :, :], b64(0, TA), ACT.Copy).then_inc(S("rw_S0c"), 1)
                    yield s0 + RW_CH[b] + 4 * c + 1
                    act.wait_ge(S("rw_SA"), cb + c + 1)
                    af(SA[r, :, :], b64(4, HA, r), ACT.Copy).then_inc(S("rw_SAc"), 1)
                yield s0 + RW_END[b]
                act.wait_ge(S("rw_y"), cb + nch)
                af(U["kr"][:, :, 0:n], bank(5, 3, n), ACT.Copy).then_inc(S("rw_y5" if b == 2 else "rw_yc"), 1)
                yield s0 + RW_END[b] + 1
                act.wait_ge(S("rw_yd"), it)
                af(U["sq"][:, :, 0:n], U["kp"][:, :, 0:n], ACT.Square).then_inc(S("rw_ysq"), 1)
                yield s0 + RW_END[b] + 2
                act.wait_ge(S("rw_var"), it)
                af(U["be"][:, :, 0:n], bank(4, 3, n), ACT.Sqrt, scale=1.0 / HD, bias=C("eps", 1, 1)).then_inc(S("rw_ysd"), 1)
                yield s0 + RW_END[b] + 4
                act.wait_ge(S("rw_yf"), it)
                af(hh[:, 0:TA, c0:c0 + n], U["kp"][:, :, 0:n], ACT.Copy).then_inc(S("rw_yh"), 1)

            def retention(l, b):
                it, (c0, n), s0 = 3 * l + b + 1, BLOCKS[b], RT_AT[b]
                yield BG[s0 + 4]
                act.wait_ge(S("rt_tr"), it)
                af(vkt[0:n, :, :], bank(6, 4, P, slice(0, n)), ACT.Copy).then_inc(S("rt_tok"), 1)
                yield BG[s0 + 5]
                act.wait_ge(S("rt_o"), it)
                af(ro[:, :, 0:n], bank(7, 2, n), ACT.Copy).then_inc(S("rt_oc"), 1)
                yield BG[s0 + 6]
                if b == 2:
                    act.wait_ge(S("rt_o2"), l + 1)
                else:
                    act.wait_ge(S("rt_oc"), it)
                af(rsq[:, :, 0:n], ro[:, :, 0:n], ACT.Square).then_inc(S("rt_sq"), 1)
                af(rsg[:, :, 0:n], cB[:, 6:8, c0:c0 + n], ACT.Silu).then_inc(S("rt_sg"), 1)
                yield BG[s0 + 7]
                act.wait_ge(S("rt_ms"), it)
                af(rsq[:, :, 0:n], bank(7, 2, n), ACT.Sqrt, scale=1.0 / HD, bias=C("eps", 0, 1)).then_inc(S("rt_sd"), 1)
                yield BG[s0 + 8]
                act.wait_ge(S("rt_y"), it)
                af(hh[:, TA:TA + TB, c0:c0 + n], ro[:, :, 0:n], ACT.Copy).then_inc(S("rt_yh"), 1)

            def mamba_dt(l):
                r = slice(0, HC)
                yield 6
                af(an[r, :], V("a_log", rows=r), ACT.Exp)
                af(dd["x"][r, :], cD[r, :], ACT.Identity, bias=V("dt_bias", rows=r))
                af(dd["e"][r, :], cD[r, :], ACT.Abs, bias=V("dt_bias", rows=r)).then_inc(S("mb_e"), 1)
                act.wait_ge(S("mb_e"), 3 * l + 1)
                af(dd["e"][r, :], dd["e"][r, :], ACT.Exp, scale=-1.0).then_inc(S("mb_e"), 1)
                yield 21
                act.wait_ge(S("mb_dt"), 2 * l + 1)
                af(dd["wk"][r, :], dd["lm"][r, :], ACT.Exp).then_inc(S("mb_e"), 1)

            def mamba(l, b):
                it, (c0, n), s0 = 3 * l + b + 1, BLOCKS[b], MB_AT[b]
                yield BG[s0 + 1]
                act.wait_ge(S("mb_t3"), it)
                af(tk3[0:n, :, :], B[6][0:n, 0:3 * HC].rearrange("p (a c) -> p a c", c=HC), ACT.Copy).then_inc(S("mb_tk3"), 1)
                yield BG[s0 + 2]
                act.wait_ge(S("mb_cv"), 4 * it)
                af(xc[:, :, 0:n], xcs[:, :, 0:n], ACT.Silu).then_inc(S("mb_xc"), 1)
                af(zs[:, :, 0:n], cZ[:, :, c0:c0 + n], ACT.Silu).then_inc(S("mb_zs"), 1)
                yield BG[s0 + 3]
                act.wait_ge(S("mb_cb"), it)
                af(ecb[:, 0:3, 0:n], bank(7, 3, n), ACT.Exp)
                af(ecb[:, 3:6, 0:n], bank(6, 3, n), ACT.Exp).then_inc(S("mb_ecb"), 1)
                yield BG[s0 + 5]
                act.wait_ge(S("mb_seg"), it)
                af(seg[0:n, :, 0:n], seg[0:n, :, 0:n], ACT.Exp).then_inc(S("mb_E"), 1)
                yield BG[s0 + 6]
                act.wait_ge(S("mb_tB"), it)
                af(Btk[0:n, :, :], bank(7, 2, P, slice(0, n)), ACT.Copy).then_inc(S("mb_Btk"), 1)
                yield BG[s0 + 10]
                act.wait_ge(S("mb_y2"), it)
                af(ysq[:, :, 0:n], yz[:, :, 0:n], ACT.Square).then_inc(S("mb_sq"), 1)
                yield BG[s0 + (15 if b == 2 else 11)]
                act.wait_ge(S("mb_ms"), it)
                af(zs[:, 0, 0:n], B[7][:, 0:n], ACT.Sqrt, scale=1.0 / (HC * HD), bias=C("eps", 2, 1)).then_inc(S("mb_sd"), 1)
                yield BG[s0 + (17 if b == 2 else 13)]
                act.wait_ge(S("mb_y3"), it)
                af(hh[:, TA + TB:KT, c0:c0 + n], yz[:, :, 0:n], ACT.Copy).then_inc(S("mb_yh"), 1)

            def rwkv_all(l):
                for b in range(3):
                    yield from rwkv(l, b)

            def others(l):
                for b in range(3):
                    yield from retention(l, b)
                for b in range(3):
                    yield from mamba(l, b)

            L = DEPTH - 1

            def next_hi(l, i, g, j):
                r = G_FFN[l] + j + HI
                hi(g + j + HI, r, i * (EXP_SLOTS // RAW) + r // RAW + 1)

            def hidden_hi(f, e):
                act.wait_ge(S("gu_free"), e * FT + f + 3)
                af(hidh[:, f, :], hid[:, f % 2, :], ACT.Copy).then_inc(S("hid_hi"), 1)

            def ffn(l):
                def body(i, g, e):
                    for j in range(EXP_SLOTS):
                        next_hi(l, i, g, j)
                        f = j // 2
                        if j < 2 * FT and j % 2:
                            act.wait_ge(S("slot_used"), g + 2 * f + 1)
                            af(sil[:, f % 2, :], B[2 * (f % 2)][:, 0:T], ACT.Silu).then_inc(S("sil"), 1)
                        elif 0 < j <= 2 * FT:
                            hidden_hi(f - 1, e)
                expert_loop(act, l, body)

            def router():
                act.wait_ge(S("slot_used"), G_FFN[L])
                act.wait_ge(S("st_out"), 16 * 8 * (L + 1))
                af(lg[:, :], B[6][0:NEXP, 0:T], ACT.Copy).then_inc(S("ro_act"), 1)
                for u in range(6):
                    if u == 2:
                        act.wait_ge(S("ro_dve"), 1)
                        af(rt["e"][:, :, :], rt["l"][:, :, :], ACT.Exp).then_inc(S("ro_act"), 1)
                    act.wait_ge(S("ro_pe"), u + 2)
                    n = BLOCKS[u // 2][1]
                    if n < P:
                        af(htk[u % 2][n:P, u // 2, :], cst[n:P, 0:D], ACT.Copy, scale=0.0)
                    for z in range(2):
                        m = af(htk[u % 2][0:n, u // 2, z * 512:(z + 1) * 512], B[2 * (u % 2) + z][0:n, :], ACT.Copy)
                    m.then_inc(S("ro_act"), 1)
                act.wait_ge(S("ro_pe"), 8)
                af(lg[:, :], B[5][0:NEXP, 0:T], ACT.Copy).then_inc(S("ro_act"), 1)

            def experts_dense():
                for e in range(NEXP):
                    act.wait_ge(S("ro_pe"), 9 + e + 1)
                    af(gbc[:, e, :], B[e % 2][:, 0:T], ACT.Copy).then_inc(S("ro_act"), 1)

                def body(i, g, e):
                    for j in range(EXP_SLOTS):
                        next_hi(L, i, g, j)
                        if j in ENDS:
                            c = ENDS[j]
                            act.wait_ge(S("slot_used"), g + j + 1)
                            tiles = range(2 * c, 2 * c + CHUNKS[c][2])
                            for f in tiles:
                                af(sil[:, f % 2, :], B[4 * (c % 2) + f % 2][:, 0:T], ACT.Silu).then_inc(S("sil"), 1)
                            for f in tiles:
                                hidden_hi(f, e)
                expert_loop(act, L, body)
                act.wait_ge(S("yt_free"), KT + KT * NEXP)

            def taken_hi(i):
                act.wait_ge(S("taken"), 2 * i + 1)
                for z in range(2):
                    m = af(hh[:, 4 * z:4 * z + 4, 0:P], bank(6 + z, 4, P), ACT.Copy)
                m.then_inc(S("taken_hi"), 1)

            def experts_picked():
                taken_hi(0)
                act.wait_ge(S("ro_pe"), 10)
                af(slot_gate[:, :], B[5][:, 0:NEXP], ACT.Copy).then_inc(S("ro_act"), 1)
                act.wait_ge(S("ro_act"), 10)

                def gated(i, g):
                    act.wait_ge(S("slot_used"), g + EXP_SLOTS)
                    for z in range(2):
                        af(hidh[:, 4 * z:4 * z + 4, P:2 * P], bank(4 + z, 4, P), ACT.Copy,
                           scale=slot_gate[:, bass.ds(i, 1)]).then_inc(S("y_hi"), 1)

                def body(i, g, e):
                    for j in range(EXP_SLOTS):
                        if j == EXP_SLOTS - 1:
                            gated(i, g)
                        next_hi(L, i, g, j)
                        if j in ENDS:
                            c, n = ENDS[j], CHUNKS[ENDS[j]][2] * P
                            act.wait_ge(S("slot_used"), g + j + 1)
                            af(sil[:, c % 2, 0:n], B[c % 2][:, 0:n], ACT.Silu).then_inc(S("sil"), 1)
                        if j in TURN:
                            c, n = TURN[j], CHUNKS[TURN[j]][2]
                            act.wait_ge(S("hid_t"), i * NC + c + 1)
                            af(hidh[:, 2 * c:2 * c + n, 0:P], bank(2 + c % 2, n, P), ACT.Copy).then_inc(S("hid_hi"), 1)
                    taken_hi(i + 1)
                    for m_ in range(0, KT, 2):
                        act.wait_ge(S("put"), i * KT + m_ + 1)
                        act.wait_ge(S("yt_free"), i * 4 + (KT - 3 + m_ // 2))
                        af(yt[:, m_ // 2, :], B[4 + m_ % 4][:, 0:T], ACT.Copy).then_inc(S("put_free"), 1)
                expert_loop(act, L, body)
                act.wait_ge(S("yt_free"), KT + 4 * NEXP)
                act.wait_ge(S("dn_free"), KT * (1 + N_E[0]) + 4 * NEXP)

            act.dma_start(cst[:, :], consts_in).then_inc(S("const_in"), 16)
            for l in range(DEPTH):
                squares(2 * l)
                if l == 0:
                    for g in range(HI):
                        hi(g, g, 1)
                act.wait_ge(S("par_in"), 16 * (l + 1))
                norm(2 * l)
                for j in range(WIN):
                    if j < WIN - HI:
                        hi_ahead(G_IN[l] + j)
                    evac_in(l, j)
                weave(rwkv_all(l), shift(l), mamba_dt(l), others(l))
                for g in range(G_OUT[l], G_OUT[l] + HI):
                    hi(g, g, g // RAW + 1)
                for j in range(KT):
                    hi_ahead(G_OUT[l] + j)
                    if j >= 1:
                        squares(2 * l + 1, [j - 1])
                squares(2 * l + 1, [KT - 1])
                norm(2 * l + 1)
                if l == DEPTH - 1:
                    hi_ahead(G_FFN[l] - 1)
                    router()
                    act.wait_ge(S("ro_dve"), 4)
                    most = act.value_load(n_most_i[0:1, 0:1], min_val=0, max_val=T)
                    with act.If(most <= P):
                        experts_picked()
                    with act.Else():
                        experts_dense()
                else:
                    act.wait_ge(S("st_out"), 16 * 8 * (l + 1))
                    ffn(l)
            squares(2 * DEPTH)
            norm(2 * DEPTH)

        @block.vector
        def _(v):
            tt, ts, stt, cp = v.tensor_tensor, v.tensor_scalar, v.scalar_tensor_tensor, v.tensor_copy
            own = [0]

            def own_count():
                own[0] += 1
                return own[0]

            def lo(g, ring):
                v.wait_ge(S("slot_hi"), g + 1)
                tt(wlo[:, ring % RAW, :], wraw[:, ring % RAW, :], whi[:, ring % HI, :].bitcast(F32),
                   ALU.subtract).then_inc(S("slot_split"), 1)

            def norm(i):
                v.wait_ge(S("nrm_sd"), i + 1)
                v.reciprocal(rstd[:, :], rstd[:, :]).then_inc(S("v_step"), 1)
                v.wait_ge(S("v_step"), own_count())
                if i == 2 * DEPTH:
                    for k in range(KT):
                        m = stt(x[:, k, :], x[:, k, :], V("g_fin", k), rstd[:, :], ALU.mult, ALU.mult)
                    m.then_inc(S("y_done"), 1)
                    return
                gain = "g_ffn" if i % 2 else "g_mix"

                def scaled(k):
                    stt(htmp[:, k % 2, :], x[:, k, :], V(gain, k), rstd[:, :], ALU.mult, ALU.mult).then_inc(S("h_k"), 1)
                scaled(0)
                scaled(1)
                for k in range(KT):
                    v.wait_ge(S("hh_k"), KT * i + k + 1)
                    tt(hl[:, k, :], htmp[:, k % 2, :], hh[:, k, :].bitcast(F32), ALU.subtract).then_inc(S("h_split"), 1)
                    if k + 2 < KT:
                        if k >= 0:
                            v.wait_ge(S("h_split"), KT * i + k + 1)
                        scaled(k + 2)

            def shift(l):
                for b in range(3):
                    (c0, n) = BLOCKS[b]
                    yield SHIFT_AT[b]
                    if b == 0:
                        v.wait_ge(S("in_read"), WIN * (l + 1))
                        v.wait_ge(S("ext_ready"), l + 1)
                    if b < 2:
                        now, prev = cR[:, :, c0 + 1:c0 + 1 + n], cR[:, :, c0:c0 + n]
                        d3 = Dx[:, :, 0:n]
                    else:
                        e3 = cR[:, :, EA:WA_].rearrange("p t (s k) -> p t s k", k=STEP + 1)
                        now, prev = e3[:, :, :, 1:], e3[:, :, :, 0:STEP]
                        d3 = Dx[:, :, 0:n].rearrange("p t (s k) -> p t s k", k=STEP)
                    for t0, t1 in ((9, A_TILES), (0, 9)):
                        yield SHIFT_AT[b] + 2 * (t0 == 0 and b > 0)
                        tt(d3[:, t0:t1], prev[:, t0:t1], now[:, t0:t1], ALU.subtract).then_inc(S("v_step"), 1)
                        v.wait_ge(S("v_step"), own_count())
                        for t in range(t0, t1):
                            m = stt(d3[:, t], d3[:, t], V("mu", t), now[:, t], ALU.mult, ALU.add)
                        m.then_inc(S("rw_xm"), 1)

            def rwkv(l, b):
                it, (c0, n) = 3 * l + b + 1, BLOCKS[b]
                nch, cb, lv, lw, s0 = chunks(b), 5 * l + 2 * b, 15 * l + 6 * b, 12 * l + 5 * b, RW_AT[b]
                nn = nch * CH
                u = {k: t[:, :, 0:n] for k, t in U.items()}
                rr = slice(0, nn)
                yield s0 + 1
                v.wait_ge(S("rw_xm"), 2 * it)
                r_, k_, v_ = Dx[:, 0:3, 0:n], Dx[:, 3:6, 0:n], Dx[:, 6:9, 0:n]
                tt(u["kr"], k_, over(V("k_k", 0, 3), n), ALU.mult).then_inc(S("rw_kr"), 1)
                yield s0 + 3
                v.wait_ge(S("rw_sig"), 3 * it - 2)
                for t in range(TA):
                    m = v.tensor_tensor_scan(U["L"][:, t, 0:n], C("scan8" if b == 2 else "scan64", 0, n),
                                             U["sg"][:, t, 0:n], 0.0, ALU.mult, ALU.add)
                m.then_inc(S("rw_scan"), 1)
                v.wait_ge(S("rw_scan"), it)
                tt(u["Lm"], u["L"], u["sg"], ALU.subtract).then_inc(S("rw_lm"), 1)
                v.wait_ge(S("rw_sig"), 3 * it - 1)
                stt(u["t1"], u["aa"], -1.0, over(V("k_a", 0, 3), n), ALU.add, ALU.mult).then_inc(S("v_step"), 1)
                v.wait_ge(S("v_step"), own_count())
                stt(u["kp"], u["t1"], 1.0, k_, ALU.add, ALU.mult).then_inc(S("rw_kp"), 1)
                yield s0 + 4
                v.wait_ge(S("rw_ss"), it)
                ts(u["be"], bank(3, 3, n), 1e-24, None, ALU.max).then_inc(S("rw_ssm"), 1)
                yield s0 + 5
                v.wait_ge(S("rw_sd"), it)
                v.reciprocal(u["be"], u["be"]).then_inc(S("v_step"), 1)
                v.wait_ge(S("v_step"), own_count())
                tt(u["kk"], u["kr"], u["be"], ALU.mult).then_inc(S("v_step"), 1)
                v.wait_ge(S("v_step"), own_count())
                v.wait_ge(S("rw_exp"), it)
                stt(u["al"], u["Pm"], -1.0, u["kk"], ALU.mult, ALU.mult)
                tt(u["be"], u["kk"], u["aa"], ALU.mult).then_inc(S("v_step"), 1)
                v.wait_ge(S("v_step"), own_count())
                tt(u["be"], u["be"], u["Pi"], ALU.mult)
                v.wait_ge(S("rw_kp"), it)
                tt(u["ka"], u["kp"], u["Pi"], ALU.mult)
                tt(u["rho"], u["P"], r_, ALU.mult).then_inc(S("rw_ops"), 1)
                v.wait_ge(S("rw_bsum"), it)
                tt(u["bonus"], bank(4, 3, n), v_, ALU.mult).then_inc(S("rw_bonus"), 1)
                sfx = "8" if b == 2 else ""
                for q, (dst, mask) in enumerate(((AB, "strict"), (C12, "incl"))):
                    yield s0 + 7 + q
                    for o in range(2):
                        v.wait_ge(S("rw_sc"), 4 * it - 3 + 2 * q + o)
                        m = tt(dst[rr, o, :, :, :].rearrange("p z t c -> p (z t) c"), b64(2 + 2 * q + o, 2 * TA, rr),
                               rep(C(mask + sfx, rows=rr), 2 * TA), ALU.mult)
                    m.then_inc(S(("rw_AT", "rw_C")[q]), 1)
                if b == 0:
                    v.memset(Sbd[:, :, :], 0.0).then_inc(S("rw_Sbd"), 1)
                yield s0 + 9
                v.wait_ge(S("rw_AL"), lv + 1)
                tt(TT[rr, :, :], AL[rr, 0, :, :], rep(C("i64", rows=rr), HA), ALU.add)
                v.wait_ge(S("rw_W"), lv + 1)
                tt(TM[rr, :, :], b64(0, HA, rr), rep(C("i64", rows=rr), HA), ALU.add).then_inc(S("rw_T"), 1)
                for q in range(1, levels(b)):
                    yield s0 + 8 + 2 * q
                    v.wait_ge(S("rw_W"), lv + q + 1)
                    cp(Wm[rr, :, :], b64(0, HA, rr)).then_inc(S("rw_Wc"), 1)
                    yield s0 + 9 + 2 * q
                    v.wait_ge(S("rw_TW"), lw + q)
                    v.wait_ge(S("rw_T"), lv + q)
                    for bk, mt, odd in ((1, TM, 0), (2, TT, 1)):
                        got = B[bk][rr, 0:HA * 32].rearrange("p (x s) -> p x s", s=1 << q)
                        part = mt[rr, :, :].rearrange("p h (a o s) -> p (h a) o s", o=2, s=1 << q)[:, :, odd, :]
                        m = tt(part, part, got, ALU.add)
                    m.then_inc(S("rw_T"), 1)
                for c in range(nch):
                    r = slice(64 * c, 64 * c + 64)
                    yield s0 + RW_CH[b] + 4 * c
                    v.wait_ge(S("rw_R"), cb + c + 1)
                    cp(Rs[r, :, :], b64(3, HA, r)).then_inc(S("rw_Rc"), 1)
                    if b < 2:
                        yield s0 + RW_CH[b] + 4 * c + 3
                        v.wait_ge(S("rw_dS"), 4 * l + 2 * b + c + 1)
                        v.wait_ge(S("zeroed"), l + 1)
                        v.wait_ge(S("rw_Sbd"), 5 * l + 2 * b + c + 1)
                        v.wait_ge(S("rw_y"), cb + c + 1)
                        tt(srw_p[:, :, :], srw_p[:, :, :], b64(0, TA), ALU.add).then_inc(S("v_step"), 1)
                        v.wait_ge(S("v_step"), own_count())
                        last = U["P"][:, :, c * CH + CH - 1:c * CH + CH]
                        tt(srw_p[:, :, :], srw_p[:, :, :], last.to_broadcast([P, TA, HD]), ALU.mult).then_inc(S("v_step"), 1)
                        v.wait_ge(S("v_step"), own_count())
                        for o in range(2):
                            p = slice(64 * o, 64 * o + 64)
                            m = cp(Sbd[p, :, 64 * o:64 * o + 64], srw_p[p, :, :])
                        m.then_inc(S("rw_Sbd"), 1)
                if b == 2:
                    yield s0 + RW_END[b] - 1
                    v.wait_ge(S("rw_SAc"), cb + 1)
                    for t in range(TA):
                        if t >= 1:
                            v.wait_ge(S("rw_ds"), 3 * l + t)
                        tt(rwx[:, 0, :, :], rep(SA[0:CH, 2 * t:2 * t + 2, :].rearrange("p h c -> p (h c)"), NSEQ),
                           over(C("seq", rows=slice(0, CH)), P), ALU.mult).then_inc(S("rw_xs"), 1)
                    for t in range(TA):
                        v.wait_ge(S("rw_ds"), 3 * l + t + 1)
                        st = srw[:, t, :, :]
                        m = tt(st, st, B[1 + t][:, :].rearrange("p (s c) -> p s c", c=HD), ALU.add)
                        if t == TA - 1:
                            m.then_inc(S("rw_sSa"), 1)
                            v.wait_ge(S("rw_sSa"), l + 1)
                        else:
                            m.then_inc(S("v_step"), 1)
                            v.wait_ge(S("v_step"), own_count())
                        last = U["P"][:, t, STEP - 1:NSEQ * STEP:STEP]
                        tt(st, st, over(last, HD), ALU.mult).then_inc(S("rw_sS"), 1)
                    yield s0 + RW_END[b]
                    v.wait_ge(S("rw_y5"), l + 1)
                    tt(u["kr"], u["kr"], bank(0, 3, n), ALU.add).then_inc(S("rw_yc"), 1)
                    v.wait_ge(S("rw_yc"), it)
                yield s0 + RW_END[b] + 1
                v.wait_ge(S("rw_mean"), it)
                stt(u["kp"], bank(3, 3, n), -1.0 / HD, u["kr"], ALU.mult, ALU.add).then_inc(S("rw_yd"), 1)
                yield s0 + RW_END[b] + 3
                v.wait_ge(S("rw_ysd"), it)
                v.reciprocal(u["be"], u["be"]).then_inc(S("v_step"), 1)
                v.wait_ge(S("v_step"), own_count())
                tt(u["kp"], u["kp"], u["be"], ALU.mult).then_inc(S("v_step"), 1)
                v.wait_ge(S("v_step"), own_count())
                for t in range(TA):
                    m = ts(U["kp"][:, t, 0:n], U["kp"][:, t, 0:n], V("ln_w", t), V("ln_b", t), ALU.mult, ALU.add)
                m.then_inc(S("v_step"), 1)
                v.wait_ge(S("v_step"), own_count())
                v.wait_ge(S("rw_bonus"), it)
                tt(u["kp"], u["kp"], u["bonus"], ALU.add).then_inc(S("v_step"), 1)
                v.wait_ge(S("v_step"), own_count())
                v.wait_ge(S("rw_sig"), 3 * it)
                tt(u["kp"], u["kp"], u["g"], ALU.mult).then_inc(S("rw_yf"), 1)
                yield s0 + RW_END[b] + 5
                v.wait_ge(S("rw_yh"), it)
                tt(hl[:, 0:TA, c0:c0 + n], u["kp"], hh[:, 0:TA, c0:c0 + n].bitcast(F32), ALU.subtract)\
                    .then_inc(S("rw_done"), 1)

            def retention(l, b):
                it, (c0, n), s0 = 3 * l + b + 1, BLOCKS[b], RT_AT[b]
                q_ = qk[:, :, 0:n]
                yield BG[s0 + 1]
                v.wait_ge(S("rt_sw"), it)
                tt(q_, bank(6, 4, n), rep(C("sin", c0, n), 4), ALU.mult).then_inc(S("v_step"), 1)
                v.wait_ge(S("v_step"), own_count())
                v.wait_ge(S("rt_q2"), it)
                tt(q_, q_, qk2[:, :, 0:n], ALU.add).then_inc(S("v_step"), 1)
                v.wait_ge(S("v_step"), own_count())
                ts(qk[:, 2:4, 0:n], qk[:, 2:4, 0:n], HD ** -0.5, None, ALU.mult).then_inc(S("rt_qk"), 1)
                v.wait_ge(S("rt_qk"), it)
                for q, nm in enumerate(("qdec", "kdec")):
                    dec = C(nm).rearrange("p (t c) -> p t c", c=T)[:, :, c0:c0 + n]
                    m = tt(qkd[:, 2 * q:2 * q + 2, 0:n], qk[:, 2 * q:2 * q + 2, 0:n], dec, ALU.mult)
                m.then_inc(S("rt_dec"), 1)
                yield BG[s0 + 3]
                v.wait_ge(S("rt_sc"), it)
                mask = C("rmask8" if b == 2 else "rmask", rows=slice(0, n)).rearrange("p (h c) -> p h c", h=HB)
                for o in range(2):
                    hs = slice(o * TB, (o + 1) * TB)
                    m = tt(rsc[0:n, hs, 0:n], bank(6 + o, TB, n, slice(0, n)), mask[:, hs, :], ALU.mult)
                m.then_inc(S("rt_scm"), 1)
                if b == 2:
                    yield BG[s0 + 5]
                    v.wait_ge(S("rt_oc"), it)
                    tt(ro[:, :, 0:n], ro[:, :, 0:n], bank(6, TB, n), ALU.add).then_inc(S("rt_o2"), 1)
                    v.wait_ge(S("rt_o2"), l + 1)
                yield BG[s0 + 7]
                v.wait_ge(S("rt_dS"), it)
                if b < 2:
                    v.wait_ge(S("zeroed"), l + 1)
                    if b > 0:
                        v.wait_ge(S("rt_S"), 3 * l + b)
                for t in range(TB):
                    if b < 2:
                        m = stt(srt_p[:, t, :], srt_p[:, t, :], C("cdec", t, 1), B[6][:, t * HD:(t + 1) * HD],
                                ALU.mult, ALU.add)
                    else:
                        st = srt[:, t, :, :].rearrange("p s c -> p (s c)")
                        m = stt(st, st, C("cdec", TB + t, 1), B[6 + t][:, :], ALU.mult, ALU.add)
                m.then_inc(S("rt_S"), 1)
                yield BG[s0 + 8]
                v.wait_ge(S("rt_sd"), it)
                v.reciprocal(rsq[:, :, 0:n], rsq[:, :, 0:n]).then_inc(S("v_step"), 1)
                v.wait_ge(S("v_step"), own_count())
                v.wait_ge(S("rt_oc"), it)
                for t in range(TB):
                    m = stt(ro[:, t, 0:n], ro[:, t, 0:n], V("ret_norm", t), rsq[:, t, 0:n], ALU.mult, ALU.mult)
                m.then_inc(S("v_step"), 1)
                v.wait_ge(S("v_step"), own_count())
                v.wait_ge(S("rt_sg"), it)
                tt(ro[:, :, 0:n], ro[:, :, 0:n], rsg[:, :, 0:n], ALU.mult).then_inc(S("rt_y"), 1)
                yield BG[s0 + 9]
                v.wait_ge(S("rt_yh"), it)
                tt(hl[:, TA:TA + TB, c0:c0 + n], ro[:, :, 0:n], hh[:, TA:TA + TB, c0:c0 + n].bitcast(F32),
                   ALU.subtract).then_inc(S("mix_done"), 1)

            def mamba_dt(l):
                r = slice(0, HC)
                d = {k: t[r, :] for k, t in dd.items()}
                coef = [1.0 / k for k in (13, 11, 9, 7, 5, 3)]
                yield 10
                v.wait_ge(S("mb_e"), 3 * l + 2)
                ts(d["z"], d["e"], 2.0, None, ALU.add).then_inc(S("v_step"), 1)
                v.wait_ge(S("v_step"), own_count())
                yield 11
                v.reciprocal(d["z"], d["z"]).then_inc(S("v_step"), 1)
                v.wait_ge(S("v_step"), own_count())
                tt(d["z"], d["z"], d["e"], ALU.mult).then_inc(S("v_step"), 1)
                v.wait_ge(S("v_step"), own_count())
                yield 12
                tt(d["z2"], d["z"], d["z"], ALU.mult).then_inc(S("v_step"), 1)
                v.wait_ge(S("v_step"), own_count())
                ts(d["p"], d["z2"], 1.0 / 15, None, ALU.mult).then_inc(S("v_step"), 1)
                v.wait_ge(S("v_step"), own_count())
                yield 13
                for c in coef:
                    stt(d["p"], d["p"], c, d["z2"], ALU.add, ALU.mult).then_inc(S("v_step"), 1)
                    v.wait_ge(S("v_step"), own_count())
                    yield 14
                stt(d["p"], d["p"], 1.0, d["z"], ALU.add, ALU.mult).then_inc(S("v_step"), 1)
                v.wait_ge(S("v_step"), own_count())
                yield 15
                ts(d["x"], d["x"], 0.0, None, ALU.max).then_inc(S("v_step"), 1)
                v.wait_ge(S("v_step"), own_count())
                stt(d["dt"], d["p"], 2.0, d["x"], ALU.mult, ALU.add).then_inc(S("v_step"), 1)
                v.wait_ge(S("v_step"), own_count())
                yield 16
                ts(d["dA"], d["dt"], an[r, :], -1.0, ALU.mult, ALU.mult).then_inc(S("v_step"), 1)
                v.wait_ge(S("v_step"), own_count())
                v.tensor_tensor_scan(d["cum"], C("scanm", rows=r), d["dA"], 0.0, ALU.mult, ALU.add).then_inc(S("v_step"), 1)
                v.wait_ge(S("v_step"), own_count())
                yield 17
                for lo_, n_, k_ in ((0, 2, P), (SEQ, NSEQ, STEP)):
                    c3_ = d["cum"][:, lo_:lo_ + n_ * k_].rearrange("p (a k) -> p a k", k=k_)
                    o3 = d["lm"][:, lo_:lo_ + n_ * k_].rearrange("p (a k) -> p a k", k=k_)
                    m = tt(o3, c3_[:, :, k_ - 1:k_].to_broadcast([HC, n_, k_]), c3_, ALU.subtract)
                m.then_inc(S("mb_dt"), 1)
                yield 22
                v.wait_ge(S("mb_e"), 3 * l + 3)
                tt(d["wk"], d["wk"], d["dt"], ALU.mult).then_inc(S("mb_dt"), 1)

            def mamba(l, b):
                it, (c0, n), s0 = 3 * l + b + 1, BLOCKS[b], MB_AT[b]
                rn = slice(0, n)
                for j in range(CONV):
                    yield BG[s0 + j // 2]
                    if b == 0 and j == 0:
                        v.wait_ge(S("st_out"), 16 * (8 * l + 4))
                    if j:
                        v.wait_ge(S("mb_cv"), 4 * it - 4 + j)
                    for t in range(XT):
                        if b < 2:
                            src, dst = cX[:, t, c0 + j:c0 + j + n], xcs[:, t, 0:n]
                        else:
                            src = cX[:, t, EX:WX_].rearrange("p (s k) -> p s k", k=STEP + 3)[:, :, j:j + STEP]
                            dst = xcs[:, t, 0:n].rearrange("p (s k) -> p s k", k=STEP)
                        if j == 0:
                            m = ts(dst, src, V("conv_w", t), V("conv_b", t), ALU.mult, ALU.add)
                        else:
                            m = stt(dst, src, V("conv_w", j * XT + t), dst, ALU.mult, ALU.add)
                    m.then_inc(S("mb_cv"), 1)
                yield BG[s0 + 4]
                v.wait_ge(S("mb_ecb"), it)
                v.wait_ge(S("mb_tk3"), it)
                for h in range(HC):
                    m = ts(seg[rn, h, 0:n], B[7 - h // 3][rn, (h % 3) * P:(h % 3) * P + n], tk3[rn, 1, h:h + 1], 0.0,
                           ALU.subtract, ALU.min)
                m.then_inc(S("mb_seg"), 1)
                yield BG[s0 + 6]
                v.wait_ge(S("mb_tB"), it)
                xt_ = B[6][rn, 0:HC * HD].rearrange("p (h c) -> p h c", c=HD)
                tt(xdt[rn, :, :], xt_, over(tk3[rn, 0, :], HD), ALU.mult)
                tt(xw[rn, :, :], xt_, over(tk3[rn, 2, :], HD), ALU.mult).then_inc(S("mb_xdt"), 1)
                yield BG[s0 + 8]
                v.wait_ge(S("mb_BC"), it)
                tt(cbm[rn, :, 0:n], bank(7, 2, n, rn), rep(C("causal8" if b == 2 else "causal", rows=rn), 2),
                   ALU.mult).then_inc(S("v_step"), 1)
                v.wait_ge(S("v_step"), own_count())
                v.wait_ge(S("mb_E"), it)
                for g in range(2):
                    m = tt(wts[rn, 3 * g:3 * g + 3, 0:n], seg[rn, 3 * g:3 * g + 3, 0:n], rep(cbm[rn, g, 0:n], 3), ALU.mult)
                m.then_inc(S("mb_wts"), 1)
                yield BG[s0 + 10]
                v.wait_ge(S("mb_y"), it)
                v.wait_ge(S("mb_xc"), it)
                for t in range(TC):
                    m = stt(yz[:, t, 0:n], xc[:, t, 0:n], V("d", t), B[6][:, t * P:t * P + n], ALU.mult, ALU.add)
                m.then_inc(S("v_step"), 1)
                v.wait_ge(S("v_step"), own_count())
                v.wait_ge(S("mb_zs"), it)
                tt(yz[:, :, 0:n], yz[:, :, 0:n], zs[:, :, 0:n], ALU.mult).then_inc(S("mb_y2"), 1)
                v.wait_ge(S("mb_ecb"), it)
                if b < 2:
                    v.wait_ge(S("zeroed"), l + 1)
                    if b > 0:
                        v.wait_ge(S("mb_S"), 2 * l + b)
                    st = smb_p[:, :].rearrange("p (h c) -> p h c", c=HD)
                    tt(st, st, ecb[:, :, n - 1:n].to_broadcast([P, HC, HD]), ALU.mult).then_inc(S("v_step"), 1)
                    v.wait_ge(S("v_step"), own_count())
                    v.wait_ge(S("mb_dS"), 2 * l + b + 1)
                    tt(smb_p[:, :], smb_p[:, :], B[7][:, 0:HC * HD], ALU.add).then_inc(S("mb_S"), 1)
                else:
                    for g in range(2):
                        for h in range(3):
                            last = ecb[:, 3 * g + h, STEP - 1:NSEQ * STEP:STEP]
                            st = smb[:, g, :, h, :]
                            m = tt(st, st, over(last, HD), ALU.mult)
                    m.then_inc(S("v_step"), 1)
                    v.wait_ge(S("v_step"), own_count())
                    for k, at in enumerate((11, 12, 12, 14, 14, 15)):
                        yield BG[s0 + at]
                        v.wait_ge(S("mb_ds"), 6 * l + k + 1)
                        f = smb[:, k // 3, :, :, :].rearrange("p s h c -> p (s h c)")[:, k % 3 * 512:(k % 3 + 1) * 512]
                        tt(f, f, B[7 - k % 2][:, :], ALU.add).then_inc(S("mb_ds_used"), 1)
                yield BG[s0 + (16 if b == 2 else 12)]
                v.wait_ge(S("mb_sd"), it)
                v.reciprocal(zs[:, 0, 0:n], zs[:, 0, 0:n]).then_inc(S("v_step"), 1)
                v.wait_ge(S("v_step"), own_count())
                v.wait_ge(S("mb_y2"), it)
                for t in range(TC):
                    m = stt(yz[:, t, 0:n], yz[:, t, 0:n], V("ssm_norm", t), zs[:, 0, 0:n], ALU.mult, ALU.mult)
                m.then_inc(S("mb_y3"), 1)
                yield BG[s0 + (18 if b == 2 else 13)]
                v.wait_ge(S("mb_yh"), it)
                tt(hl[:, TA + TB:KT, c0:c0 + n], yz[:, :, 0:n], hh[:, TA + TB:KT, c0:c0 + n].bitcast(F32),
                   ALU.subtract).then_inc(S("mix_done"), 1)

            def rwkv_all(l):
                for b in range(3):
                    yield from rwkv(l, b)

            def others(l):
                for b in range(3):
                    yield from retention(l, b)
                for b in range(3):
                    yield from mamba(l, b)

            def router():
                v.tensor_tensor_scan(count_up[:, :], C("ones"), C("ones"), 0.0, ALU.mult, ALU.add)
                v.tensor_reduce(slot_no[:, :], C("causal"), AX.X, ALU.add)
                v.memset(rt["pos"][:, :, :], 0.0)
                v.memset(rt["l"][:, :, :], 0.0).then_inc(S("v_step"), 1)
                v.wait_ge(S("v_step"), own_count())
                ts(slot_no[:, :], slot_no[:, :], -1.0, P + 1.0, ALU.mult, ALU.add)
                v.wait_ge(S("ro_pe"), 1)
                for q, (c0, n) in enumerate(BLOCKS):
                    m = cp(rt["l"][0:n, q, :], B[7][0:n, q * NEXP:(q + 1) * NEXP])
                m.then_inc(S("v_step"), 1)
                v.wait_ge(S("v_step"), own_count())
                l_, e_, p_, rk, g_ = (rt[k][:, :, :] for k in ("l", "e", "p", "rank", "g"))
                v.tensor_reduce(rt1[:, :, 0], l_, AX.X, ALU.max).then_inc(S("v_step"), 1)
                v.wait_ge(S("v_step"), own_count())
                tt(l_, l_, over(rt1[:, :, 0], NEXP), ALU.subtract).then_inc(S("ro_dve"), 1)
                v.wait_ge(S("ro_act"), 4)
                v.tensor_reduce(rt1[:, :, 1], e_, AX.X, ALU.add).then_inc(S("v_step"), 1)
                v.wait_ge(S("v_step"), own_count())
                v.reciprocal(rt1[:, :, 1], rt1[:, :, 1]).then_inc(S("v_step"), 1)
                v.wait_ge(S("v_step"), own_count())
                tt(p_, e_, over(rt1[:, :, 1], NEXP), ALU.mult).then_inc(S("v_step"), 1)
                v.wait_ge(S("v_step"), own_count())
                for q in range(3):
                    of_j, of_e = rep(rt["p"][:, q, :], NEXP), over(rt["p"][:, q, :], NEXP)
                    tt(cmp[:, q, :, :], of_j, of_e, ALU.is_gt)
                    m = tt(cmq[:, q, :, :], of_j, of_e, ALU.is_equal)
                m.then_inc(S("v_step"), 1)
                v.wait_ge(S("v_step"), own_count())
                for q in range(3):
                    m = tt(cmq[:, q, :, :], cmq[:, q, :, :], C("before").rearrange("p (e j) -> p e j", j=NEXP), ALU.mult)
                m.then_inc(S("v_step"), 1)
                v.wait_ge(S("v_step"), own_count())
                tt(cmp[:, :, :, :], cmp[:, :, :, :], cmq[:, :, :, :], ALU.add).then_inc(S("v_step"), 1)
                v.wait_ge(S("v_step"), own_count())
                for q in range(3):
                    m = v.tensor_reduce(rt["rank"][:, q, :], cmp[:, q, :, :], AX.X, ALU.add)
                m.then_inc(S("v_step"), 1)
                v.wait_ge(S("v_step"), own_count())
                stt(g_, rk, 1.5, p_, ALU.is_lt, ALU.mult).then_inc(S("v_step"), 1)
                v.wait_ge(S("v_step"), own_count())
                v.tensor_reduce(rt1[:, :, 2], g_, AX.X, ALU.add).then_inc(S("v_step"), 1)
                v.wait_ge(S("v_step"), own_count())
                v.reciprocal(rt1[:, :, 2], rt1[:, :, 2]).then_inc(S("v_step"), 1)
                v.wait_ge(S("v_step"), own_count())
                tt(g_, g_, over(rt1[:, :, 2], NEXP), ALU.mult).then_inc(S("v_step"), 1)
                v.wait_ge(S("v_step"), own_count())
                last = BLOCKS[2][1]
                v.memset(rt["g"][last:P, 2, :], 0.0).then_inc(S("ro_dve"), 1)
                v.wait_ge(S("ro_act"), 9)
                ts(chosen[:, :], lg[:, :], 0.0, None, ALU.is_gt)
                ts(ones8[:, :], lg[:, :], 0.0, None, ALU.is_ge).then_inc(S("v_step"), 1)
                v.wait_ge(S("v_step"), own_count())
                v.tensor_tensor_scan(upto[:, :], ones8[:, :], chosen[:, :], 0.0, ALU.mult, ALU.add).then_inc(S("v_step"), 1)
                v.wait_ge(S("v_step"), own_count())
                tt(pos1[:, :], upto[:, :], chosen[:, :], ALU.mult).then_inc(S("ro_dve"), 1)
                v.wait_ge(S("ro_pe"), 9)
                for q, (c0, n) in enumerate(BLOCKS):
                    cp(rt["pos"][0:n, q, :], B[7][0:n, q * NEXP:(q + 1) * NEXP])
                v.tensor_reduce(n_most[:, 0:1], B[7][0:1, 32:32 + NEXP], AX.X, ALU.max).then_inc(S("v_step"), 1)
                v.wait_ge(S("v_step"), own_count())
                cp(n_most_i[:, :], n_most[:, 0:1]).then_inc(S("ro_dve"), 1)

            L = DEPTH - 1

            def times_up(f, e, bk):
                v.wait_ge(S("sil"), e * FT + f + 1)
                tt(hid[:, f % 2, :], sil[:, f % 2, :], B[bk][:, 0:T], ALU.mult).then_inc(S("gu_free"), 1)

            def hidden_lo(f, e):
                v.wait_ge(S("hid_hi"), e * FT + f + 1)
                tt(hidl[:, f, :], hid[:, f % 2, :], hidh[:, f, :].bitcast(F32), ALU.subtract).then_inc(S("hid_split"), 1)

            def ffn(l):
                ends = {2 * FT + (FT * m_ + FT - 1) // KT: m_ for m_ in range(KT)}

                def body(i, g, e):
                    for j in range(EXP_SLOTS):
                        lo(g + j + HI, G_FFN[l] + j + HI)
                        if j < 2 * FT and j % 2:
                            v.wait_ge(S("slot_used"), g + j + 1)
                            times_up(j // 2, e, 2 * (j // 2 % 2) + 1)
                        elif 0 < j <= 2 * FT:
                            hidden_lo(j // 2 - 1, e)
                        if j in ends:
                            m_ = ends[j]
                            if m_ < KT - 1:
                                v.wait_ge(S("dn"), e * (KT - 1) + m_ + 1)
                            else:
                                v.wait_ge(S("slot_used"), g + EXP_SLOTS)
                            v.wait_ge(S("dn_free"), e * KT + m_ + 1)
                            tt(x[:, m_, :], x[:, m_, :], B[4 + m_ % 4][:, 0:T], ALU.add).then_inc(S("dn_free"), 1)
                expert_loop(v, l, body)

            def experts_dense():
                v.wait_ge(S("ro_act"), 9 + NEXP)

                def body(i, g, e):
                    for j in range(EXP_SLOTS):
                        lo(g + j + HI, G_FFN[L] + j + HI)
                        if j in ENDS:
                            c = ENDS[j]
                            v.wait_ge(S("slot_used"), g + j + 1)
                            tiles = range(2 * c, 2 * c + CHUNKS[c][2])
                            v.wait_ge(S("hid_split"), e * FT + 2 * c)
                            for f in tiles:
                                times_up(f, e, 4 * (c % 2) + 2 + f % 2)
                            for f in tiles:
                                hidden_lo(f, e)
                    v.wait_ge(S("slot_used"), g + EXP_SLOTS)
                    for m_ in range(KT):
                        v.wait_ge(S("yt_free"), i * KT + m_ + KT - YR + 1)
                        gate = gbc[:, bass.ds(i, 1), :].rearrange("p o t -> p (o t)")
                        tt(yt[:, m_ % YR, :], B[m_][:, 0:T], gate, ALU.mult).then_inc(S("dn_free"), 1)
                expert_loop(v, L, body)

            def taken_lo(i):
                v.wait_ge(S("taken"), 2 * i + 2)
                for z in range(2):
                    m = cp(hl[:, 4 * z:4 * z + 4, 0:P], bank(2 + z, 4, P))
                m.then_inc(S("taken_lo"), 1)

            def experts_picked():
                for q in range(3):
                    tt(pick[:, 0:NEXP, q, :], rep(count_up[:, :], NEXP), over(rt["pos"][:, q, :], P), ALU.is_equal)
                    m = ts(pick[:, NEXP, q, :], count_up[:, :], 0.0, None, ALU.mult)
                m.then_inc(S("ro_dve"), 1)
                taken_lo(0)
                for e in range(NEXP):
                    v.wait_ge(S("ro_pe"), 10 + e + 1)
                    ts(place[:, e, :], B[e % 2][:, 0:T], slot_no[:, :], None, ALU.is_equal).then_inc(S("ro_dve"), 1)
                v.wait_ge(S("ro_act"), 10)

                def body(i, g, e):
                    for j in range(EXP_SLOTS):
                        if j == EXP_SLOTS - 1:
                            for z in range(2):
                                v.wait_ge(S("y_hi"), 2 * i + z + 1)
                                stt(hidl[:, 4 * z:4 * z + 4, P:2 * P], bank(4 + z, 4, P), slot_gate[:, bass.ds(i, 1)],
                                    hidh[:, 4 * z:4 * z + 4, P:2 * P].bitcast(F32), ALU.mult, ALU.subtract)\
                                    .then_inc(S("y_lo"), 1)
                        lo(g + j + HI, G_FFN[L] + j + HI)
                        if j in ENDS:
                            c, n = ENDS[j], CHUNKS[ENDS[j]][2] * P
                            v.wait_ge(S("sil"), i * NC + (N_E[0] * FT + c + 1))
                            tt(hid[:, c % 2, 0:n], sil[:, c % 2, 0:n], B[c % 2][:, n:2 * n], ALU.mult)\
                                .then_inc(S("gu_free"), 1)
                        if j in TURN:
                            c, n = TURN[j], CHUNKS[TURN[j]][2]
                            v.wait_ge(S("hid_hi"), i * NC + (N_E[0] * FT + c + 1))
                            tt(hidl[:, 2 * c:2 * c + n, 0:P], bank(2 + c % 2, n, P),
                               hidh[:, 2 * c:2 * c + n, 0:P].bitcast(F32), ALU.subtract).then_inc(S("hid_split"), 1)
                    taken_lo(i + 1)
                    v.wait_ge(S("dn_free"), i * 4 + KT * (1 + N_E[0]))
                    for m_ in range(1, KT, 2):
                        v.wait_ge(S("put"), i * KT + m_ + 1)
                        tt(x[:, m_, :], x[:, m_, :], B[4 + m_ % 4][:, 0:T], ALU.add).then_inc(S("dn_free"), 1)
                expert_loop(v, L, body)

            v.sem_inc(S("gu_free"), 2)
            v.sem_inc(S("dn_free"), KT)
            v.sem_inc(S("put_free"), 4)
            v.wait_ge(S("const_in"), 16)
            for g in range(HI):
                lo(g, g)
            for l in range(DEPTH):
                v.wait_ge(S("par_in"), 16 * (l + 1))
                norm(2 * l)
                for g in range(G_IN[l] + HI, G_OUT[l]):
                    lo(g, g)
                weave(rwkv_all(l), shift(l), mamba_dt(l), others(l))
                for g in range(G_OUT[l], G_OUT[l] + HI):
                    lo(g, g)
                for j in range(KT):
                    lo(G_OUT[l] + j + HI, G_OUT[l] + j + HI)
                    v.wait_ge(S("slot_used"), G_OUT[l] + j + 1)
                    tt(x[:, j, :], x[:, j, :], B[6 + j % 2][:, 0:T], ALU.add).then_inc(S("out_read"), 1)
                norm(2 * l + 1)
                v.wait_ge(S("st_out"), 16 * 8 * (l + 1))
                if l == DEPTH - 1:
                    lo(G_FFN[l] - 1 + HI, G_FFN[l] - 1 + HI)
                    router()
                    v.wait_ge(S("ro_dve"), 4)
                    most = v.value_load(n_most_i[0:1, 0:1], min_val=0, max_val=T)
                    with v.If(most <= P):
                        experts_picked()
                    with v.Else():
                        experts_dense()
                else:
                    ffn(l)
            norm(2 * DEPTH)

        @block.gpsimd
        def _(gp):
            tt = gp.tensor_tensor
            own = [0]

            def own_count():
                own[0] += 1
                return own[0]

            def rwkv(l, b):
                it, (c0, n), s0 = 3 * l + b + 1, BLOCKS[b], RW_AT[b]
                lv, rr = 15 * l + 6 * b, slice(0, chunks(b) * CH)
                yield s0 + 3
                gp.wait_ge(S("rw_kp"), it)
                tt(U["br"][:, :, 0:n], Dx[:, 0:3, 0:n], U["kp"][:, :, 0:n], ALU.mult).then_inc(S("gp_step"), 1)
                gp.wait_ge(S("gp_step"), own_count())
                tt(U["br"][:, :, 0:n], U["br"][:, :, 0:n], over(V("r_k", 0, 3), n), ALU.mult).then_inc(S("rw_br"), 1)
                yield s0 + 7
                gp.wait_ge(S("rw_AT"), it)
                for q in range(levels(b)):
                    if q >= 2:
                        yield s0 + max(10, 5 + 2 * q)
                        gp.wait_ge(S("rw_W"), lv + q - 1)
                        gp.wait_ge(S("rw_T"), lv + 1)
                    m = C("lev").rearrange("p (q c) -> p q c", c=CH)[rr, q, :]
                    for o in range(2):
                        i_ = tt(AL[rr, q % 2, o * TA:(o + 1) * TA, :], AB[rr, o, 0, :, :], rep(m, TA), ALU.mult)
                    i_.then_inc(S("rw_AL"), 1)
                if b == 2:
                    yield s0 + RW_END[b] - 1
                    gp.wait_ge(S("rw_tok"), 3 * it - 2)
                    gp.wait_ge(S("rw_SAc"), 5 * (l + 1))
                    for t in range(TA):
                        if t >= 1:
                            gp.wait_ge(S("rw_ds"), 3 * l + t)
                        tt(rwx[:, 1, :, :], rep(tok[0:CH, 0, t, :], NSEQ), over(C("seq", rows=slice(0, CH)), P),
                           ALU.mult).then_inc(S("rw_xv"), 1)

            def retention(l, b):
                it, (c0, n), s0 = 3 * l + b + 1, BLOCKS[b], RT_AT[b]
                yield BG[s0]
                if b > 0:
                    gp.wait_ge(S("rt_qk"), it - 1)
                tt(qk2[:, :, 0:n], cB[:, 0:4, c0:c0 + n], rep(C("cos", c0, n), 4), ALU.mult).then_inc(S("rt_q2"), 1)
                if b == 2:
                    yield BG[s0 + 5]
                    gp.wait_ge(S("rt_tok"), it)
                    vt = vkt[0:CH, 0:2, :].rearrange("p a (h c) -> p (a h) c", c=HD)
                    for h in range(HB):
                        m = tt(vx[:, h, :, :], rep(vt[:, h, :], NSEQ), over(C("seq", rows=slice(0, CH)), HD), ALU.mult)
                    m.then_inc(S("rt_vx"), 1)

            def mamba(l, b):
                it, (c0, n), s0 = 3 * l + b + 1, BLOCKS[b], MB_AT[b]
                yield BG[s0 + 4]
                gp.wait_ge(S("mb_ecb"), it)
                gp.wait_ge(S("mb_xc"), it)
                for g in range(2):
                    m = tt(cde[:, 3 * g:3 * g + 3, 0:n], ecb[:, 3 * g:3 * g + 3, 0:n], rep(xc[:, 5 + g, 0:n], 3), ALU.mult)
                m.then_inc(S("mb_cde"), 1)
                if b == 2:
                    for g in range(2):
                        yield BG[s0 + (8, 12)[g]]
                        if g:
                            gp.wait_ge(S("mb_ds"), 6 * l + 3)
                        else:
                            gp.wait_ge(S("mb_xdt"), it)
                        tt(xwe[:, :, :, :].rearrange("p s h c -> p s (h c)"),
                           rep(xw[0:CH, 3 * g:3 * g + 3, :].rearrange("p h c -> p (h c)"), NSEQ),
                           over(C("seq", rows=slice(0, CH)), 3 * HD), ALU.mult).then_inc(S("mb_xwe"), 1)

            def rwkv_all(l):
                for b in range(3):
                    yield from rwkv(l, b)

            def others(l):
                yield 0
                gp.dma_start(srt[:, :, :, :], s_rt[l]).then_inc(S("srt_in"), 16)
                gp.dma_start(smb[:, :, :, :, :], s_mb[l]).then_inc(S("smb_in"), 16)
                for b in range(3):
                    yield from retention(l, b)
                yield BG[RT_AT[2] + 9]
                gp.wait_ge(S("rt_S"), 3 * (l + 1))
                out(p_rt[l], srt_p[:, :, :])
                out(o_rt[l], srt[:, :, :, :])
                for b in range(3):
                    yield from mamba(l, b)
                yield BG[MB_AT[2] + 18]
                gp.wait_ge(S("mb_S"), 2 * (l + 1))
                out(p_mb[l], smb_p[:, :])
                gp.wait_ge(S("mb_ds_used"), 6 * (l + 1))
                out(o_mb[l], smb[:, :, :, :, :])
                gp.wait_ge(S("mix_done"), 6 * (l + 1))
                gp.wait_ge(S("st_out"), 16 * (8 * l + 6))
                gp.sem_inc(S("rings_free"), 1)

            def out(dst, src):
                gp.dma_start(dst, src).then_inc(S("st_out"), 16)

            gp.sem_inc(S("yt_free"), KT)
            gp.dma_start(par[:, :], par_in[0]).then_inc(S("par_in"), 16)
            gp.wait_ge(S("const_in"), 16)
            for l in range(DEPTH):
                if l:
                    gp.wait_ge(S("h_split"), KT * 2 * l + 1)
                    gp.wait_ge(S("st_out"), 16 * 8 * l)
                gp.dma_start(sh_in[:, :, :], s_sh[l]).then_inc(S("ends_in"), 16)
                gp.dma_start(cv_in[:, :, :, :], s_cv[l]).then_inc(S("ends_in"), 16)
                gp.dma_start(srw[:, :, :, :], s_rw[l]).then_inc(S("srw_in"), 16)
                gp.memset(srw_p[:, :, :], 0.0)
                gp.memset(srt_p[:, :, :], 0.0)
                gp.memset(smb_p[:, :], 0.0).then_inc(S("zeroed"), 1)
                gp.memset(cR[:, :, 0:1], 0.0)
                gp.memset(cX[:, :, 0:3], 0.0)
                gp.wait_ge(S("ends_in"), 32 * (l + 1))
                rows = cR[:, :, EA:WA_].rearrange("p t (s k) -> p t s k", k=STEP + 1)
                xrows = cX[:, :, EX:WX_].rearrange("p t (s k) -> p t s k", k=STEP + 3)
                gp.tensor_copy(rows[:, :, :, 0], sh_in[:, :, :])
                gp.tensor_copy(xrows[:, :, :, 0:3], cv_in[:, :, :, :]).then_inc(S("ext_ready"), 1)
                gp.wait_ge(S("in_read"), WIN * (l + 1))
                gp.tensor_copy(sh_out[:, :, 0:1], cR[:, :, EA - 1:EA])
                gp.tensor_copy(sh_out[:, :, 1:], rows[:, :, :, STEP])
                gp.tensor_copy(cv_out[:, :, 0, :], cX[:, :, EX - 3:EX])
                gp.tensor_copy(cv_out[:, :, 1:, :], xrows[:, :, :, STEP:]).then_inc(S("gp_step"), 1)
                gp.wait_ge(S("gp_step"), own_count())
                out(o_sh[l], sh_out[:, :, :])
                out(o_cv[l], cv_out[:, :, :, :])
                weave(rwkv_all(l), others(l))
                gp.wait_ge(S("rw_Sbd"), 5 * (l + 1))
                out(p_rw[l], srw_p[:, :, :])
                gp.wait_ge(S("rw_sS"), 3 * (l + 1))
                out(o_rw[l], srw[:, :, :, :])
                if l + 1 < DEPTH:
                    gp.wait_ge(S("h_split"), KT * (2 * l + 2))
                    gp.dma_start(par[:, :], par_in[l + 1]).then_inc(S("par_in"), 16)
                else:
                    gp.wait_ge(S("ro_dve"), 4)
                    most = gp.value_load(n_most_i[0:1, 0:1], min_val=0, max_val=T)
                    with gp.If(most <= P):
                        with gp.Fori(0, NEXP) as i:
                            for m_ in range(0, KT, 2):
                                gp.wait_ge(S("put_free"), i * 4 + m_ // 2 + 5)
                                gp.wait_ge(S("yt_free"), i * 4 + (KT - 3 + m_ // 2))
                                tt(x[:, m_, :], x[:, m_, :], yt[:, m_ // 2, :], ALU.add).then_inc(S("yt_free"), 1)
                    with gp.Else():
                        with gp.Fori(0, NEXP) as i:
                            for m_ in range(KT):
                                gp.wait_ge(S("dn_free"), i * KT + (N_E[0] * KT + KT + m_ + 1))
                                gp.wait_ge(S("yt_free"), i * KT + m_ + 1)
                                tt(x[:, m_, :], x[:, m_, :], yt[:, m_ % YR, :], ALU.add).then_inc(S("yt_free"), 1)
            gp.wait_ge(S("st_out"), 16 * 8 * DEPTH)



def tiles_of(m):
    a, b = m.shape
    return m.reshape(a // P, P, b // P, P).transpose(2, 1, 0, 3)


def slots_in(m):
    b = -(-m.shape[1] // P) * P
    pad = np.zeros((m.shape[0], b), m.dtype)
    pad[:, :m.shape[1]] = m
    return tiles_of(pad).reshape(b // P, P, D)


def slots_by_row(wg, wu, wd):
    out = []
    for j, n, nf in CHUNKS:
        c = slice(j * P // 2, j * P // 2 + nf * P)
        m = np.concatenate([wg[:, c], wu[:, c]], 1)
        out.append(m.reshape(n, KT // n, P, 2 * nf * P).transpose(0, 2, 1, 3).reshape(n, P, D))
    return out + [wd.reshape(FT, P, D)]


def slots_expert(wg, wu, wd):
    gu = np.stack([slots_in(wg), slots_in(wu)], 1).reshape(2 * FT, P, D)
    dn = tiles_of(wd).transpose(0, 2, 1, 3).reshape(KT * FT, P, P)
    return [gu, dn.reshape(FT, KT, P, P).transpose(0, 2, 1, 3).reshape(FT, P, D)]


def fm(a, axis=-1):
    return a.reshape(-1, P).T


def kernel(**inputs):
    import concourse.bacc as bacc
    from concourse.bass_utils import run_bass_kernel_spmd

    a = {k: np.asarray(v) for k, v in inputs.items()}
    f32 = np.float32
    xt = np.concatenate([a["x_prompt"].reshape(SEQ, D), a["x_sample"].reshape(NSEQ * STEP, D)], 0)
    x_in = xt.T.reshape(KT, P, T).transpose(1, 0, 2)

    stream = []
    for l in range(DEPTH):
        stream += [slots_in(a["w_in"][l]), slots_in(a["w_out"][l])]
        if l == 0:
            for h in range(2):
                c = slice(h * FE, (h + 1) * FE)
                stream += slots_expert(a["ffn_w_gate"][0][:, c], a["ffn_w_up"][0][:, c], a["ffn_w_down"][0][c])
        else:
            stream.append(slots_in(a["moe_router"][0]))
            for e in range(NEXP):
                stream += slots_by_row(a["moe_w_gate"][0, e], a["moe_w_up"][0, e], a["moe_w_down"][0, e])
    stream.append(np.zeros((N_SLOTS - G_END, P, D), f32))
    w_in = np.concatenate(stream, 0)
    assert w_in.shape[0] == N_SLOTS

    par = np.zeros((DEPTH, P, NPAR), f32)

    def put(name, l, v):
        par[l, :v.shape[0], PAR[name]:PAR[name] + v.shape[1]] = v

    for l in range(DEPTH):
        for name, src in [("g_mix", a["norm_mix"][l]), ("g_ffn", a["norm_ffn"][l]), ("g_fin", a["norm_final"]),
                          ("mu", a["rwkv_mu"][l]), ("w0", a["rwkv_w0"][l]), ("a0", a["rwkv_a0"][l]),
                          ("k_k", a["rwkv_k_k"][l]), ("k_a", a["rwkv_k_a"][l]), ("r_k", a["rwkv_r_k"][l]),
                          ("ln_w", a["rwkv_ln_w"][l]), ("ln_b", a["rwkv_ln_b"][l]), ("ret_norm", a["ret_norm"][l]),
                          ("conv_b", a["ssm_conv_b"][l]), ("ssm_norm", a["ssm_norm"][l]),
                          ("d", np.repeat(a["ssm_d"][l], HD))]:
            put(name, l, fm(src.reshape(-1)))
        put("conv_w", l, np.concatenate([fm(a["ssm_conv_w"][l, j]) for j in range(CONV)], 1))
        put("dt_bias", l, a["ssm_dt_bias"][l][:, None])
        put("a_log", l, a["ssm_a_log"][l][:, None])
        put("wa_up", l, np.concatenate([a["rwkv_w_up"][l], a["rwkv_a_up"][l]], 0))
        put("g_up", l, a["rwkv_g_up"][l])

    rw = a["state_rwkv"].transpose(0, 2, 4, 1, 3).reshape(DEPTH, TA, P, NSEQ, HD).transpose(0, 2, 1, 3, 4)
    rt = a["state_ret"].transpose(0, 2, 3, 1, 4).reshape(DEPTH, TB, P, NSEQ, HD).transpose(0, 2, 1, 3, 4)
    mb = a["state_ssm"].transpose(0, 4, 1, 2, 3).reshape(DEPTH, NST, NSEQ, 2, 3, HD).transpose(0, 1, 3, 2, 4, 5)
    sh = a["state_shift"].transpose(0, 2, 1).reshape(DEPTH, A_TILES, P, NSEQ).transpose(0, 2, 1, 3)
    cv = a["state_conv"].transpose(0, 3, 1, 2).reshape(DEPTH, XT, P, NSEQ, 3).transpose(0, 2, 1, 3, 4)
    ins = [("x", x_in), ("w", w_in), ("consts", constants()[0]), ("par", par), ("s_rwkv", rw), ("s_ret", rt),
           ("s_ssm", mb), ("s_shift", sh), ("s_conv", cv)]
    outs = [("y", (P, KT, T)), ("p_rwkv", (DEPTH, P, TA, HD)), ("p_ret", (DEPTH, P, TB, HD)),
            ("p_ssm", (DEPTH, P, HC * HD)), ("o_rwkv", rw.shape), ("o_ret", rt.shape), ("o_ssm", mb.shape),
            ("o_shift", (DEPTH, P, A_TILES, 1 + NSEQ)), ("o_conv", (DEPTH, P, XT, 1 + NSEQ, 3))]

    nc = bacc.Bacc("TRN2", target_bir_lowering=False, num_devices=1)
    arrays, args = {}, []
    for name, v in ins:
        arrays["in_" + name] = np.ascontiguousarray(v)
        args.append(nc.dram_tensor("in_" + name, v.shape, F32, kind="ExternalInput").ap())
    for name, shape in outs:
        args.append(nc.dram_tensor("out_" + name, shape, F32, kind="ExternalOutput").ap())
    trunk(nc, *args)
    r = run_bass_kernel_spmd(nc, [arrays], core_ids=[0]).results[0]
    y, p_rw, p_rt, p_mb, o_rw, o_rt, o_mb, o_sh, o_cv = (np.asarray(r["out_" + name]) for name, _ in outs)

    y = y.transpose(2, 1, 0).reshape(T, D)

    def heads_rw(s):
        n = s.shape[3]
        return s.transpose(0, 2, 1, 3, 4).reshape(DEPTH, HA, HD, n, HD).transpose(0, 3, 1, 4, 2)

    def heads_rt(s):
        n = s.shape[3]
        return s.transpose(0, 2, 1, 3, 4).reshape(DEPTH, HB, HD, n, HD).transpose(0, 3, 1, 2, 4)

    p_ssm = p_mb.reshape(DEPTH, NST, HC, HD).transpose(0, 2, 3, 1)[:, None]
    s_ssm = o_mb.transpose(0, 3, 2, 4, 5, 1).reshape(DEPTH, NSEQ, HC, HD, NST)
    shift = o_sh.transpose(0, 3, 2, 1).reshape(DEPTH, 1 + NSEQ, COLS_A)
    conv = o_cv.transpose(0, 3, 4, 2, 1).reshape(DEPTH, 1 + NSEQ, 3, CONV_DIM)
    return (y[:SEQ].reshape(1, SEQ, D), y[SEQ:].reshape(NSEQ, STEP, D),
            heads_rw(p_rw[:, :, :, None]), shift[:, :1], heads_rt(p_rt[:, :, :, None]), p_ssm, conv[:, :1],
            heads_rw(o_rw), shift[:, 1:], heads_rt(o_rt), s_ssm, conv[:, 1:])
```
